# Optimizing a Trainium2 kernel written in Bass

```python
import jax, jax.numpy as jnp
from jax import lax
import numpy as np

D_MODEL = 1024
BATCH = 1
SEQ = 512
DEPTH = 1

CHUNK = 64
HEAD_DIM = 64
N_HEADS_FOX = 8
N_HEADS_SB = 8
D_FOX = N_HEADS_FOX * HEAD_DIM
D_SB = N_HEADS_SB * HEAD_DIM
W_IN = 3 * D_FOX + N_HEADS_FOX + 3 * D_SB + 2 * D_MODEL
Q_BLOCK = 128
N_GROUPS = 4
EXPERTS_PER_GROUP = 8
N_EXPERTS = N_GROUPS * EXPERTS_PER_GROUP
TOP_K_IN_GROUP = 2
D_EXPERT = 512
DISPATCH_BLOCK = 256
DN_ALPHA = (2.0 * DEPTH) ** 0.25
DN_BETA = (8.0 * DEPTH) ** -0.25
LN_EPS = 1e-5

kernel_name = 'hybrid_fox_stickbreaking_hmoe_block'

def layer_norm(x, g, b):
    xf = x.astype(jnp.float32)
    mu = jnp.mean(xf, axis=-1, keepdims=True)
    var = jnp.mean(jnp.square(xf - mu), axis=-1, keepdims=True)
    return ((xf - mu) * lax.rsqrt(var + LN_EPS) * g.astype(jnp.float32) + b.astype(jnp.float32)).astype(x.dtype)

def to_heads(t, n_heads):
    B, S, _ = t.shape
    return t.reshape(B, S, n_heads, HEAD_DIM).transpose(0, 2, 1, 3)

def from_heads(t):
    B, H, S, Dh = t.shape
    return t.transpose(0, 2, 1, 3).reshape(B, S, H * Dh)

def sweep_query_blocks(block_fn, seq_len):
    out = lax.map(block_fn, jnp.arange(seq_len // Q_BLOCK))
    out = jnp.moveaxis(out, 0, 2)
    B, H, nb, Q, Dh = out.shape
    return out.reshape(B, H, nb * Q, Dh)

def forgetting_attention(q, k, v, log_f):
    B, H, S, Dh = q.shape
    scale = Dh ** -0.5
    F = jnp.cumsum(log_f.astype(jnp.float32), axis=-1)
    kf = k.astype(jnp.float32)
    vf = v.astype(jnp.float32)
    s_pos = jnp.arange(S)

    def block(i):
        start = i * Q_BLOCK
        qb = lax.dynamic_slice_in_dim(q, start, Q_BLOCK, axis=2).astype(jnp.float32)
        Fq = lax.dynamic_slice_in_dim(F, start, Q_BLOCK, axis=2)
        t_pos = start + jnp.arange(Q_BLOCK)
        logits = jnp.einsum('bhqd,bhkd->bhqk', qb, kf) * scale + Fq[..., :, None] - F[..., None, :]
        causal = s_pos[None, :] <= t_pos[:, None]
        p = jax.nn.softmax(jnp.where(causal, logits, -jnp.inf), axis=-1)
        return jnp.einsum('bhqk,bhkd->bhqd', p, vf)

    return sweep_query_blocks(block, S).astype(q.dtype)

def stick_breaking_attention(q, k, v):
    B, H, S, Dh = q.shape
    scale = Dh ** -0.5
    kf = k.astype(jnp.float32)
    vf = v.astype(jnp.float32)
    s_pos = jnp.arange(S)

    def block(i):
        start = i * Q_BLOCK
        qb = lax.dynamic_slice_in_dim(q, start, Q_BLOCK, axis=2).astype(jnp.float32)
        t_pos = start + jnp.arange(Q_BLOCK)
        z = jnp.einsum('bhqd,bhkd->bhqk', qb, kf) * scale
        strict = s_pos[None, :] < t_pos[:, None]
        log_one_minus_beta = jnp.where(strict, jax.nn.log_sigmoid(-z), 0.0)
        suffix = lax.cumsum(log_one_minus_beta, axis=3, reverse=True) - log_one_minus_beta
        a = jnp.where(strict, jnp.exp(jax.nn.log_sigmoid(z) + suffix), 0.0)
        return jnp.einsum('bhqk,bhkd->bhqd', a, vf)

    return sweep_query_blocks(block, S).astype(q.dtype)

def hybrid_mixer(x, w_in, b_forget, w_up_fox, w_up_sb, w_out):
    proj = jnp.einsum('bsd,de->bse', x, w_in)
    cuts = [D_FOX, 2 * D_FOX, 3 * D_FOX, 3 * D_FOX + N_HEADS_FOX,
            3 * D_FOX + N_HEADS_FOX + D_SB, 3 * D_FOX + N_HEADS_FOX + 2 * D_SB,
            3 * D_FOX + N_HEADS_FOX + 3 * D_SB, 3 * D_FOX + N_HEADS_FOX + 3 * D_SB + D_MODEL]
    q_f, k_f, v_f, f_logit, q_s, k_s, v_s, g_fox, g_sb = jnp.split(proj, cuts, axis=-1)
    log_f = jax.nn.log_sigmoid(f_logit.astype(jnp.float32) + b_forget.astype(jnp.float32))
    y_fox = forgetting_attention(to_heads(q_f, N_HEADS_FOX), to_heads(k_f, N_HEADS_FOX),
                                 to_heads(v_f, N_HEADS_FOX), jnp.transpose(log_f, (0, 2, 1)))
    y_sb = stick_breaking_attention(to_heads(q_s, N_HEADS_SB), to_heads(k_s, N_HEADS_SB),
                                    to_heads(v_s, N_HEADS_SB))
    up_fox = jnp.einsum('bse,ed->bsd', from_heads(y_fox), w_up_fox)
    up_sb = jnp.einsum('bse,ed->bsd', from_heads(y_sb), w_up_sb)
    merged = jax.nn.sigmoid(g_fox) * up_fox + jax.nn.sigmoid(g_sb) * up_sb
    return jnp.einsum('bsd,de->bse', merged, w_out)

def hierarchical_moe(h, w_group, b_group, w_expert_router, b_expert_router, w1, w3, w2):
    B, S, D = h.shape
    N = B * S
    M = N * TOP_K_IN_GROUP
    hf = h.reshape(N, D)
    g_logits = jnp.einsum('nd,dg->ng', hf, w_group).astype(jnp.float32) + b_group.astype(jnp.float32)
    g_prob = jax.nn.softmax(g_logits, axis=-1)
    g_sel = jnp.argmax(g_logits, axis=-1)
    g_gate = jnp.take_along_axis(g_prob, g_sel[:, None], axis=-1)[:, 0]
    e_all = (jnp.einsum('nd,de->ne', hf, w_expert_router).astype(jnp.float32)
             + b_expert_router.astype(jnp.float32)).reshape(N, N_GROUPS, EXPERTS_PER_GROUP)
    e_logits = jnp.take_along_axis(e_all, g_sel[:, None, None], axis=1)[:, 0]
    top_p, top_i = lax.top_k(jax.nn.softmax(e_logits, axis=-1), TOP_K_IN_GROUP)
    top_p = top_p / jnp.sum(top_p, axis=-1, keepdims=True)
    gate = (g_gate[:, None] * top_p).reshape(M)
    expert_id = (g_sel[:, None] * EXPERTS_PER_GROUP + top_i).reshape(M)
    token_id = jnp.arange(M) // TOP_K_IN_GROUP
    order = jnp.argsort(expert_id)
    s_e, s_tok, s_w = expert_id[order], token_id[order], gate[order]
    counts = jnp.bincount(expert_id, length=N_EXPERTS)
    padded = ((counts + DISPATCH_BLOCK - 1) // DISPATCH_BLOCK) * DISPATCH_BLOCK
    starts = jnp.cumsum(counts) - counts
    pstarts = jnp.cumsum(padded) - padded
    dest = pstarts[s_e] + (jnp.arange(M) - starts[s_e])
    n_blocks = (M + N_EXPERTS * (DISPATCH_BLOCK - 1) + DISPATCH_BLOCK - 1) // DISPATCH_BLOCK
    P = n_blocks * DISPATCH_BLOCK
    x_pad = jnp.zeros((P, D), h.dtype).at[dest].set(hf[s_tok])
    block_expert = jnp.repeat(jnp.arange(N_EXPERTS), padded // DISPATCH_BLOCK,
                              total_repeat_length=n_blocks)

    def expert_block(args):
        xb, e = args
        return (jax.nn.silu(xb @ w1[e]) * (xb @ w3[e])) @ w2[e]

    y_pad = lax.map(expert_block, (x_pad.reshape(n_blocks, DISPATCH_BLOCK, D), block_expert))
    y_assign = y_pad.reshape(P, D)[dest] * s_w[:, None].astype(h.dtype)
    y = jnp.zeros((N, D), h.dtype).at[s_tok].add(y_assign)
    return y.reshape(B, S, D)

def setup_inputs(seed: int = 0) -> dict:
    key = jax.random.key(seed)
    ks = jax.random.split(key, 24)
    f32 = jnp.float32
    L, D = DEPTH, D_MODEL
    std = D ** -0.5

    def nrm(k, shape, scale):
        return jax.random.normal(k, shape, f32) * scale

    x = nrm(ks[0], (BATCH, SEQ, D), 1.0)
    ln_in_g = 1.0 + nrm(ks[1], (D,), 0.02)
    ln_in_b = nrm(ks[2], (D,), 0.02)
    w_in = jnp.concatenate([
        nrm(ks[3], (L, D, 2 * D_FOX), std),
        nrm(ks[4], (L, D, D_FOX), std * DN_BETA),
        nrm(ks[5], (L, D, N_HEADS_FOX), std),
        nrm(ks[6], (L, D, 2 * D_SB), std),
        nrm(ks[7], (L, D, D_SB), std * DN_BETA),
        nrm(ks[8], (L, D, 2 * D), std),
    ], axis=-1)
    b_forget = jax.random.uniform(ks[9], (L, N_HEADS_FOX), f32, 1.0, 5.0)
    w_up_fox = nrm(ks[10], (L, D_FOX, D), D_FOX ** -0.5)
    w_up_sb = nrm(ks[11], (L, D_SB, D), D_SB ** -0.5)
    w_out = nrm(ks[12], (L, D, D), std * DN_BETA)
    ln1_g = 1.0 + nrm(ks[13], (L, D), 0.02)
    ln1_b = nrm(ks[14], (L, D), 0.02)
    w_group = nrm(ks[15], (L, D, N_GROUPS), std)
    b_group = nrm(ks[16], (L, N_GROUPS), 0.01)
    w_expert_router = nrm(ks[17], (L, D, N_EXPERTS), std)
    b_expert_router = nrm(ks[18], (L, N_EXPERTS), 0.01)
    w1 = nrm(ks[19], (L, N_EXPERTS, D, D_EXPERT), std * DN_BETA)
    w3 = nrm(ks[20], (L, N_EXPERTS, D, D_EXPERT), std * DN_BETA)
    w2 = nrm(ks[21], (L, N_EXPERTS, D_EXPERT, D), (D_EXPERT ** -0.5) * DN_BETA)
    ln2_g = 1.0 + nrm(ks[22], (L, D), 0.02)
    ln2_b = nrm(ks[23], (L, D), 0.02)
    return {'x': x, 'ln_in_g': ln_in_g, 'ln_in_b': ln_in_b, 'w_in': w_in, 'b_forget': b_forget,
            'w_up_fox': w_up_fox, 'w_up_sb': w_up_sb, 'w_out': w_out, 'ln1_g': ln1_g, 'ln1_b': ln1_b,
            'w_group': w_group, 'b_group': b_group, 'w_expert_router': w_expert_router,
            'b_expert_router': b_expert_router, 'w1': w1, 'w3': w3, 'w2': w2,
            'ln2_g': ln2_g, 'ln2_b': ln2_b}

def reference(x, ln_in_g, ln_in_b, w_in, b_forget, w_up_fox, w_up_sb, w_out, ln1_g, ln1_b,
              w_group, b_group, w_expert_router, b_expert_router, w1, w3, w2, ln2_g, ln2_b):
    h = layer_norm(x, ln_in_g, ln_in_b)
    for l in range(DEPTH):
        mix = hybrid_mixer(h, w_in[l], b_forget[l], w_up_fox[l], w_up_sb[l], w_out[l])
        h = layer_norm(DN_ALPHA * h + mix, ln1_g[l], ln1_b[l])
        ffn = hierarchical_moe(h, w_group[l], b_group[l], w_expert_router[l], b_expert_router[l],
                               w1[l], w3[l], w2[l])
        h = layer_norm(DN_ALPHA * h + ffn, ln2_g[l], ln2_b[l])
    return h


_drawn_inputs = setup_inputs


def setup_inputs(seed=0):
    import zlib

    import numpy as np

    out = dict(_drawn_inputs(seed))
    spreads = {}
    factors = {'ln1_g': 2.686,
     'ln1_b': 2.807,
     'b_group': 28.895,
     'b_expert_router': 21.49,
     'ln2_g': 7.963,
     'ln2_b': 8.211}
    for name, (base, spread) in spreads.items():
        noise = np.random.default_rng([zlib.crc32(name.encode()), seed]).standard_normal(out[name].shape)
        drawn = base * np.exp(spread * noise) if base else spread * noise
        out[name] = __import__('jax').numpy.asarray(drawn.astype(out[name].dtype))
    for name, factor in factors.items():
        out[name] = (out[name] * factor).astype(out[name].dtype)
    return out
```

```python
from contextlib import ExitStack

import concourse.bass as bass
from concourse import mybir

ALU = mybir.AluOpType
ACT = mybir.ActivationFunctionType
AX = mybir.AxisListType
F32 = mybir.dt.float32
BF16 = mybir.dt.bfloat16
I32 = mybir.dt.int32
U32 = mybir.dt.uint32

P = 128
D = 1024
S = 512
KT = D // P
TT = S // P
HD = 64
NH = 8
PAIRS = NH * HD // P
DH = NH * HD
SCALE = HD ** -0.5
GATE0 = 6 * DH + NH
SB_SHIFT = 3 * DH + NH
E = 32
NG = 4
EPG = E // NG
FE = 512
FT = FE // P
CAP = 64
QB = 4
MAIN = E // QB
MAXOV = 16
SLOTS = (E + MAXOV) * CAP
NR = NG + E
ALPHA = 2.0 ** 0.25
EPS = 1e-5
BIG = 1e30
PART_STEPS = 10
RING = 6
UNIT = 4096


class Steps:

    def __init__(self, eng, sem, base=0):
        self.eng, self.sem, self.base, self.n = eng, sem, base, 0

    def mark(self, ins):
        self.n += 1
        ins.then_inc(self.sem, 1)
        return self.base + self.n

    def wait(self, value):
        self.eng.wait_ge(self.sem, value)

    def done(self, ins):
        self.wait(self.mark(ins))


def build(nc, x, ln_in_g, ln_in_b, w_in, b_forget, w_up_fox, w_up_sb, w_out, ln1_g, ln1_b,
          w_group, b_group, w_expert_router, b_expert_router, w1, w3, w2, ln2_g, ln2_b, out):
    ctx = ExitStack()
    with ctx:
        base = (nc.sbuf_base + 63) // 64 * 64

        def at(name, offset, shape, dt=F32):
            return nc.alloc_sbuf_tensor_at(name, [shape[0]] + list(shape[1:]), dt, offset=offset)

        KB = 1024
        r = [base + 16 * KB * n for n in range(RING)]
        ring = [at(f"ring{n}", r[n], [P, UNIT]) for n in range(RING)]
        hT = at("hT", r[0], [P, KT, S])
        qkvw = at("qkvw", r[1], [P, 3, KT, P])
        probT = at("probT", r[1] + 12 * KB, [P, 2, S])
        gatew = at("gatew", r[2], [P, KT, 2 * P])
        qz = at("qz", r[2] + 8 * KB, [P, 2, S])
        kT = at("kT", r[2] + 12 * KB, [P, S])
        vp = at("vp", r[2] + 14 * KB, [P, TT, P])
        wa = at("wa", r[3], [P, 2, S])
        wb = at("wb", r[3] + 4 * KB, [P, 2, S])
        wc = at("wc", r[3] + 8 * KB, [P, 2, S])
        negf = at("negf", r[3] + 12 * KB, [P, 2, S])
        wupf = at("wupf", r[4], [P, PAIRS, D])
        wups = at("wups", r[5], [P, PAIRS, D])
        b0 = base + 16 * KB * RING
        h = at("h", b0, [P, TT, D])
        b1 = b0 + 16 * KB
        sg = at("sg", b1, [P, 2 * KT, S])
        xn = at("xn", b1, [P, TT, D])
        parts = at("parts", b1 + 16 * KB, [P, 3, TT, D], BF16)
        b2 = b1 + 32 * KB
        yT = at("yT", b2, [P, 2 * PAIRS, S])
        wr = at("wr", b2 + 8 * KB, [P, KT, P])
        h1T = at("h1T", b2 + 12 * KB, [P, KT, P])
        b3 = b2 + 16 * KB
        wout = at("wout", b3, [P, KT, D])
        xg = at("xg", b3, [P, KT, QB * CAP])
        oh = at("oh", b3 + 8 * KB, [P, TT, QB * CAP], BF16)
        silu = at("silu", b3 + 10 * KB, [P, 2 * P])
        hm = at("hm", b3 + 11 * KB, [P, 2 * P])
        hmT = at("hmT", b3 + 12 * KB, [P, 2, P])
        ysb = at("ysb", b3 + 14 * KB, [P, 2, S])
        rt = [at(f"rt{n}", b3 + 18 * KB + 512 * n, [P, TT, E]) for n in range(8)]
        ovc = at("ovc", b3 + 22 * KB, [P, MAXOV, E])
        cnt8 = at("cnt8", b3 + 24 * KB, [P, E, 8])
        ehot = at("ehot", b3 + 25 * KB, [P, TT, E], BF16)
        b4 = b3 + 32 * KB
        rows = at("rows", b4, [P, 2, D])
        cur = b4 + 8 * KB
        small = {}

        def sm(name, shape, dt=F32):
            nonlocal cur
            n = 1
            for s in shape[1:]:
                n *= s
            small[name] = at(name, cur, shape, dt)
            cur += (n * (2 if dt == BF16 else 4) + 31) // 32 * 32
            return small[name]

        ident = sm("ident", [P, P])
        cmask = sm("cmask", [P, P])
        keep = sm("keep", [P, P])
        smask = sm("smask", [P, P])
        tri = sm("tri", [P, P], BF16)
        ones = sm("ones", [P, P], BF16)
        io = sm("io", [P, QB * CAP])
        desc = sm("desc", [P, E])
        thr = sm("thr", [P, 8])
        zero = sm("zero", [P, 1])
        inT = sm("inT", [P, 2, KT])
        bfor = sm("bfor", [NH, 1])
        rbias = sm("rbias", [P, NR])
        stats = sm("stats", [P, TT, 2, 6])
        mv = sm("mv", [P, TT, 2])
        lnt = sm("lnt", [P, 4, TT])
        mx = sm("mx", [P, 2, 8])
        rs = sm("rs", [P, 2, 8])
        lg = sm("lg", [P, TT, NR])
        gt = sm("gt", [P, 4, TT, NG])
        r4 = sm("r4", [P, 12, TT])
        gate = sm("gate", [P, 2, TT])
        dest = sm("dest", [P, 2, TT])
        dsh = sm("dsh", [P, 2, TT])
        destu = sm("destu", [P, 2, TT], U32)
        ov = sm("ov", [P, 4, E])
        eb = sm("eb", [P, MAXOV + 1])
        ctl = sm("ctl", [P, MAXOV + 1], I32)
        gw4 = sm("gw4", [P, 4])
        rest = sm("rest", [P, D // 4])
        assert cur <= nc.sbuf_usable_end, (cur, nc.sbuf_usable_end)
        fw = at("fw", r[3] + 12 * KB, [P, KT, NH])
        fl = at("fl", r[3], [NH, 4, S])
        ioi = at("ioi", r[3] + 14 * KB, [P, QB * CAP], I32)
        yg = at("yg", r[0], [P, 2, TT, D])

        ps = ctx.enter_context(nc.psum_tensor("ps", [P, 8, S], F32))
        fdram = nc.dram_tensor("forget_sums", (NH, S), F32, kind="Internal").ap()
        ydram = nc.dram_tensor("y_by_slot", (SLOTS, D), F32, kind="Internal").ap()

        def sem(name):
            return ctx.enter_context(nc.semaphore(name))

        x_in = [sem(f"x_in{t}") for t in range(TT)]
        rows_in = [sem(f"rows_in{n}") for n in range(3)]
        inT_in = sem("inT_in")
        rb_in = sem("rb_in")
        bf_in = sem("bf_in")
        fw_in = sem("fw_in")
        qkv_in = sem("qkv_in")
        gw_in = sem("gw_in")
        wup_in = sem("wup_in")
        wout_in = sem("wout_in")
        wr_in = sem("wr_in")
        f_out = sem("f_out")
        nf_in = sem("nf_in")
        ring_in = [sem(f"ring_in{n}") for n in range(RING)]
        y_out = [sem(f"y_out{n}") for n in range(2)]
        stored = sem("stored")
        yg_in = [sem(f"yg_in{t}") for t in range(TT)]
        o_out = sem("o_out")

        pool_s = sem("pool_s")
        consts = sem("consts")
        qz_zero = sem("qz_zero")
        dve_s = sem("dve_s")
        act_s = sem("act_s")
        var_ok = sem("var_ok")
        rstd_ok = sem("rstd_ok")
        xn_ok = sem("xn_ok")
        xt_ok = sem("xt_ok")
        hT_a = sem("hT_a")
        hT_v = sem("hT_v")
        fl_mm = sem("fl_mm")
        fl_a = sem("fl_a")
        fl_v = sem("fl_v")
        score = sem("score")
        f_read = sem("f_read")
        f_negm = sem("f_negm")
        f_exp = sem("f_exp")
        f_prob = sem("f_prob")
        s_abs = sem("s_abs")
        s_z = sem("s_z")
        s_ln = sem("s_ln")
        s_sp = sem("s_sp")
        s_msk = sem("s_msk")
        s_u = sem("s_u")
        s_um = sem("s_um")
        s_prob = sem("s_prob")
        pt_mm = sem("pt_mm")
        pt_a = sem("pt_a")
        pt_v = sem("pt_v")
        pv_mm = sem("pv_mm")
        y_sb = sem("y_sb")
        g_mm = sem("g_mm")
        g_exp = sem("g_exp")
        g_ok = sem("g_ok")
        q_mm = sem("q_mm")
        k_mm = sem("k_mm")
        v_mm = sem("v_mm")
        q_sb = sem("q_sb")
        k_sb = sem("k_sb")
        v_sb = sem("v_sb")
        up_mm = sem("up_mm")
        mg = sem("mg")
        o_mm = sem("o_mm")
        o_rd = sem("o_rd")
        h1_ok = sem("h1_ok")
        h1t_mm = sem("h1t_mm")
        h1t_a = sem("h1t_a")
        h1t_v = sem("h1t_v")
        r_mm = sem("r_mm")
        lg_ok = sem("lg_ok")
        part_s = sem("part_s")
        wr_ok = sem("wr_ok")
        gx = sem("gx")
        gx_a = sem("gx_a")
        eh_ok = sem("eh_ok")
        rank_mm = sem("rank_mm")
        oh_ok = sem("oh_ok")
        ctl_ok = sem("ctl_ok")
        ga_mm = sem("ga_mm")
        xg_a = sem("xg_a")
        xg_v = sem("xg_v")
        h1_mm = sem("h1_mm")
        h3_mm = sem("h3_mm")
        si_ok = sem("si_ok")
        hm_ok = sem("hm_ok")
        ht_mm = sem("ht_mm")
        ht_ok = sem("ht_ok")
        ye_mm = sem("ye_mm")
        ye_sb = sem("ye_sb")
        fin_a = sem("fin_a")
        rows_used = sem("rows_used")
        fin_d = sem("fin_d")
        fin_v = sem("fin_v")
        fin_p = sem("fin_p")

        x_t = x[0].rearrange("(t p) d -> t p d", p=P)
        out_t = out[0].rearrange("(t p) d -> t p d", p=P)
        win = w_in[0].rearrange("(k p) c -> p k c", p=P)
        NFOX = PAIRS
        LAST = 2 * PAIRS - 1

        block = ctx.enter_context(nc.Block())

        @block.sync
        def _(sp):
            for t in range(TT):
                sp.dma_start(h[:, t, :], x_t[t]).then_inc(x_in[t], 16)
            sp.dma_start(inT[:, 0, :], ln_in_g.rearrange("(k p) -> p k", p=P),
                             allow_slow_non_contiguous=True).then_inc(inT_in, 16)
            sp.dma_start(inT[:, 1, :], ln_in_b.rearrange("(k p) -> p k", p=P),
                             allow_slow_non_contiguous=True).then_inc(inT_in, 16)
            sp.dma_start(fw[:], win[:, :, 3 * DH:3 * DH + NH]).then_inc(fw_in, 16)

            def load_qkv(col):
                for c in range(3):
                    sp.dma_start(qkvw[:, c, :, :], win[:, :, bass.ds(col + c * DH, P)]).then_inc(qkv_in, 16)

            def load_gates(col):
                sp.dma_start(gatew[:], win[:, :, bass.ds(col, 2 * P)]).then_inc(gw_in, 16)

            def load_negf(head):
                for a in range(2):
                    sp.dma_start(negf[:, a, :], fdram[head + a].partition_broadcast(P)).then_inc(nf_in, 16)

            load_qkv(0)
            load_gates(GATE0)
            sp.dma_start(rows[:, 0, :], ln_in_g.partition_broadcast(P)).then_inc(rows_in[0], 16)
            sp.dma_start(rows[:, 1, :], ln_in_b.partition_broadcast(P)).then_inc(rows_in[0], 16)
            sp.wait_ge(v_mm, 1)
            load_qkv(P)
            sp.wait_ge(f_out, 16)
            sp.wait_ge(fl_mm, 1)
            sp.wait_ge(consts, 9)
            load_negf(0)
            sp.dma_start(wupf[:], w_up_fox[0].rearrange("(k p) n -> p k n", p=P)).then_inc(wup_in, 16)
            sp.dma_start(wups[:], w_up_sb[0].rearrange("(k p) n -> p k n", p=P)).then_inc(wup_in, 16)
            sp.dma_start(wout[:], w_out[0].rearrange("(k p) n -> p k n", p=P)).then_inc(wout_in, 16)
            for n in range(E * CAP, SLOTS, S):
                sp.dma_start(ydram[n:n + S, :], x[0]).then_inc(y_out[n // S % 2], 16)
            sp.wait_ge(rows_used, 1)
            sp.dma_start(rows[:, 0, :], ln1_g[0].partition_broadcast(P)).then_inc(rows_in[1], 16)
            sp.dma_start(rows[:, 1, :], ln1_b[0].partition_broadcast(P)).then_inc(rows_in[1], 16)

            def refill(it, qkv, fox):
                sp.wait_ge(g_mm, 2 * it + 2)
                load_gates(2 * P * it + (GATE0 + 2 * P))
                if fox:
                    sp.wait_ge(f_read, 8 * it + 8)
                    load_negf(2 * it + 2)
                if qkv is not None:
                    sp.wait_ge(k_mm, it + 2)
                    load_qkv(P * it + (2 * P + qkv))

            with sp.Fori(0, NFOX - 2) as it:
                refill(it, 0, True)
            refill(NFOX - 2, SB_SHIFT - NFOX * P, True)
            with sp.Fori(NFOX - 1, LAST - 1) as it:
                refill(it, SB_SHIFT - NFOX * P, False)
            refill(LAST - 1, None, False)

            def load_w(e, half, k):
                slot = 3 * half + k
                if k < 2:
                    src = (w1, w3)[k][0, e].rearrange("(k p) f -> p k f", p=P)
                    sp.dma_start(ring[slot][:].rearrange("p (k f) -> p k f", f=FE), src).then_inc(ring_in[slot], 16)
                else:
                    src = w2[0, e].rearrange("(k p) n -> p k n", p=P)
                    sp.dma_start(ring[slot][:].rearrange("p (k n) -> p k n", n=D), src).then_inc(ring_in[slot], 16)

            sp.wait_ge(pv_mm, 4 * (LAST + 1))
            sp.wait_ge(g_mm, 2 * (LAST + 1))
            sp.wait_ge(y_sb, LAST + 1)
            for k in range(3):
                load_w(0, 0, k)
            load_w(1, 1, 0)
            sp.wait_ge(up_mm, 2 * KT)
            load_w(1, 1, 1)
            load_w(1, 1, 2)
            sp.wait_ge(wr_ok, 1)
            sp.dma_start(wr[:, :, 0:NG], w_group[0].rearrange("(k p) c -> p k c", p=P)).then_inc(wr_in, 16)
            sp.dma_start(wr[:, :, NG:NR], w_expert_router[0].rearrange("(k p) c -> p k c", p=P)).then_inc(wr_in, 16)
            sp.wait_ge(h1_ok, TT)
            sp.dma_start(rows[:, 0, :], ln2_g[0].partition_broadcast(P)).then_inc(rows_in[2], 16)
            sp.dma_start(rows[:, 1, :], ln2_b[0].partition_broadcast(P)).then_inc(rows_in[2], 16)

            def refill_w(done, e, half):
                for k, used in enumerate((h1_mm, h3_mm, ye_mm)):
                    sp.wait_ge(used, done + 1)
                    load_w(e, half, k)

            with sp.Fori(0, MAIN - 1) as g:
                for q in range(QB):
                    refill_w(QB * g + q, QB * g + (q + 2), q % 2)
            for q in range(QB - 2):
                refill_w(QB * (MAIN - 1) + q, QB * (MAIN - 1) + q + 2, q % 2)
            sp.wait_ge(ctl_ok, 1)
            groups = sp.value_load(ctl[0:1, 0:1], min_val=MAIN, max_val=MAIN + MAXOV // QB)
            with sp.If(groups > MAIN):
                with sp.Fori(MAIN, groups) as g:
                    for q in range(QB):
                        e = sp.value_load(ctl[0:1, bass.ds(QB * g + (q + 1 - E), 1)], min_val=0, max_val=E - 1)
                        refill_w(QB * g + (q - 2), e, q % 2)
            with sp.Else():
                sp.nop()
            for n in range(2):
                sp.wait_ge(y_out[n], groups * (QB * 16) + 16)
            sp.sem_inc(stored, 1)
            for t in range(TT):
                sp.wait_ge(fin_p, t + 1)
                sp.dma_start(out_t[t], h[:, t, :]).then_inc(o_out, 16)
            sp.wait_ge(o_out, 16 * TT)

        @block.gpsimd
        def _(pool):
            st = Steps(pool, pool_s)
            pool.dma_start(bfor[:], b_forget[0].rearrange("(h o) -> h o", o=1)).then_inc(bf_in, 16)
            st.mark(pool.memset(ident[:], 0.0))
            st.mark(pool.memset(cmask[:], 0.0))
            st.mark(pool.memset(tri[:], 1.0))
            st.mark(pool.iota(ioi[:], pattern=[[1, QB * CAP]], base=0, channel_multiplier=0))
            st.mark(pool.memset(keep[:], 1.0))
            st.mark(pool.memset(smask[:], 0.0))
            a = st.mark(pool.memset(ones[:], 1.0))
            st.wait(a)
            pool.affine_select(out=ident[:], in_=ident[:], compare_op=ALU.not_equal, fill=1.0, base=0,
                               pattern=[[-1, P]], channel_multiplier=1).then_inc(consts, 1)
            pool.memset(zero[:], 0.0).then_inc(consts, 1)
            pool.affine_select(out=cmask[:], in_=cmask[:], compare_op=ALU.is_ge, fill=-BIG, base=0,
                               pattern=[[-1, P]], channel_multiplier=1).then_inc(consts, 1)
            pool.affine_select(out=keep[:], in_=keep[:], compare_op=ALU.is_gt, fill=0.0, base=0,
                               pattern=[[-1, P]], channel_multiplier=1).then_inc(consts, 1)
            pool.affine_select(out=smask[:], in_=smask[:], compare_op=ALU.is_gt, fill=-BIG, base=0,
                               pattern=[[-1, P]], channel_multiplier=1).then_inc(consts, 1)
            pool.affine_select(out=tri[:], in_=tri[:], compare_op=ALU.is_gt, fill=0.0, base=0,
                               pattern=[[1, P]], channel_multiplier=-1).then_inc(consts, 1)
            b = st.mark(pool.tensor_copy(io[:], ioi[:]))
            st.wait(b)
            pool.tensor_scalar(desc[:], io[:, 0:E], -1.0, float(E), ALU.mult, ALU.add).then_inc(consts, 1)
            pool.tensor_scalar(thr[:], io[:, 0:8], float(CAP), float(CAP), ALU.mult, ALU.add).then_inc(consts, 1)
            pool.tensor_scalar(gw4[:], io[:, 0:4], float(QB), None, ALU.mult).then_inc(consts, 1)
            pool.dma_start(rbias[:, 0:NG], b_group[0].partition_broadcast(P)).then_inc(rb_in, 16)
            pool.dma_start(rbias[:, NG:NR], b_expert_router[0].partition_broadcast(P)).then_inc(rb_in, 16)

            pool.wait_ge(fl_v, 1)
            pool.dma_start(fdram[:, :], fl[:, 2, :]).then_inc(f_out, 16)

            def masks(j):
                for u in range(TT):
                    i = TT - 1 - u
                    dg = slice(i * P, i * P + P)
                    for a in range(2):
                        pool.wait_ge(s_sp, j * 8 + 2 * u + a + 1)
                        pool.tensor_tensor(wa[:, a, dg], wa[:, a, dg], keep[:], ALU.mult).then_inc(s_msk, 1)
                    for a in range(2):
                        pool.wait_ge(s_u, j * 8 + 2 * u + a + 1)
                        pool.tensor_tensor(wb[:, a, dg], wb[:, a, dg], smask[:], ALU.add).then_inc(s_um, 1)

            with pool.Fori(0, PAIRS) as j:
                masks(j)

            pool.wait_ge(up_mm, 2 * KT)
            pool.memset(wr[:], 0.0).then_inc(wr_ok, 1)
            pool.wait_ge(mg, KT)
            pst = Steps(pool, part_s)
            for t in range(TT):
                pool.wait_ge(h1_ok, t + 1)
                pst.done(pool.tensor_copy(parts[:, 0, t, :], h[:, t, :]))
                pst.done(pool.tensor_tensor(parts[:, 1, t, :], h[:, t, :], parts[:, 0, t, :], ALU.subtract))
                for c in range(0, D, D // 4):
                    q = slice(c, c + D // 4)
                    pst.done(pool.tensor_tensor(rest[:], h[:, t, q], parts[:, 0, t, q], ALU.subtract))
                    pst.done(pool.tensor_tensor(parts[:, 2, t, q], rest[:], parts[:, 1, t, q], ALU.subtract))

            pool.wait_ge(stored, 1)
            for t in range(TT):
                for c in range(2):
                    pool.indirect_dma_start(yg[:, c, t, :], None, ydram[:, :],
                                            bass.IndirectOffsetOnAxis(ap=destu[:, c, t:t + 1], axis=0)
                                            ).then_inc(yg_in[t], 16)
            for t in range(TT):
                pool.wait_ge(fin_v, t + 1)
                pool.tensor_tensor(h[:, t, :], h[:, t, :], rows[:, 1, :], ALU.add).then_inc(fin_p, 1)

        @block.scalar
        def _(act):
            st = Steps(act, act_s)

            def rsqrt(n, t):
                act.wait_ge(var_ok, n + 1)
                st.done(act.activation(lnt[:, 1, t:t + 1], lnt[:, 0, t:t + 1], ACT.Ln))
                act.activation(lnt[:, 1, t:t + 1], lnt[:, 1, t:t + 1], ACT.Exp, scale=-0.5).then_inc(rstd_ok, 1)

            for t in range(TT):
                rsqrt(t, t)
            act.wait_ge(inT_in, 32)
            for k in range(0, KT, 2):
                act.wait_ge(xt_ok, k + 1)
                act.activation(hT[:, k, :], ps[:, k, :], ACT.Identity, bias=inT[:, 1, k:k + 1],
                               scale=inT[:, 0, k:k + 1]).then_inc(hT_a, 1)
            act.wait_ge(fl_mm, 1)
            act.wait_ge(bf_in, 16)
            st.done(act.activation(fl[:, 0, :], ps[0:NH, 4, :], ACT.Identity, bias=bfor[:, 0:1]))
            st.done(act.activation(fl[:, 1, :], fl[:, 0, :], ACT.Abs))
            st.done(act.activation(fl[:, 1, :], fl[:, 1, :], ACT.Exp, scale=-1.0))
            act.activation(fl[:, 1, :], fl[:, 1, :], ACT.Ln, bias=1.0).then_inc(fl_a, 1)

            def copy_q(n):
                act.wait_ge(q_mm, n)
                for a in range(2):
                    rows_ = slice(64 * a, 64 * a + 64)
                    act.activation(qz[rows_, a, :], ps[rows_, 5, :], ACT.Copy, scale=SCALE).then_inc(q_sb, 1)

            act.wait_ge(qz_zero, 2)
            copy_q(1)

            def gate_exp(it, c):
                act.wait_ge(g_mm, 2 * it + c + 1)
                act.activation(sg[:, bass.ds(2 * it + c, 1), :], ps[:, 5 + c:6 + c, :], ACT.Exp,
                               scale=-1.0).then_inc(g_exp, 1)

            def attend(j, it, fox, last):
                own = Steps(act, act_s, st.n + 8 * j) if not fox else None
                for u in range(TT):
                    i = TT - 1 - u
                    W = P * (i + 1)
                    if fox:
                        for a in range(2):
                            act.wait_ge(f_negm, j * 8 + 2 * u + a + 1)
                            if u > 0:
                                act.wait_ge(pt_mm, 8 * it + 2 * u + a - 1)
                            act.activation(wc[:, a, 0:W], wa[:, a, 0:W], ACT.Exp, bias=mx[:, 1, 2 * u + a:2 * u + a + 1],
                                           accum_out=rs[:, 0, 2 * u + a:2 * u + a + 1]).then_inc(f_exp, 1)
                    else:
                        for a in range(2):
                            act.wait_ge(s_z, 8 * j + 2 * u + a + 1)
                            act.activation(wa[:, a, 0:W], wb[:, a, 0:W], ACT.Abs).then_inc(s_abs, 1)
                        marks = []
                        for a in range(2):
                            act.wait_ge(s_abs, j * 8 + 2 * u + a + 1)
                            marks.append(own.mark(act.activation(wa[:, a, 0:W], wa[:, a, 0:W], ACT.Exp, scale=-1.0)))
                        for a in range(2):
                            own.wait(marks[a])
                            act.activation(wa[:, a, 0:W], wa[:, a, 0:W], ACT.Ln, bias=1.0).then_inc(s_ln, 1)
                        for a in range(2):
                            act.wait_ge(s_um, j * 8 + 2 * u + a + 1)
                            if u > 0:
                                act.wait_ge(pt_mm, 8 * it + 2 * u + a - 1)
                            act.activation(wc[:, a, 0:W], wb[:, a, 0:W], ACT.Exp).then_inc(s_prob, 1)
                    if u < 2:
                        gate_exp(it, u)
                    if u == 3 and not last:
                        act.wait_ge(score, 8 * it + 8)
                        copy_q(it + 2)
                    act.wait_ge(pt_mm, 8 * it + 2 * u + 1)
                    if u > 0:
                        act.wait_ge(pv_mm, 4 * it + u)
                    act.activation(probT[:, 0, 0:W], ps[:, 2, 0:W], ACT.Copy).then_inc(pt_a, 1)
                act.wait_ge(pv_mm, 4 * it + 4)
                act.activation(yT[:, bass.ds(it, 1), :], ps[:, 4:5, :], ACT.Copy).then_inc(y_sb, 1)
                if own:
                    assert own.n == 8

            act.wait_ge(rows_used, 1)
            with act.Fori(0, PAIRS) as j:
                attend(j, j, True, False)
            with act.Fori(0, PAIRS - 1) as j:
                attend(j, j + PAIRS, False, False)
            attend(PAIRS - 1, LAST, False, True)
            st.n += 8 * PAIRS

            def h1t_copy(t):
                act.wait_ge(h1t_mm, 2 * t + 1)
                if t > 0:
                    act.wait_ge(r_mm, t)
                act.activation(h1T[:, 0:4, :], ps[:, 4, :].rearrange("p (k c) -> p k c", c=P), ACT.Copy
                               ).then_inc(h1t_a, 1)

            for t in range(TT):
                rsqrt(TT + t, t)
                if t > 0:
                    h1t_copy(t - 1)
            h1t_copy(TT - 1)
            act.wait_ge(gx, 1)
            act.activation(gt[:, 1, :, :], gt[:, 0, :, :], ACT.Exp).then_inc(gx_a, 1)
            act.wait_ge(gx, 2)
            act.activation(r4[:, 5, :], r4[:, 4, :], ACT.Exp).then_inc(gx_a, 1)

            def xg_copy(n):
                act.wait_ge(ga_mm, n)
                for b in range(0, 4, 2):
                    act.activation(xg[:, 2 * b:2 * b + 2, :], ps[:, b, :].rearrange("p (k c) -> p k c", k=2),
                                   ACT.Copy).then_inc(xg_a, 1)

            xg_copy(1)
            act.wait_ge(ctl_ok, 1)
            groups = act.value_load(ctl[0:1, 0:1], min_val=MAIN, max_val=MAIN + MAXOV // QB)
            with act.Fori(0, groups) as g:
                for q in range(QB):
                    n = QB * g + q
                    act.wait_ge(h1_mm, n + 1)
                    act.activation(silu[:], ps[:, 4, 0:2 * P], ACT.Silu).then_inc(si_ok, 1)
                    if q == QB - 1:
                        xg_copy(g + 2)
                    act.wait_ge(ye_mm, n + 1)
                    act.wait_ge(y_out[q % 2], 64 * g + 32 * (q // 2) + 16)
                    act.activation(ysb[:, q % 2, :], ps[:, 7, :], ACT.Copy).then_inc(ye_sb, 1)
                    act.wait_ge(ye_sb, n + 1)
                    for half in range(2):
                        dst = ydram[bass.ds(QB * CAP * g + q * CAP, CAP), half * S:(half + 1) * S]
                        act.dma_start(dst, ysb[64 * half:64 * half + 64, q % 2, :]).then_inc(y_out[q % 2], 16)

            for t in range(TT):
                act.wait_ge(yg_in[t], 32)
                act.activation(yg[:, 0, t, :], yg[:, 0, t, :], ACT.Copy, scale=gate[:, 0, t:t + 1]).then_inc(fin_a, 1)
                if t > 0:
                    rsqrt(2 * TT + t - 1, t - 1)
            rsqrt(3 * TT - 1, TT - 1)

        @block.vector
        def _(dve):
            st = Steps(dve, dve_s)

            def norm(n, t, src, dst):
                for c in range(2):
                    a = st.mark(dve.bn_stats(stats[:, t, c, :], src[:, c * S:(c + 1) * S]))
                st.wait(a)
                st.done(dve.bn_aggr(mv[:, t, :], stats[:, t, :, :]))
                v, r0, w = lnt[:, 0, t:t + 1], lnt[:, 1, t:t + 1], lnt[:, 2, t:t + 1]
                dve.tensor_scalar(v, mv[:, t, 1:2], EPS, None, ALU.add).then_inc(var_ok, 1)
                dve.wait_ge(rstd_ok, n + 1)
                st.done(dve.tensor_tensor(w, r0, r0, ALU.mult))
                st.done(dve.tensor_tensor(w, w, v, ALU.mult))
                st.done(dve.tensor_scalar(w, w, -0.5, 1.5, ALU.mult, ALU.add))
                st.done(dve.tensor_tensor(r0, r0, w, ALU.mult))
                return dve.tensor_scalar(dst, src, mv[:, t, 0:1], r0, ALU.subtract, ALU.mult)

            dve.memset(qz[64:128, 0, :], 0.0).then_inc(qz_zero, 1)
            dve.memset(qz[0:64, 1, :], 0.0).then_inc(qz_zero, 1)
            for t in range(TT):
                dve.wait_ge(x_in[t], 16)
                norm(t, t, h[:, t, :], xn[:, t, :]).then_inc(xn_ok, 1)
            dve.wait_ge(inT_in, 32)
            for k in range(1, KT, 2):
                dve.wait_ge(xt_ok, k + 1)
                dve.tensor_scalar(hT[:, k, :], ps[:, k, :], inT[:, 0, k:k + 1], inT[:, 1, k:k + 1],
                                  ALU.mult, ALU.add).then_inc(hT_v, 1)

            def copy_k(n):
                dve.wait_ge(k_mm, n)
                dve.tensor_copy(kT[:], ps[:, 6, :]).then_inc(k_sb, 1)

            def copy_v(n):
                dve.wait_ge(v_mm, n)
                dve.tensor_copy(vp[:].rearrange("p t c -> p (t c)"), ps[:, 7, :]).then_inc(v_sb, 1)

            dve.wait_ge(fl_a, 1)
            dve.wait_ge(consts, 9)
            st.done(dve.scalar_tensor_tensor(out=fl[:, 2, :], in0=fl[:, 0, :], scalar=0.0, in1=fl[:, 1, :],
                                             op0=ALU.min, op1=ALU.subtract))
            st.done(dve.tensor_tensor_scan(fl[:, 3, :], fl[:, 2, :], zero[0:NH, :].to_broadcast([NH, S]), 0.0,
                                           ALU.add, ALU.add))
            dve.tensor_scalar(fl[:, 2, :], fl[:, 3, :], -1.0, None, ALU.mult).then_inc(fl_v, 1)
            copy_k(1)
            copy_v(1)
            dve.wait_ge(rows_in[0], 32)
            dve.wait_ge(xn_ok, TT)
            for t in range(TT):
                a = st.mark(dve.tensor_tensor(h[:, t, :], xn[:, t, :], rows[:, 0, :], ALU.mult))
            for t in range(TT):
                st.wait(a - (TT - 1) + t)
                ins = dve.tensor_tensor(h[:, t, :], h[:, t, :], rows[:, 1, :], ALU.add)
                if t < TT - 1:
                    st.mark(ins)
            ins.then_inc(rows_used, 1)
            dve.wait_ge(rows_used, 1)
            dve.wait_ge(f_out, 16)

            def gate_sum(own, it, c):
                dve.wait_ge(g_exp, 2 * it + c + 1)
                tile = sg[:, bass.ds(2 * it + c, 1), :]
                return own.mark(dve.tensor_scalar(tile, tile, 1.0, None, ALU.add))

            OWN = {True: 2 + 8 + 8 + 8, False: 2 + 8}

            def attend(j, it, fox, last):
                own = Steps(dve, dve_s, st.n + OWN[fox] * j)
                for u in range(TT):
                    i = TT - 1 - u
                    W = P * (i + 1)
                    dg = slice(i * P, i * P + P)
                    if fox:
                        if u == 0:
                            dve.wait_ge(nf_in, 32 * it + 32)
                        for a in range(2):
                            dve.wait_ge(score, 8 * it + 2 * u + a + 1)
                            dve.tensor_tensor(wa[:, a, 0:W], ps[:, a, 0:W], negf[:, a, 0:W],
                                              ALU.add).then_inc(f_read, 1)
                        marks = []
                        for a in range(2):
                            dve.wait_ge(f_read, 8 * j + 2 * u + a + 1)
                            marks.append(own.mark(dve.tensor_tensor(wa[:, a, dg], wa[:, a, dg], cmask[:], ALU.add)))
                        for a in range(2):
                            c = 2 * u + a
                            own.wait(marks[a])
                            marks[a] = own.mark(dve.tensor_reduce(mx[:, 0, c:c + 1], wa[:, a, 0:W], AX.X, ALU.max))
                        for a in range(2):
                            c = 2 * u + a
                            own.wait(marks[a])
                            dve.tensor_scalar(mx[:, 1, c:c + 1], mx[:, 0, c:c + 1], -1.0, None,
                                              ALU.mult).then_inc(f_negm, 1)
                        marks = []
                        for a in range(2):
                            c = 2 * u + a
                            dve.wait_ge(f_exp, 8 * j + c + 1)
                            marks.append(own.mark(dve.reciprocal(rs[:, 1, c:c + 1], rs[:, 0, c:c + 1])))
                        for a in range(2):
                            c = 2 * u + a
                            own.wait(marks[a])
                            dve.tensor_scalar(wc[:, a, 0:W], wc[:, a, 0:W], rs[:, 1, c:c + 1], None,
                                              ALU.mult).then_inc(f_prob, 1)
                    else:
                        for a in range(2):
                            dve.wait_ge(score, 8 * it + 2 * u + a + 1)
                            dve.tensor_copy(wb[:, a, 0:W], ps[:, a, 0:W]).then_inc(s_z, 1)
                        for a in range(2):
                            dve.wait_ge(s_ln, 8 * j + 2 * u + a + 1)
                            dve.wait_ge(s_z, 8 * j + 2 * u + a + 1)
                            dve.scalar_tensor_tensor(out=wa[:, a, 0:W], in0=wb[:, a, 0:W], scalar=0.0,
                                                     in1=wa[:, a, 0:W], op0=ALU.max, op1=ALU.add).then_inc(s_sp, 1)
                        marks = []
                        for a in range(2):
                            dve.wait_ge(s_msk, 8 * j + 2 * u + a + 1)
                            rev = wa[:, a, 0:W][:, ::-1]
                            marks.append(own.mark(dve.tensor_tensor_scan(
                                rev, rev, zero[:, :].to_broadcast([P, W]), 0.0, ALU.add, ALU.add)))
                        for a in range(2):
                            own.wait(marks[a])
                            dve.tensor_tensor(wb[:, a, 0:W], wb[:, a, 0:W], wa[:, a, 0:W],
                                              ALU.subtract).then_inc(s_u, 1)
                    if u < 2:
                        summed = gate_sum(own, it, u)
                        own.wait(summed)
                    dve.wait_ge(pt_mm, 8 * it + 2 * u + 2)
                    if u > 0:
                        dve.wait_ge(pv_mm, 4 * it + u)
                    dve.tensor_copy(probT[:, 1, 0:W], ps[:, 3, 0:W]).then_inc(pt_v, 1)
                    if u < 2:
                        tile = sg[:, bass.ds(2 * it + u, 1), :]
                        dve.reciprocal(tile, tile).then_inc(g_ok, 1)
                if not last:
                    dve.wait_ge(score, 8 * it + 8)
                    copy_k(it + 2)
                    dve.wait_ge(pv_mm, 4 * it + 4)
                    copy_v(it + 2)
                assert own.n == OWN[fox], own.n

            with dve.Fori(0, PAIRS) as j:
                attend(j, j, True, False)
            st.n += OWN[True] * PAIRS
            with dve.Fori(0, PAIRS - 1) as j:
                attend(j, j + PAIRS, False, False)
            attend(PAIRS - 1, LAST, False, True)
            st.n += OWN[False] * PAIRS

            for k in range(KT):
                b = 2 * (k % 2)
                dve.wait_ge(up_mm, 2 * k + 2)
                dve.wait_ge(g_ok, 2 * (LAST + 1))
                st.mark(dve.tensor_tensor(sg[:, k, :], sg[:, k, :], ps[:, b, :], ALU.mult))
                st.done(dve.tensor_tensor(sg[:, KT + k, :], sg[:, KT + k, :], ps[:, b + 1, :], ALU.mult))
                dve.tensor_tensor(sg[:, k, :], sg[:, k, :], sg[:, KT + k, :], ALU.add).then_inc(mg, 1)

            def h1t_copy(t):
                dve.wait_ge(h1t_mm, 2 * t + 2)
                if t > 0:
                    dve.wait_ge(r_mm, t)
                dve.tensor_copy(h1T[:, 4:8, :], ps[:, 5, :].rearrange("p (k c) -> p k c", c=P)).then_inc(h1t_v, 1)

            def logits(t):
                dve.wait_ge(r_mm, t + 1)
                dve.tensor_tensor(lg[:, t, :], ps[:, 6 + t % 2, 0:NR], rbias[:], ALU.add).then_inc(lg_ok, 1)

            dve.wait_ge(rows_in[1], 32)
            dve.wait_ge(rb_in, 32)
            for t in range(TT):
                for c in range(2):
                    half = h[:, t, c * S:(c + 1) * S]
                    dve.wait_ge(o_mm, 2 * t + c + 1)
                    a = dve.scalar_tensor_tensor(out=half, in0=half, scalar=ALPHA, in1=ps[:, 2 * (t % 2) + c, :],
                                                 op0=ALU.mult, op1=ALU.add).then_inc(o_rd, 1)
                dve.wait_ge(o_rd, 2 * t + 2)
                st.done(norm(TT + t, t, h[:, t, :], h[:, t, :]))
                st.done(dve.tensor_tensor(h[:, t, :], h[:, t, :], rows[:, 0, :], ALU.mult))
                dve.tensor_tensor(h[:, t, :], h[:, t, :], rows[:, 1, :], ALU.add).then_inc(h1_ok, 1)
                if t > 0:
                    h1t_copy(t - 1)
                    if t > 1:
                        logits(t - 2)
            logits(TT - 2)
            h1t_copy(TT - 1)
            logits(TT - 1)
            dve.wait_ge(lg_ok, TT)

            gl = lg[:, :, 0:NG]
            el = lg[:, :, NG:NR]

            def row(n):
                return r4[:, n, :]

            def wide(ap, n):
                return ap.unsqueeze(2).to_broadcast([P, TT, n])

            def first_max(vals, eq, key, top, width, drop):
                d = desc[:, E - width:E].unsqueeze(1).to_broadcast([P, TT, width])
                st.done(dve.tensor_reduce(row(top), vals, AX.X, ALU.max))
                st.done(dve.tensor_tensor(eq, vals, wide(row(top), width), ALU.is_equal))
                st.done(dve.tensor_tensor(eq, eq, d, ALU.mult))
                st.done(dve.tensor_reduce(row(drop), eq, AX.X, ALU.max))
                st.done(dve.tensor_tensor(key, d, wide(row(drop), width), ALU.is_equal))

            ghot = gt[:, 2, :, :]
            first_max(gl, gt[:, 3, :, :], ghot, 0, NG, 1)
            dve.tensor_tensor(gt[:, 0, :, :], gl, wide(row(0), NG), ALU.subtract).then_inc(gx, 1)
            st.done(dve.tensor_scalar(gt[:, 3, :, :], ghot, 1.0, BIG, ALU.subtract, ALU.mult))
            st.done(dve.tensor_tensor(rt[0][:].rearrange("p t (g e) -> p t g e", e=EPG),
                                      el.rearrange("p t (g e) -> p t g e", e=EPG),
                                      gt[:, 3, :, :].unsqueeze(3).to_broadcast([P, TT, NG, EPG]), ALU.add))
            first_max(rt[0][:], rt[1][:], rt[2][:], 2, E, 1)
            st.done(dve.scalar_tensor_tensor(out=rt[0][:], in0=rt[2][:], scalar=-2.0 * BIG, in1=rt[0][:],
                                             op0=ALU.mult, op1=ALU.add))
            first_max(rt[0][:], rt[1][:], rt[3][:], 3, E, 1)
            dve.tensor_tensor(ehot[:], rt[2][:], rt[3][:], ALU.add).then_inc(eh_ok, 1)
            dve.tensor_tensor(row(4), row(3), row(2), ALU.subtract).then_inc(gx, 1)
            dve.wait_ge(gx_a, 1)
            st.done(dve.tensor_reduce(row(6), gt[:, 1, :, :], AX.X, ALU.add))
            dve.wait_ge(gx_a, 2)
            st.done(dve.scalar_tensor_tensor(out=row(7), in0=row(5), scalar=1.0, in1=row(6),
                                             op0=ALU.add, op1=ALU.mult))
            st.done(dve.reciprocal(gate[:, 0, :], row(7)))
            st.done(dve.tensor_tensor(gate[:, 1, :], gate[:, 0, :], row(5), ALU.mult))
            dve.wait_ge(rank_mm, 1)
            cnt = ps[:, 7, 0:E]
            st.done(dve.tensor_copy(ov[:, 0, :], cnt))
            st.done(dve.tensor_tensor(cnt8[:], ov[:, 0, :].unsqueeze(2).to_broadcast([P, E, 8]),
                                      thr[:].unsqueeze(1).to_broadcast([P, E, 8]), ALU.is_gt))
            st.done(dve.tensor_reduce(ov[:, 1, :], cnt8[:], AX.X, ALU.add))
            st.done(dve.tensor_tensor_scan(ov[:, 2, :], ov[:, 1, :], zero[:, :].to_broadcast([P, E]), 0.0,
                                           ALU.add, ALU.add))
            st.done(dve.tensor_tensor(ov[:, 1, :], ov[:, 2, :], ov[:, 1, :], ALU.subtract))
            st.done(dve.tensor_scalar(ov[:, 1, :], ov[:, 1, :], float(CAP), float(CAP * (E - 1)), ALU.mult, ALU.add))
            st.done(dve.scalar_tensor_tensor(out=ov[:, 3, :], in0=io[:, 0:E], scalar=float(CAP), in1=ov[:, 1, :],
                                             op0=ALU.mult, op1=ALU.subtract))
            rank = ps[:, 7, P:P + TT * E].rearrange("p (t e) -> p t e", e=E)

            def tiles(ap):
                return ap.unsqueeze(1).to_broadcast([P, TT, E])

            st.done(dve.tensor_copy(rt[4][:], rank))
            st.done(dve.tensor_scalar(rt[5][:], rt[4][:], float(CAP), None, ALU.is_lt))
            st.done(dve.tensor_tensor(rt[5][:], rt[5][:], tiles(ov[:, 3, :]), ALU.mult))
            st.done(dve.tensor_tensor(rt[5][:], rt[5][:], tiles(ov[:, 1, :]), ALU.add))
            st.done(dve.tensor_tensor(rt[4][:], rt[4][:], rt[5][:], ALU.add))
            for c in range(2):
                st.done(dve.tensor_tensor(rt[5 + c][:], rt[4][:], rt[2 + c][:], ALU.mult))
                st.done(dve.tensor_reduce(dest[:, c, :], rt[5 + c][:], AX.X, ALU.add))
            st.done(dve.tensor_copy(dsh[:], dest[:]))

            def one_hot(own, n):
                marks = []
                for t in range(TT):
                    marks.append(own.mark(dve.tensor_scalar(oh[:, t, :], io[:], dsh[:, 0, t:t + 1], None, ALU.is_equal)))
                for t in range(TT):
                    own.wait(marks[t])
                    ins = dve.scalar_tensor_tensor(out=oh[:, t, :], in0=io[:], scalar=dsh[:, 1, t:t + 1],
                                                   in1=oh[:, t, :], op0=ALU.is_equal, op1=ALU.add)
                    ins.then_inc(oh_ok, 1)
                dve.wait_ge(oh_ok, n * 4 + 4)
                own.done(dve.tensor_scalar(dsh[:], dsh[:], float(-QB * CAP), None, ALU.add))

            one_hot(st, 0)
            st.done(dve.tensor_tensor(ovc[:], ov[:, 2, :].unsqueeze(1).to_broadcast([P, MAXOV, E]),
                                      io[:, 0:MAXOV].unsqueeze(2).to_broadcast([P, MAXOV, E]), ALU.is_le))
            st.done(dve.tensor_reduce(eb[:, 1:], ovc[:], AX.X, ALU.add))
            st.done(dve.tensor_scalar(eb[:, 1:], eb[:, 1:], float(E - 1), None, ALU.min))
            st.done(dve.tensor_tensor(cnt8[:, 0, 0:4], ov[:, 2, E - 1:E].to_broadcast([P, 4]), gw4[:], ALU.is_gt))
            st.done(dve.tensor_reduce(eb[:, 0:1], cnt8[:, 0, 0:4], AX.X, ALU.add))
            st.done(dve.tensor_scalar(eb[:, 0:1], eb[:, 0:1], float(MAIN), None, ALU.add))
            st.done(dve.tensor_copy(destu[:], dest[:]))
            dve.tensor_copy(ctl[:], eb[:]).then_inc(ctl_ok, 1)
            dve.wait_ge(ctl_ok, 1)

            def xg_copy(n):
                dve.wait_ge(ga_mm, n)
                for b in range(1, 4, 2):
                    dve.tensor_copy(xg[:, 2 * b:2 * b + 2, :], ps[:, b, :].rearrange("p (k c) -> p k c", k=2)
                                    ).then_inc(xg_v, 1)

            xg_copy(1)
            groups = dve.value_load(ctl[0:1, 0:1], min_val=MAIN, max_val=MAIN + MAXOV // QB)
            with dve.Fori(0, groups) as g:
                own = Steps(dve, dve_s, st.n + (TT + 1) * g)
                one_hot(own, g + 1)
                for q in range(QB):
                    n = QB * g + q
                    dve.wait_ge(si_ok, n + 1)
                    dve.wait_ge(h3_mm, n + 1)
                    dve.tensor_tensor(hm[:], silu[:], ps[:, 5, 0:2 * P], ALU.mult).then_inc(hm_ok, 1)
                    dve.wait_ge(ht_mm, n + 1)
                    dve.tensor_copy(hmT[:].rearrange("p j c -> p (j c)"), ps[:, 6, 0:2 * P]).then_inc(ht_ok, 1)
                xg_copy(g + 2)
                assert own.n == TT + 1
            dve.wait_ge(part_s, PART_STEPS * TT)
            st = Steps(dve, fin_d)
            for t in range(TT):
                a = st.mark(dve.tensor_scalar(h[:, t, :], h[:, t, :], ALPHA, None, ALU.mult))
            st.wait(a)
            dve.wait_ge(rows_in[2], 32)
            for t in range(TT):
                dve.wait_ge(fin_a, t + 1)
                dve.wait_ge(yg_in[t], 32)
                st.done(dve.scalar_tensor_tensor(out=yg[:, 0, t, :], in0=yg[:, 1, t, :], scalar=gate[:, 1, t:t + 1],
                                                 in1=yg[:, 0, t, :], op0=ALU.mult, op1=ALU.add))
                st.done(dve.tensor_tensor(h[:, t, :], h[:, t, :], yg[:, 0, t, :], ALU.add))
                st.done(norm(2 * TT + t, t, h[:, t, :], h[:, t, :]))
                dve.tensor_tensor(h[:, t, :], h[:, t, :], rows[:, 0, :], ALU.mult).then_inc(fin_v, 1)

        @block.tensor
        def _(pe):
            pe.wait_ge(consts, 1)
            pe.wait_ge(xn_ok, TT)
            for k in range(KT):
                for t in range(TT):
                    mm = pe.transpose(ps[:, k, t * P:(t + 1) * P], xn[:, t, k * P:(k + 1) * P], ident[:])
                mm.then_inc(xt_ok, 1)
            pe.wait_ge(fw_in, 16)
            pe.wait_ge(hT_a, KT // 2)
            pe.wait_ge(hT_v, KT // 2)
            for k in range(KT):
                mm = pe.matmul(ps[0:NH, 4, :], fw[:, k, :], hT[:, k, :], start=(k == 0), stop=(k == KT - 1))
            mm.then_inc(fl_mm, 1)

            def project(w, bank, done):
                for k in range(KT):
                    mm = pe.matmul(ps[:, bank, :], w[:, k, :], hT[:, k, :], start=(k == 0), stop=(k == KT - 1))
                mm.then_inc(done, 1)

            def project_v():
                for t in range(TT):
                    for k in range(KT):
                        mm = pe.matmul(ps[:, 7, t * P:(t + 1) * P], hT[:, k, t * P:(t + 1) * P], qkvw[:, 2, k, :],
                                       start=(k == 0), stop=(k == KT - 1))
                mm.then_inc(v_mm, 1)

            pe.wait_ge(qkv_in, 48)
            project(qkvw[:, 0, :, :], 5, q_mm)
            project(qkvw[:, 1, :, :], 6, k_mm)
            project_v()

            def attend(j, it, fox, last):
                read = f_read if fox else s_z

                def scores(u):
                    W = P * (TT - u)
                    i = TT - 1 - u
                    for a in range(2):
                        if u > 0:
                            pe.wait_ge(read, 8 * j + 2 * u + a - 1)
                        pe.matmul(ps[:, a, 0:W], qz[:, a, i * P:(i + 1) * P], kT[:, 0:W],
                                  start=True, stop=True).then_inc(score, 1)

                def turn(u):
                    i = TT - 1 - u
                    for a in range(2):
                        pe.wait_ge(f_prob if fox else s_prob, 8 * j + 2 * u + a + 1)
                        for s in range(i + 1):
                            mm = pe.transpose(ps[:, 2 + a, s * P:(s + 1) * P], wc[:, a, s * P:(s + 1) * P], ident[:])
                        mm.then_inc(pt_mm, 1)

                def values(u):
                    i = TT - 1 - u
                    if u == 0:
                        pe.wait_ge(v_sb, it + 1)
                    pe.wait_ge(pt_a, 4 * it + u + 1)
                    pe.wait_ge(pt_v, 4 * it + u + 1)
                    for s in range(i + 1):
                        for a in range(2):
                            mm = pe.matmul(ps[64 * a:64 * a + 64, 4, i * P:(i + 1) * P], vp[:, s, 64 * a:64 * a + 64],
                                           probT[:, a, s * P:(s + 1) * P], start=(s == 0), stop=(s == i))
                    mm.then_inc(pv_mm, 1)

                def gate_tile(c):
                    if c == 0:
                        pe.wait_ge(gw_in, 16 * it + 16)
                        pe.wait_ge(q_sb, 2 * it + 2)
                    else:
                        pe.wait_ge(k_sb, it + 1)
                    project(gatew[:, :, c * P:(c + 1) * P], 5 + c, g_mm)

                pe.wait_ge(q_sb, 2 * it + 2)
                pe.wait_ge(k_sb, it + 1)
                scores(0)
                gate_tile(0)
                scores(1)
                turn(0)
                gate_tile(1)
                values(0)
                scores(2)
                turn(1)
                if not last:
                    pe.wait_ge(qkv_in, 48 * it + 96)
                    pe.wait_ge(v_sb, it + 1)
                    project_v()
                values(1)
                scores(3)
                turn(2)
                if not last:
                    pe.wait_ge(g_exp, 2 * it + 2)
                    project(qkvw[:, 0, :, :], 5, q_mm)
                values(2)
                turn(3)
                if not last:
                    project(qkvw[:, 1, :, :], 6, k_mm)
                values(3)

            with pe.Fori(0, PAIRS) as j:
                attend(j, j, True, False)
            with pe.Fori(0, PAIRS - 1) as j:
                attend(j, j + PAIRS, False, False)
            attend(PAIRS - 1, LAST, False, True)

            pe.wait_ge(wup_in, 32)
            pe.wait_ge(y_sb, LAST + 1)
            for k in range(KT):
                b = 2 * (k % 2)
                if k >= 2:
                    pe.wait_ge(mg, k - 1)
                for c, w in ((0, wupf), (1, wups)):
                    for e in range(PAIRS):
                        mm = pe.matmul(ps[:, b + c, :], w[:, e, k * P:(k + 1) * P], yT[:, PAIRS * c + e, :],
                                       start=(e == 0), stop=(e == PAIRS - 1))
                    mm.then_inc(up_mm, 1)

            def project_out(t):
                for c in range(2):
                    if t >= 2:
                        pe.wait_ge(o_rd, 2 * (t - 2) + c + 1)
                    for k in range(KT):
                        mm = pe.matmul(ps[:, 2 * (t % 2) + c, :], sg[:, k, t * P:(t + 1) * P],
                                       wout[:, k, c * S:(c + 1) * S], start=(k == 0), stop=(k == KT - 1))
                    mm.then_inc(o_mm, 1)

            def turn_h1(t):
                pe.wait_ge(h1_ok, t + 1)
                for c in range(2):
                    if t > 0:
                        pe.wait_ge((h1t_a, h1t_v)[c], t)
                    for k in range(4):
                        mm = pe.transpose(ps[:, 4 + c, k * P:(k + 1) * P], h[:, t, (4 * c + k) * P:(4 * c + k + 1) * P],
                                          ident[:])
                    mm.then_inc(h1t_mm, 1)

            def route(t):
                if t == 0:
                    pe.wait_ge(wr_in, 32)
                if t >= 2:
                    pe.wait_ge(lg_ok, t - 1)
                pe.wait_ge(h1t_a, t + 1)
                pe.wait_ge(h1t_v, t + 1)
                for k in range(KT):
                    mm = pe.matmul(ps[:, 6 + t % 2, 0:P], h1T[:, k, :], wr[:, k, :],
                                   start=(k == 0), stop=(k == KT - 1))
                mm.then_inc(r_mm, 1)

            pe.wait_ge(wout_in, 16)
            pe.wait_ge(mg, KT)
            project_out(0)
            project_out(1)
            turn_h1(0)
            project_out(2)
            route(0)
            turn_h1(1)
            project_out(3)
            route(1)
            turn_h1(2)
            route(2)
            turn_h1(3)
            route(3)

            pe.wait_ge(eh_ok, 1)
            for t in range(TT):
                for s in range(t + 1):
                    pe.matmul(ps[:, 7, P + t * E:P + (t + 1) * E], (tri if s == t else ones)[:], ehot[:, s, :],
                              start=(s == 0), stop=(s == t))
            for s in range(TT):
                mm = pe.matmul(ps[:, 7, 0:E], ones[:], ehot[:, s, :], start=(s == 0), stop=(s == TT - 1))
            mm.then_inc(rank_mm, 1)

            def gather(dk):
                for t in range(TT):
                    for c in range(3):
                        mm = pe.matmul(ps[:, dk // 2, (dk % 2) * 256:(dk % 2) * 256 + 256],
                                       parts[:, c, t, dk * P:(dk + 1) * P], oh[:, t, :],
                                       start=(t == 0 and c == 0), stop=(t == TT - 1 and c == 2))
                return mm

            pe.wait_ge(oh_ok, TT)
            pe.wait_ge(part_s, PART_STEPS * TT)
            for dk in range(KT):
                mm = gather(dk)
            mm.then_inc(ga_mm, 1)

            pe.wait_ge(ctl_ok, 1)
            groups = pe.value_load(ctl[0:1, 0:1], min_val=MAIN, max_val=MAIN + MAXOV // QB)
            with pe.Fori(0, groups) as g:
                for q in range(QB):
                    n = QB * g + q
                    slots = range(3 * (q % 2), 3 * (q % 2) + 3)
                    loaded = 32 * g + 16 * (q // 2) + 16
                    if q == 0:
                        pe.wait_ge(xg_a, 2 * g + 2)
                        pe.wait_ge(xg_v, 2 * g + 2)
                    for c, done in ((0, h1_mm), (1, h3_mm)):
                        pe.wait_ge(ring_in[slots[c]], loaded)
                        w = ring[slots[c]]
                        for k in range(KT):
                            for half in range(2):
                                mm = pe.matmul(ps[64 * half:64 * half + 64, 4 + c, 0:256],
                                               xg[:, k, q * CAP:(q + 1) * CAP],
                                               w[:, k * FE + half * 256:k * FE + half * 256 + 256],
                                               start=(k == 0), stop=(k == KT - 1))
                        mm.then_inc(done, 1)
                    if q == 0:
                        pe.wait_ge(oh_ok, TT * g + 2 * TT)
                    gather(2 * q)
                    pe.wait_ge(hm_ok, n + 1)
                    for c in range(2):
                        mm = pe.transpose(ps[:, 6, c * P:(c + 1) * P], hm[:, c * P:(c + 1) * P], ident[:])
                    mm.then_inc(ht_mm, 1)
                    mm = gather(2 * q + 1)
                    if q == QB - 1:
                        mm.then_inc(ga_mm, 1)
                    pe.wait_ge(ht_ok, n + 1)
                    pe.wait_ge(ring_in[slots[2]], loaded)
                    w = ring[slots[2]]
                    for k in range(FT):
                        for half in range(2):
                            mm = pe.matmul(ps[64 * half:64 * half + 64, 7, :],
                                           hmT[:, k % 2, 64 * (k // 2):64 * (k // 2) + 64],
                                           w[:, k * D + half * S:k * D + half * S + S],
                                           start=(k == 0), stop=(k == FT - 1))
                    mm.then_inc(ye_mm, 1)


_INS = ['x', 'ln_in_g', 'ln_in_b', 'w_in', 'b_forget', 'w_up_fox', 'w_up_sb', 'w_out', 'ln1_g', 'ln1_b',
        'w_group', 'b_group', 'w_expert_router', 'b_expert_router', 'w1', 'w3', 'w2', 'ln2_g', 'ln2_b']


def kernel(**inputs):
    import numpy as _np
    import concourse.bacc as _bacc
    from concourse import mybir as _mybir
    from concourse.bass_utils import run_bass_kernel_spmd as _run

    nc = _bacc.Bacc("TRN2", target_bir_lowering=False, num_devices=1)
    arrays, args = {}, []
    for name in _INS:
        a = _np.ascontiguousarray(inputs[name])
        arrays[f"in_{name}_dram"] = a
        args.append(nc.dram_tensor(f"in_{name}_dram", a.shape, _mybir.dt.from_np(a.dtype), kind="ExternalInput").ap())
    args.append(nc.dram_tensor("out_0_dram", (1, S, D), F32, kind="ExternalOutput").ap())
    build(nc, *args)
    res = _run(nc, [arrays], core_ids=[0])
    return res.results[0]["out_0_dram"]
```

```python
from contextlib import ExitStack

import concourse.bass as bass
from concourse import mybir

ALU = mybir.AluOpType
ACT = mybir.ActivationFunctionType
AX = mybir.AxisListType
F32 = mybir.dt.float32
F32R = mybir.dt.float32r
BF16 = mybir.dt.bfloat16
I32 = mybir.dt.int32
U32 = mybir.dt.uint32

P = 128
D = 1024
S = 512
KT = D // P
TT = S // P
HD = 64
NH = 8
PAIRS = NH * HD // P
DH = NH * HD
SCALE = HD ** -0.5
GATE0 = 6 * DH + NH
SB_SHIFT = 3 * DH + NH
E = 32
NG = 4
EPG = E // NG
FE = 512
FT = FE // P
CAP = 64
QB = 4
MAIN = E // QB
MAXOV = 16
SLOTS = (E + MAXOV) * CAP
NR = NG + E
ALPHA = 2.0 ** 0.25
EPS = 1e-5
BIG = 1e30
UP_ROWS = [[0], [1, 2], [3, 4], [5, 6, 7]]
UP_BANK = [7, 5, 6, 7, 5, 6, 7, 5]
PART_STEPS = 10
KORD = [4, 5, 6, 7, 0, 1, 2, 3]
EXP_LN = "natural_log_exp_and_others"
RING = 6
UNIT = 4096


class Steps:

    def __init__(self, eng, sem, base=0):
        self.eng, self.sem, self.base, self.n = eng, sem, base, 0

    def mark(self, ins):
        self.n += 1
        ins.then_inc(self.sem, 1)
        return self.base + self.n

    def wait(self, value):
        self.eng.wait_ge(self.sem, value)

    def done(self, ins):
        self.wait(self.mark(ins))


def build(nc, x, ln_in_g, ln_in_b, w_in, b_forget, w_up_fox, w_up_sb, w_out, ln1_g, ln1_b,
          w_group, b_group, w_expert_router, b_expert_router, w1, w3, w2, ln2_g, ln2_b, out):
    ctx = ExitStack()
    with ctx:
        base = (nc.sbuf_base + 63) // 64 * 64

        def at(name, offset, shape, dt=F32):
            return nc.alloc_sbuf_tensor_at(name, [shape[0]] + list(shape[1:]), dt, offset=offset)

        KB = 1024
        r = [base + 16 * KB * n for n in range(RING)]
        ring = [at(f"ring{n}", r[n], [P, UNIT]) for n in range(RING)]
        g_hi = at("g_hi", r[0], [P, 2, KT, P], F32R)
        g_lo = at("g_lo", r[0] + 8 * KB, [P, 2, KT, P], F32R)
        g_raw = at("g_raw", r[0] + 8 * KB, [P, 2, KT, P])
        w_hi = at("w_hi", r[1], [P, 3, KT, P], F32R)
        probT = at("probT", r[1] + 12 * KB, [P, 2, S])
        wa = at("wa", r[2], [P, 2, S])
        wb = at("wb", r[2] + 4 * KB, [P, 2, S])
        wc = at("wc", r[2] + 8 * KB, [P, 2, S])
        negf = at("negf", r[2] + 12 * KB, [P, 2, S])
        qz = at("qz", r[3], [P, 2, S])
        kT = at("kT", r[3] + 4 * KB, [P, S])
        vp = at("vp", r[3] + 6 * KB, [P, TT, P])
        vT = at("vT", r[3] + 8 * KB, [P, S])
        gexp = at("gexp", r[3] + 12 * KB, [P, 2, S])
        wupf = at("wupf", r[4], [P, PAIRS, D])
        w_lo = at("w_lo", r[5], [P, 3, KT, P], F32R)
        w_raw = at("w_raw", r[5], [P, 3, KT, P])
        wups = at("wups", r[5], [P, PAIRS, D])
        wus_lo = at("wus_lo", r[5], [P, PAIRS, D], F32R)
        wus_hi = at("wus_hi", r[0], [P, PAIRS, D], F32R)
        wo_hi = at("wo_hi", r[1], [P, KT, D], F32R)
        mg_hi = at("mg_hi", r[3], [P, KT, S], F32R)
        b0 = base + 16 * KB * RING
        h = at("h", b0, [P, TT, D])
        b1 = b0 + 16 * KB
        hTf = at("hTf", b1 + 16 * KB, [P, KT, S])
        sg = at("sg", b1, [P, 2 * KT, S])
        mg_lo = at("mg_lo", b1, [P, KT, S], F32R)
        xn = at("xn", b1, [P, TT, D])
        parts = at("parts", b1 + 16 * KB, [P, 3, TT, D], BF16)
        b2 = b1 + 32 * KB
        yT = at("yT", b2, [P, 2 * PAIRS, S])
        ys_hi = at("ys_hi", b2, [P, PAIRS, S], F32R)
        ys_lo = at("ys_lo", b2 + 8 * KB, [P, PAIRS, S], F32R)
        wr = at("wr", b2 + 8 * KB, [P, KT, P])
        h1T = at("h1T", b2 + 12 * KB, [P, KT, P])
        b3 = b2 + 16 * KB
        hT_hi = at("hT_hi", b3, [P, KT, S], F32R)
        hT_lo = at("hT_lo", b3 + 16 * KB, [P, KT, S], F32R)
        wo_lo = at("wo_lo", b3, [P, KT, D], F32R)
        wout = at("wout", b3, [P, KT, D])
        w2buf = [ring[2], ring[5], at("w2_2", b1, [P, UNIT]), at("w2_3", b2 + 8 * KB, [P, UNIT])]
        xg = at("xg", b3 + 8 * KB, [P, KT, QB * CAP])
        oh = at("oh", b3 + 16 * KB, [P, TT, QB * CAP], BF16)
        silu = at("silu", b3 + 18 * KB, [P, 2 * P])
        hm = at("hm", b3 + 19 * KB, [P, 2 * P])
        hmT = at("hmT", b3 + 20 * KB, [P, 2, P])
        ysb = at("ysb", b3 + 22 * KB, [P, 2, S])
        rt = [at(f"rt{n}", b3 + 26 * KB + 512 * n, [P, TT, E]) for n in range(8)]
        ovc = at("ovc", b3 + 30 * KB, [P, MAXOV, E])
        cnt8 = at("cnt8", b3 + 18 * KB, [P, E, 8])
        ehot = at("ehot", b3 + 19 * KB, [P, TT, E], BF16)
        b4 = b3 + 32 * KB
        rows = at("rows", b4, [P, 2, D])
        cur = b4 + 8 * KB
        small = {}

        def sm(name, shape, dt=F32):
            nonlocal cur
            n = 1
            for s in shape[1:]:
                n *= s
            small[name] = at(name, cur, shape, dt)
            cur += (n * (2 if dt == BF16 else 4) + 31) // 32 * 32
            return small[name]

        ident = sm("ident", [P, P])
        cmask = sm("cmask", [P, P])
        keep = sm("keep", [P, P])
        smask = sm("smask", [P, P])
        tri = sm("tri", [P, P], BF16)
        ones = sm("ones", [P, P], BF16)
        io = sm("io", [P, QB * CAP])
        desc = sm("desc", [P, E])
        thr = sm("thr", [P, 8])
        zero = sm("zero", [P, 1])
        inT = sm("inT", [P, 2, KT])
        bfor = sm("bfor", [NH, 1])
        rbias = sm("rbias", [P, NR])
        stats = sm("stats", [P, TT, 2, 6])
        mv = sm("mv", [P, TT, 2])
        lnt = sm("lnt", [P, 4, TT])
        mx = sm("mx", [P, 2, 8])
        rs = sm("rs", [P, 2, 8])
        lg = sm("lg", [P, TT, NR])
        gt = sm("gt", [P, 4, TT, NG])
        r4 = sm("r4", [P, 12, TT])
        gate = sm("gate", [P, 2, TT])
        dest = sm("dest", [P, 2, TT])
        dsh = sm("dsh", [P, 2, TT])
        destu = sm("destu", [P, 2, TT], U32)
        ov = sm("ov", [P, 4, E])
        eb = sm("eb", [P, MAXOV + 1])
        ctl = sm("ctl", [P, MAXOV + 1], I32)
        gw4 = sm("gw4", [P, 4])
        rest = sm("rest", [P, D // 4])
        assert cur <= nc.sbuf_usable_end, (cur, nc.sbuf_usable_end)
        f_hi = at("f_hi", r[3] + 10 * KB, [P, KT, NH], F32R)
        f_lo = at("f_lo", r[3] + 11 * KB, [P, KT, NH], F32R)
        f_raw = at("f_raw", r[3] + 11 * KB, [P, KT, NH])
        fl = at("fl", r[2], [NH, 4, S])
        ioi = at("ioi", cur - QB * CAP * 4, [P, QB * CAP], I32)
        yg = at("yg", r[0], [P, 2, TT, D])

        ps = ctx.enter_context(nc.psum_tensor("ps", [P, 8, S], F32))
        fdram = nc.dram_tensor("forget_sums", (NH, S), F32, kind="Internal").ap()
        ydram = nc.dram_tensor("y_by_slot", (SLOTS, D), F32, kind="Internal").ap()

        def sem(name):
            return ctx.enter_context(nc.semaphore(name))

        x_in = [sem(f"x_in{t}") for t in range(TT)]
        rows_in = [sem(f"rows_in{n}") for n in range(3)]
        inT_in = sem("inT_in")
        rb_in = sem("rb_in")
        bf_in = sem("bf_in")
        NAMES = ("q", "k", "v", "gate0", "gate1", "forget")
        raw_in = [sem(f"raw_{n}") for n in NAMES]
        hi_ok = [sem(f"hi_{n}") for n in NAMES]
        lo_ok = [sem(f"lo_{n}") for n in NAMES]
        wupf_in = sem("wupf_in")
        wups_in = sem("wups_in")
        wout_in = sem("wout_in")
        wr_in = sem("wr_in")
        f_out = sem("f_out")
        nf_in = sem("nf_in")
        ring_in = [sem(f"ring_in{n}") for n in range(RING)]
        w2_in = [sem(f"w2_in{n}") for n in range(QB)]
        y_out = [sem(f"y_out{n}") for n in range(2)]
        stored = sem("stored")
        yg_in = [sem(f"yg_in{t}") for t in range(TT)]
        o_out = sem("o_out")

        pool_s = sem("pool_s")
        consts = sem("consts")
        qz_zero = sem("qz_zero")
        dve_s = sem("dve_s")
        act_s = sem("act_s")
        var_ok = sem("var_ok")
        rstd_ok = sem("rstd_ok")
        xn_ok = sem("xn_ok")
        xt_ok = sem("xt_ok")
        hT_h = sem("hT_h")
        hT_t = sem("hT_t")
        hT_p = sem("hT_p")
        hT_v = sem("hT_v")
        fl_mm = sem("fl_mm")
        fl_a = sem("fl_a")
        fl_v = sem("fl_v")
        score = sem("score")
        f_read = sem("f_read")
        f_negm = sem("f_negm")
        f_exp = sem("f_exp")
        f_prob = sem("f_prob")
        s_abs = sem("s_abs")
        s_z = sem("s_z")
        s_ln = sem("s_ln")
        s_um = sem("s_um")
        s_prob = sem("s_prob")
        pt_mm = sem("pt_mm")
        pt_a = sem("pt_a")
        pt_v = sem("pt_v")
        pv_mm = sem("pv_mm")
        y_sb = sem("y_sb")
        g_mm = sem("g_mm")
        g_exp = sem("g_exp")
        g_ok = sem("g_ok")
        q_mm = sem("q_mm")
        k_mm = sem("k_mm")
        v_mm = sem("v_mm")
        q_sb = sem("q_sb")
        k_sb = sem("k_sb")
        v_sb = sem("v_sb")
        vt_sb = sem("vt_sb")
        vt_mm = sem("vt_mm")
        ups_hi = sem("ups_hi")
        ups_lo = sem("ups_lo")
        ysb_hi = sem("ysb_hi")
        ysb_lo = sem("ysb_lo")
        wo_h = sem("wo_h")
        wo_l = sem("wo_l")
        mg_f = sem("mg_f")
        mg_h = sem("mg_h")
        up_mm = sem("up_mm")
        upf_mm = sem("upf_mm")
        upf_rd = sem("upf_rd")
        mg = sem("mg")
        o_mm = sem("o_mm")
        o_rd = sem("o_rd")
        h1_ok = sem("h1_ok")
        h1t_mm = sem("h1t_mm")
        h1t_a = sem("h1t_a")
        h1t_v = sem("h1t_v")
        r_mm = sem("r_mm")
        lg_ok = sem("lg_ok")
        part_s = sem("part_s")
        wr_ok = sem("wr_ok")
        gx = sem("gx")
        gx_a = sem("gx_a")
        eh_ok = sem("eh_ok")
        rank_mm = sem("rank_mm")
        oh_ok = sem("oh_ok")
        ctl_ok = sem("ctl_ok")
        ga_mm = sem("ga_mm")
        xg_a = sem("xg_a")
        xg_v = sem("xg_v")
        h1_mm = sem("h1_mm")
        h3_mm = sem("h3_mm")
        si_ok = sem("si_ok")
        hm_ok = sem("hm_ok")
        ht_mm = sem("ht_mm")
        ht_ok = sem("ht_ok")
        ye_mm = sem("ye_mm")
        ye_sb = sem("ye_sb")
        fin_a = sem("fin_a")
        rows_used = sem("rows_used")
        fin_d = sem("fin_d")
        fin_h = sem("fin_h")
        fin_s = sem("fin_s")
        fin_r = sem("fin_r")
        fin_n = sem("fin_n")
        fin_l = sem("fin_l")
        fin_v = sem("fin_v")
        fin_p = sem("fin_p")

        x_t = x[0].rearrange("(t p) d -> t p d", p=P)
        out_t = out[0].rearrange("(t p) d -> t p d", p=P)
        win = w_in[0].rearrange("(k p) c -> p k c", p=P)
        NFOX = PAIRS
        Q, K, V, G0, FORGET = 0, 1, 2, 3, 5
        high = [w_hi[:, 0], w_hi[:, 1], w_hi[:, 2], g_hi[:, 0], g_hi[:, 1], f_hi[:]]
        low = [w_lo[:, 0], w_lo[:, 1], w_lo[:, 2], g_lo[:, 0], g_lo[:, 1], f_lo[:]]
        raw = [w_raw[:, 0], w_raw[:, 1], w_raw[:, 2], g_raw[:, 0], g_raw[:, 1], f_raw[:]]
        LAST = 2 * PAIRS - 1

        block = ctx.enter_context(nc.Block())

        @block.sync
        def _(sp):
            for t in range(TT):
                sp.dma_start(h[:, t, :], x_t[t]).then_inc(x_in[t], 16)
            sp.dma_start(inT[:, 0, :], ln_in_g.rearrange("(k p) -> p k", p=P),
                             allow_slow_non_contiguous=True).then_inc(inT_in, 16)
            sp.dma_start(inT[:, 1, :], ln_in_b.rearrange("(k p) -> p k", p=P),
                             allow_slow_non_contiguous=True).then_inc(inT_in, 16)
            def load_raw(c, col):
                width = NH if c == FORGET else P
                sp.dma_start(raw[c], win[:, :, bass.ds(col, width)]).then_inc(raw_in[c], 16)

            def load_negf(head):
                for a in range(2):
                    sp.dma_start(negf[:, a, :], fdram[head + a].partition_broadcast(P)).then_inc(nf_in, 16)

            load_raw(FORGET, 3 * DH)
            for c in (Q, K, V):
                load_raw(c, c * DH)
            for c in range(2):
                load_raw(G0 + c, GATE0 + c * P)
            sp.dma_start(rows[:, 0, :], ln_in_g.partition_broadcast(P)).then_inc(rows_in[0], 16)
            sp.dma_start(rows[:, 1, :], ln_in_b.partition_broadcast(P)).then_inc(rows_in[0], 16)
            for c, done in ((Q, q_mm), (K, k_mm), (V, v_mm)):
                sp.wait_ge(done, 1)
                load_raw(c, P + c * DH)
            sp.wait_ge(f_out, 16)
            load_negf(0)
            sp.dma_start(wupf[:], w_up_fox[0].rearrange("(k p) n -> p k n", p=P)).then_inc(wupf_in, 16)
            for n in range(E * CAP, SLOTS, S):
                sp.dma_start(ydram[n:n + S, :], x[0]).then_inc(y_out[n // S % 2], 16)
            sp.wait_ge(rows_used, 1)
            sp.dma_start(rows[:, 0, :], ln1_g[0].partition_broadcast(P)).then_inc(rows_in[1], 16)
            sp.dma_start(rows[:, 1, :], ln1_b[0].partition_broadcast(P)).then_inc(rows_in[1], 16)

            def refill(it, qkv, fox):
                for c in range(2):
                    sp.wait_ge(g_mm, 2 * it + 1 + c)
                    load_raw(G0 + c, 2 * P * it + (GATE0 + 2 * P + c * P))
                if qkv is not None:
                    for c, done in ((V, v_mm), (Q, q_mm), (K, k_mm)):
                        sp.wait_ge(done, it + 2)
                        load_raw(c, P * it + (2 * P + qkv + c * DH))
                if fox:
                    sp.wait_ge(f_read, 8 * it + 8)
                    load_negf(2 * it + 2)

            with sp.Fori(0, NFOX - 2) as it:
                refill(it, 0, True)
            refill(NFOX - 2, SB_SHIFT - NFOX * P, True)
            with sp.Fori(NFOX - 1, LAST - 1) as it:
                refill(it, SB_SHIFT - NFOX * P, False)
            refill(LAST - 1, None, False)
            sp.wait_ge(k_mm, LAST + 1)
            sp.dma_start(wups[:], w_up_sb[0].rearrange("(k p) n -> p k n", p=P)).then_inc(wups_in, 16)
            sp.wait_ge(g_mm, 2 * (LAST + 1))
            sp.dma_start(wout[:], w_out[0].rearrange("(k p) n -> p k n", p=P)).then_inc(wout_in, 16)

            def load_w13(e, half, k):
                slot = 3 * half + k
                src = (w1, w3)[k][0, e].rearrange("(k p) f -> p k f", p=P)
                sp.dma_start(ring[slot][:].rearrange("p (k f) -> p k f", f=FE), src).then_inc(ring_in[slot], 16)

            def load_w2(e, place):
                src = w2[0, e].rearrange("(k p) n -> p k n", p=P)
                sp.dma_start(w2buf[place][:].rearrange("p (k n) -> p k n", n=D), src).then_inc(w2_in[place], 16)

            sp.wait_ge(upf_mm, KT)
            load_w13(1, 1, 1)
            sp.wait_ge(up_mm, KT)
            load_w13(0, 0, 0)
            load_w2(1, 1)
            sp.wait_ge(wr_ok, 1)
            sp.dma_start(wr[:, :, 0:NG], w_group[0].rearrange("(k p) c -> p k c", p=P)).then_inc(wr_in, 16)
            sp.dma_start(wr[:, :, NG:NR], w_expert_router[0].rearrange("(k p) c -> p k c", p=P)).then_inc(wr_in, 16)
            sp.wait_ge(o_mm, 2 * TT)
            load_w13(0, 0, 1)
            load_w2(0, 0)
            load_w13(1, 1, 0)
            load_w2(2, 2)
            sp.wait_ge(h1_ok, TT)
            sp.dma_start(rows[:, 0, :], ln2_g[0].partition_broadcast(P)).then_inc(rows_in[2], 16)
            sp.dma_start(rows[:, 1, :], ln2_b[0].partition_broadcast(P)).then_inc(rows_in[2], 16)
            sp.wait_ge(r_mm, TT)
            load_w2(3, 3)

            def refill_w13(done, e, half):
                for k, used in enumerate((h1_mm, h3_mm)):
                    sp.wait_ge(used, done + 1)
                    load_w13(e, half, k)

            with sp.Fori(0, MAIN - 1) as g:
                for q in range(QB):
                    refill_w13(QB * g + q, QB * g + (q + 2), q % 2)
                    sp.wait_ge(ye_mm, QB * g + q + 1)
                    load_w2(QB * g + (q + QB), q)
            for q in range(QB - 2):
                refill_w13(QB * (MAIN - 1) + q, QB * (MAIN - 1) + q + 2, q % 2)
            sp.wait_ge(ctl_ok, 1)
            groups = sp.value_load(ctl[0:1, 0:1], min_val=MAIN, max_val=MAIN + MAXOV // QB)
            with sp.If(groups > MAIN):
                with sp.Fori(MAIN, groups) as g:
                    for q in range(QB):
                        e = sp.value_load(ctl[0:1, bass.ds(QB * g + (q + 1 - E), 1)], min_val=0, max_val=E - 1)
                        refill_w13(QB * g + (q - 2), e, q % 2)
                        sp.wait_ge(ye_mm, QB * g + (q - QB + 1))
                        load_w2(e, q)
            with sp.Else():
                sp.nop()
            for n in range(2):
                sp.wait_ge(y_out[n], groups * (QB * 16) + 16)
            sp.sem_inc(stored, 1)
            for t in range(TT):
                if t < TT - 1:
                    sp.wait_ge(fin_p, t + 1)
                else:
                    sp.wait_ge(fin_l, 1)
                sp.dma_start(out_t[t], h[:, t, :]).then_inc(o_out, 16)
            sp.wait_ge(o_out, 16 * TT)

        @block.gpsimd
        def _(pool):
            st = Steps(pool, pool_s)
            pool.dma_start(bfor[:], b_forget[0].rearrange("(h o) -> h o", o=1)).then_inc(bf_in, 16)
            st.mark(pool.memset(ident[:], 0.0))
            st.mark(pool.memset(cmask[:], 0.0))
            st.mark(pool.memset(tri[:], 1.0))
            st.mark(pool.iota(ioi[:], pattern=[[1, QB * CAP]], base=0, channel_multiplier=0))
            st.mark(pool.memset(keep[:], 1.0))
            st.mark(pool.memset(smask[:], 0.0))
            a = st.mark(pool.memset(ones[:], 1.0))
            st.wait(a)
            pool.affine_select(out=ident[:], in_=ident[:], compare_op=ALU.not_equal, fill=1.0, base=0,
                               pattern=[[-1, P]], channel_multiplier=1).then_inc(consts, 1)
            pool.memset(zero[:], 0.0).then_inc(consts, 1)
            pool.affine_select(out=cmask[:], in_=cmask[:], compare_op=ALU.is_ge, fill=-BIG, base=0,
                               pattern=[[-1, P]], channel_multiplier=1).then_inc(consts, 1)
            pool.affine_select(out=keep[:], in_=keep[:], compare_op=ALU.is_gt, fill=0.0, base=0,
                               pattern=[[-1, P]], channel_multiplier=1).then_inc(consts, 1)
            pool.affine_select(out=smask[:], in_=smask[:], compare_op=ALU.is_gt, fill=-BIG, base=0,
                               pattern=[[-1, P]], channel_multiplier=1).then_inc(consts, 1)
            pool.affine_select(out=tri[:], in_=tri[:], compare_op=ALU.is_gt, fill=0.0, base=0,
                               pattern=[[1, P]], channel_multiplier=-1).then_inc(consts, 1)
            b = st.mark(pool.tensor_copy(io[:], ioi[:]))
            st.wait(b)
            pool.tensor_scalar(desc[:], io[:, 0:E], -1.0, float(E), ALU.mult, ALU.add).then_inc(consts, 1)
            pool.tensor_scalar(thr[:], io[:, 0:8], float(CAP), float(CAP), ALU.mult, ALU.add).then_inc(consts, 1)
            pool.tensor_scalar(gw4[:], io[:, 0:4], float(QB), None, ALU.mult).then_inc(consts, 1)
            pool.dma_start(rbias[:, 0:NG], b_group[0].partition_broadcast(P)).then_inc(rb_in, 16)
            pool.dma_start(rbias[:, NG:NR], b_expert_router[0].partition_broadcast(P)).then_inc(rb_in, 16)

            for c in (FORGET, Q, K, V):
                pool.wait_ge(hi_ok[c], 1)
                pool.tensor_tensor(low[c], raw[c], high[c].bitcast(F32),
                                   ALU.subtract).then_inc(lo_ok[c], 1)
            for n in range(0, KT, 2):
                k = KORD[n]
                pool.wait_ge(hT_t, n + 1)
                pool.tensor_tensor(hT_lo[:, k, :], hTf[:, k, :], hT_hi[:, k, :].bitcast(F32),
                                   ALU.subtract).then_inc(hT_p, 1)
            for c in (G0, G0 + 1):
                pool.wait_ge(hi_ok[c], 1)
                pool.tensor_tensor(low[c], raw[c], high[c].bitcast(F32),
                                   ALU.subtract).then_inc(lo_ok[c], 1)
            pool.wait_ge(fl_v, 1)
            pool.dma_start(fdram[:, :], fl[:, 2, :]).then_inc(f_out, 16)

            def split_lo(c, n):
                pool.wait_ge(hi_ok[c], n)
                pool.tensor_tensor(low[c], raw[c], high[c].bitcast(F32),
                                   ALU.subtract).then_inc(lo_ok[c], 1)

            with pool.Fori(0, LAST) as it:
                for c in (V, Q, K, G0, G0 + 1):
                    split_lo(c, it + 2)

            for e in range(PAIRS):
                pool.wait_ge(ups_hi, e + 1)
                pool.tensor_tensor(wus_lo[:, e, :], wups[:, e, :], wus_hi[:, e, :].bitcast(F32),
                                   ALU.subtract).then_inc(ups_lo, 1)
            for k in range(KT):
                pool.wait_ge(wo_h, k + 1)
                pool.tensor_tensor(wo_lo[:, k, :], wout[:, k, :], wo_hi[:, k, :].bitcast(F32),
                                   ALU.subtract).then_inc(wo_l, 1)
            pool.wait_ge(up_mm, KT)
            pool.memset(wr[:], 0.0).then_inc(wr_ok, 1)
            pool.wait_ge(mg, KT)
            pst = Steps(pool, part_s)
            for t in range(TT):
                pool.wait_ge(h1_ok, t + 1)
                pst.done(pool.tensor_copy(parts[:, 0, t, :], h[:, t, :]))
                pst.done(pool.tensor_tensor(parts[:, 1, t, :], h[:, t, :], parts[:, 0, t, :], ALU.subtract))
                for c in range(0, D, D // 4):
                    q = slice(c, c + D // 4)
                    pst.done(pool.tensor_tensor(rest[:], h[:, t, q], parts[:, 0, t, q], ALU.subtract))
                    pst.done(pool.tensor_tensor(parts[:, 2, t, q], rest[:], parts[:, 1, t, q], ALU.subtract))

            pool.wait_ge(stored, 1)
            for t in range(TT):
                for c in range(2):
                    pool.indirect_dma_start(yg[:, c, t, :], None, ydram[:, :],
                                            bass.IndirectOffsetOnAxis(ap=destu[:, c, t:t + 1], axis=0)
                                            ).then_inc(yg_in[t], 16)

            def add_choice0(t):
                pool.wait_ge(fin_a, t)
                pool.wait_ge(fin_h, 1)
                pool.tensor_tensor(h[:, t, :], h[:, t, :], yg[:, 0, t, :], ALU.add).then_inc(fin_s, 1)

            add_choice0(1)
            add_choice0(2)
            for t in range(TT - 1):
                pool.wait_ge(fin_v, t + 1)
                pool.tensor_tensor(h[:, t, :], h[:, t, :], rows[:, 1, :], ALU.add).then_inc(fin_p, 1)
                if t == 0:
                    add_choice0(3)

        @block.scalar
        def _(act):
            st = Steps(act, act_s)
            act.preload_act_table_set(EXP_LN)

            def rsqrt(n, t):
                act.wait_ge(var_ok, n + 1)
                st.done(act.activation(lnt[:, 1, t:t + 1], lnt[:, 0, t:t + 1], ACT.Ln))
                act.activation(lnt[:, 1, t:t + 1], lnt[:, 1, t:t + 1], ACT.Exp, scale=-0.5).then_inc(rstd_ok, 1)

            def split_hi(c, n):
                act.wait_ge(raw_in[c], 16 * n)
                act.activation(high[c], raw[c], ACT.Copy).then_inc(hi_ok[c], 1)

            rsqrt(0, 0)
            rsqrt(1, 1)
            split_hi(FORGET, 1)
            split_hi(Q, 1)
            rsqrt(2, 2)
            split_hi(K, 1)
            rsqrt(3, 3)
            split_hi(V, 1)
            act.wait_ge(inT_in, 32)
            act.wait_ge(xt_ok, 1)
            for k in KORD:
                act.activation(hT_hi[:, k, :], ps[:, k, :], ACT.Identity, bias=inT[:, 1, k:k + 1],
                               scale=inT[:, 0, k:k + 1]).then_inc(hT_h, 1)
            for c in range(2):
                split_hi(G0 + c, 1)
            act.wait_ge(fl_mm, 1)
            act.wait_ge(bf_in, 16)
            st.done(act.activation(fl[:, 0, :], ps[0:NH, 4, :], ACT.Identity, bias=bfor[:, 0:1]))
            st.done(act.activation(fl[:, 1, :], fl[:, 0, :], ACT.Abs))
            st.done(act.activation(fl[:, 1, :], fl[:, 1, :], ACT.Exp, scale=-1.0))
            act.activation(fl[:, 1, :], fl[:, 1, :], ACT.Ln, bias=1.0).then_inc(fl_a, 1)

            def copy_q(n):
                act.wait_ge(q_mm, n)
                for a in range(2):
                    rows_ = slice(64 * a, 64 * a + 64)
                    act.activation(qz[rows_, a, :], ps[rows_, 5, :], ACT.Copy, scale=SCALE).then_inc(q_sb, 1)

            act.wait_ge(qz_zero, 2)
            copy_q(1)

            def copy_vt(n):
                act.wait_ge(v_mm, n)
                act.activation(vT[:], ps[:, 7, :], ACT.Copy).then_inc(vt_sb, 1)

            copy_vt(1)

            def gate_exp(it, c):
                act.wait_ge(g_mm, 2 * it + c + 1)
                act.activation(gexp[:, c, :], ps[:, 5 + c, :], ACT.Exp, scale=-1.0).then_inc(g_exp, 1)

            def gate_ln(own, it):
                act.wait_ge(g_exp, 2 * it + 2)
                return own.mark(act.activation(gexp[:], gexp[:], ACT.Ln, bias=1.0))

            def gate_sigmoid(it):
                act.activation(sg[:, bass.ds(2 * it, 2), :], gexp[:], ACT.Exp, scale=-1.0).then_inc(g_ok, 1)

            OWN = {True: 1, False: 8 + 1}

            def attend(j, it, fox, last):
                own = Steps(act, act_s, st.n + OWN[fox] * j)
                if not last:
                    split_hi(V, it + 2)
                for u in range(TT):
                    i = TT - 1 - u
                    W = P * (i + 1)
                    if fox:
                        for a in range(2):
                            act.wait_ge(f_negm, j * 8 + 2 * u + a + 1)
                            if u > 0:
                                act.wait_ge(pt_mm, 8 * it + 2 * u + a - 1)
                            act.activation(wc[:, a, 0:W], wa[:, a, 0:W], ACT.Exp, bias=mx[:, 1, 2 * u + a:2 * u + a + 1],
                                           accum_out=rs[:, 0, 2 * u + a:2 * u + a + 1]).then_inc(f_exp, 1)
                    else:
                        for a in range(2):
                            act.wait_ge(s_z, 8 * j + 2 * u + a + 1)
                            act.activation(wa[:, a, 0:W], wb[:, a, 0:W], ACT.Abs).then_inc(s_abs, 1)
                        marks = []
                        for a in range(2):
                            act.wait_ge(s_abs, j * 8 + 2 * u + a + 1)
                            marks.append(own.mark(act.activation(wa[:, a, 0:W], wa[:, a, 0:W], ACT.Exp, scale=-1.0)))
                        for a in range(2):
                            own.wait(marks[a])
                            act.activation(wa[:, a, 0:W], wa[:, a, 0:W], ACT.Ln, bias=1.0).then_inc(s_ln, 1)
                        for a in range(2):
                            act.wait_ge(s_um, j * 8 + 2 * u + a + 1)
                            if u > 0:
                                act.wait_ge(pt_mm, 8 * it + 2 * u + a - 1)
                            act.activation(wc[:, a, 0:W], wb[:, a, 0:W], ACT.Exp).then_inc(s_prob, 1)
                    if u < 2:
                        gate_exp(it, u)
                    if u == 2:
                        logs = gate_ln(own, it)
                        if not last:
                            copy_vt(it + 2)
                    if u == 3:
                        own.wait(logs)
                        gate_sigmoid(it)
                    if u == 3 and not last:
                        act.wait_ge(score, 8 * it + 8)
                        copy_q(it + 2)
                    act.wait_ge(pt_mm, 8 * it + 2 * u + 1)
                    if u > 0:
                        act.wait_ge(pv_mm, 4 * it + u)
                    act.activation(probT[:, 0, 0:W], ps[:, 2, 0:W], ACT.Copy).then_inc(pt_a, 1)
                    if not last:
                        split_hi((Q, K, G0, G0 + 1)[u], it + 2)
                    else:
                        act.wait_ge(wups_in, 16)
                        act.wait_ge(g_mm, 2 * (LAST + 1))
                        act.activation(wus_hi[:, u, :], wups[:, u, :], ACT.Copy).then_inc(ups_hi, 1)
                if last:
                    act.wait_ge(upf_mm, KT)
                    act.wait_ge(y_sb, LAST)
                    for e in range(PAIRS - 1):
                        act.activation(ys_hi[:, e, :], yT[:, PAIRS + e, :], ACT.Copy).then_inc(ysb_hi, 1)
                act.wait_ge(pv_mm, 4 * it + 4)
                act.activation(yT[:, bass.ds(it, 1), :], ps[:, 4:5, :], ACT.Copy).then_inc(y_sb, 1)
                assert own.n == OWN[fox]

            act.wait_ge(rows_used, 1)
            with act.Fori(0, PAIRS) as j:
                attend(j, j, True, False)
            st.n += OWN[True] * PAIRS
            with act.Fori(0, PAIRS - 1) as j:
                attend(j, j + PAIRS, False, False)
            attend(PAIRS - 1, LAST, False, True)
            st.n += OWN[False] * PAIRS

            act.wait_ge(y_sb, LAST + 1)
            act.activation(ys_hi[:, PAIRS - 1, :], yT[:, LAST, :], ACT.Copy).then_inc(ysb_hi, 1)
            act.wait_ge(wout_in, 16)
            for k in range(KT):
                act.activation(wo_hi[:, k, :], wout[:, k, :], ACT.Copy).then_inc(wo_h, 1)
                act.wait_ge(mg_f, k + 1)
                act.activation(mg_hi[:, k, :], sg[:, k, :], ACT.Copy).then_inc(mg_h, 1)

            def h1t_copy(t):
                act.wait_ge(h1t_mm, 2 * t + 1)
                if t > 0:
                    act.wait_ge(r_mm, t)
                act.activation(h1T[:, 0:4, :], ps[:, 4, :].rearrange("p (k c) -> p k c", c=P), ACT.Copy
                               ).then_inc(h1t_a, 1)

            for t in range(TT):
                rsqrt(TT + t, t)
                if t > 0:
                    h1t_copy(t - 1)
            h1t_copy(TT - 1)
            act.wait_ge(gx, 1)
            act.activation(gt[:, 1, :, :], gt[:, 0, :, :], ACT.Exp).then_inc(gx_a, 1)
            act.wait_ge(gx, 2)
            act.activation(r4[:, 5, :], r4[:, 4, :], ACT.Exp).then_inc(gx_a, 1)

            def xg_copy(n):
                act.wait_ge(ga_mm, n)
                for b in range(0, 4, 2):
                    act.activation(xg[:, 2 * b:2 * b + 2, :], ps[:, b, :].rearrange("p (k c) -> p k c", k=2),
                                   ACT.Copy).then_inc(xg_a, 1)

            xg_copy(1)
            act.wait_ge(ctl_ok, 1)
            groups = act.value_load(ctl[0:1, 0:1], min_val=MAIN, max_val=MAIN + MAXOV // QB)
            with act.Fori(0, groups) as g:
                for q in range(QB):
                    n = QB * g + q
                    act.wait_ge(h1_mm, n + 1)
                    act.activation(silu[:], ps[:, 4, 0:2 * P], ACT.Silu).then_inc(si_ok, 1)
                    if q == QB - 1:
                        xg_copy(g + 2)
                    act.wait_ge(ye_mm, n + 1)
                    act.wait_ge(y_out[q % 2], 64 * g + 32 * (q // 2) + 16)
                    act.activation(ysb[:, q % 2, :], ps[:, 7, :], ACT.Copy).then_inc(ye_sb, 1)
                    act.wait_ge(ye_sb, n + 1)
                    for half in range(2):
                        dst = ydram[bass.ds(QB * CAP * g + q * CAP, CAP), half * S:(half + 1) * S]
                        act.dma_start(dst, ysb[64 * half:64 * half + 64, q % 2, :]).then_inc(y_out[q % 2], 16)

            act.preload_act_table_set(EXP_LN)
            def scale_choice0(t):
                act.wait_ge(yg_in[t], 32)
                act.activation(yg[:, 0, t, :], yg[:, 0, t, :], ACT.Copy, scale=gate[:, 0, t:t + 1]).then_inc(fin_a, 1)

            def normalise(t):
                rsqrt(2 * TT + t, t)
                act.wait_ge(fin_r, t + 1)
                act.activation(h[:, t, :], h[:, t, :], ACT.Identity, bias=lnt[:, 3, t:t + 1],
                               scale=lnt[:, 1, t:t + 1]).then_inc(fin_n, 1)

            scale_choice0(1)
            normalise(0)
            scale_choice0(2)
            normalise(1)
            scale_choice0(3)
            normalise(2)
            normalise(3)

        @block.vector
        def _(dve):
            st = Steps(dve, dve_s)

            def moments(t, src):
                for c in range(2):
                    a = st.mark(dve.bn_stats(stats[:, t, c, :], src[:, c * S:(c + 1) * S]))
                st.wait(a)
                st.done(dve.bn_aggr(mv[:, t, :], stats[:, t, :, :]))
                dve.tensor_scalar(lnt[:, 0, t:t + 1], mv[:, t, 1:2], EPS, None, ALU.add).then_inc(var_ok, 1)

            def rstd(n, t):
                v, r0, w = lnt[:, 0, t:t + 1], lnt[:, 1, t:t + 1], lnt[:, 2, t:t + 1]
                dve.wait_ge(rstd_ok, n + 1)
                st.done(dve.tensor_tensor(w, r0, r0, ALU.mult))
                st.done(dve.tensor_tensor(w, w, v, ALU.mult))
                st.done(dve.tensor_scalar(w, w, -0.5, 1.5, ALU.mult, ALU.add))
                st.done(dve.tensor_tensor(r0, r0, w, ALU.mult))

            def norm(n, t, src, dst):
                moments(t, src)
                rstd(n, t)
                return dve.tensor_scalar(dst, src, mv[:, t, 0:1], lnt[:, 1, t:t + 1], ALU.subtract, ALU.mult)

            dve.memset(qz[64:128, 0, :], 0.0).then_inc(qz_zero, 1)
            dve.memset(qz[0:64, 1, :], 0.0).then_inc(qz_zero, 1)
            for t in range(TT):
                dve.wait_ge(x_in[t], 16)
                norm(t, t, h[:, t, :], xn[:, t, :]).then_inc(xn_ok, 1)
            dve.wait_ge(inT_in, 32)
            for n, k in enumerate(KORD):
                dve.wait_ge(hT_h, n + 1)
                dve.tensor_scalar(hTf[:, k, :], ps[:, k, :], inT[:, 0, k:k + 1], inT[:, 1, k:k + 1],
                                  ALU.mult, ALU.add).then_inc(hT_t, 1)
                if n % 2:
                    dve.wait_ge(hT_t, n + 1)
                    dve.tensor_tensor(hT_lo[:, k, :], hTf[:, k, :], hT_hi[:, k, :].bitcast(F32),
                                      ALU.subtract).then_inc(hT_v, 1)

            def copy_k(n):
                dve.wait_ge(k_mm, n)
                dve.tensor_copy(kT[:], ps[:, 6, :]).then_inc(k_sb, 1)

            def copy_v(n):
                dve.wait_ge(vt_mm, n)
                dve.tensor_copy(vp[:].rearrange("p t c -> p (t c)"), ps[:, 7, :]).then_inc(v_sb, 1)

            dve.wait_ge(fl_a, 1)
            dve.wait_ge(consts, 9)
            st.done(dve.scalar_tensor_tensor(out=fl[:, 2, :], in0=fl[:, 0, :], scalar=0.0, in1=fl[:, 1, :],
                                             op0=ALU.min, op1=ALU.subtract))
            st.done(dve.tensor_tensor_scan(fl[:, 3, :], fl[:, 2, :], zero[0:NH, :].to_broadcast([NH, S]), 0.0,
                                           ALU.add, ALU.add))
            dve.tensor_scalar(fl[:, 2, :], fl[:, 3, :], -1.0, None, ALU.mult).then_inc(fl_v, 1)
            copy_k(1)
            copy_v(1)
            dve.wait_ge(rows_in[0], 32)
            dve.wait_ge(xn_ok, TT)
            for t in range(TT):
                a = st.mark(dve.tensor_tensor(h[:, t, :], xn[:, t, :], rows[:, 0, :], ALU.mult))
            for t in range(TT):
                st.wait(a - (TT - 1) + t)
                ins = dve.tensor_tensor(h[:, t, :], h[:, t, :], rows[:, 1, :], ALU.add)
                if t < TT - 1:
                    st.mark(ins)
            ins.then_inc(rows_used, 1)
            dve.wait_ge(rows_used, 1)
            dve.wait_ge(f_out, 16)

            OWN = {True: 8 + 8 + 8, False: 32}

            def attend(j, it, fox, last):
                own = Steps(dve, dve_s, st.n + OWN[fox] * j)
                for u in range(TT):
                    i = TT - 1 - u
                    W = P * (i + 1)
                    dg = slice(i * P, i * P + P)
                    if fox:
                        if u == 0:
                            dve.wait_ge(nf_in, 32 * it + 32)
                        for a in range(2):
                            dve.wait_ge(score, 8 * it + 2 * u + a + 1)
                            dve.tensor_tensor(wa[:, a, 0:W], ps[:, a, 0:W], negf[:, a, 0:W],
                                              ALU.add).then_inc(f_read, 1)
                        marks = []
                        for a in range(2):
                            dve.wait_ge(f_read, 8 * j + 2 * u + a + 1)
                            marks.append(own.mark(dve.tensor_tensor(wa[:, a, dg], wa[:, a, dg], cmask[:], ALU.add)))
                        for a in range(2):
                            c = 2 * u + a
                            own.wait(marks[a])
                            marks[a] = own.mark(dve.tensor_reduce(mx[:, 0, c:c + 1], wa[:, a, 0:W], AX.X, ALU.max))
                        for a in range(2):
                            c = 2 * u + a
                            own.wait(marks[a])
                            dve.tensor_scalar(mx[:, 1, c:c + 1], mx[:, 0, c:c + 1], -1.0, None,
                                              ALU.mult).then_inc(f_negm, 1)
                        marks = []
                        for a in range(2):
                            c = 2 * u + a
                            dve.wait_ge(f_exp, 8 * j + c + 1)
                            marks.append(own.mark(dve.reciprocal(rs[:, 1, c:c + 1], rs[:, 0, c:c + 1])))
                        for a in range(2):
                            c = 2 * u + a
                            own.wait(marks[a])
                            dve.tensor_scalar(wc[:, a, 0:W], wc[:, a, 0:W], rs[:, 1, c:c + 1], None,
                                              ALU.mult).then_inc(f_prob, 1)
                    else:
                        for a in range(2):
                            dve.wait_ge(score, 8 * it + 2 * u + a + 1)
                            dve.tensor_copy(wb[:, a, 0:W], ps[:, a, 0:W]).then_inc(s_z, 1)
                        marks = []
                        for a in range(2):
                            dve.wait_ge(s_ln, 8 * j + 2 * u + a + 1)
                            dve.wait_ge(s_z, 8 * j + 2 * u + a + 1)
                            marks.append(own.mark(dve.scalar_tensor_tensor(
                                out=wa[:, a, 0:W], in0=wb[:, a, 0:W], scalar=0.0, in1=wa[:, a, 0:W],
                                op0=ALU.max, op1=ALU.add)))
                        for a in range(2):
                            own.wait(marks[a])
                            marks[a] = own.mark(dve.tensor_tensor(wa[:, a, dg], wa[:, a, dg], keep[:], ALU.mult))
                        for a in range(2):
                            own.wait(marks[a])
                            rev = wa[:, a, 0:W][:, ::-1]
                            marks[a] = own.mark(dve.tensor_tensor_scan(
                                rev, rev, zero[:, :].to_broadcast([P, W]), 0.0, ALU.add, ALU.add))
                        for a in range(2):
                            own.wait(marks[a])
                            marks[a] = own.mark(dve.tensor_tensor(wb[:, a, 0:W], wb[:, a, 0:W], wa[:, a, 0:W],
                                                                  ALU.subtract))
                        for a in range(2):
                            own.wait(marks[a])
                            dve.tensor_tensor(wb[:, a, dg], wb[:, a, dg], smask[:], ALU.add).then_inc(s_um, 1)
                    dve.wait_ge(pt_mm, 8 * it + 2 * u + 2)
                    if u > 0:
                        dve.wait_ge(pv_mm, 4 * it + u)
                    dve.tensor_copy(probT[:, 1, 0:W], ps[:, 3, 0:W]).then_inc(pt_v, 1)
                    if last:
                        dve.wait_ge(g_ok, NFOX)
                        for k in UP_ROWS[u]:
                            dve.wait_ge(upf_mm, k + 1)
                            dve.tensor_tensor(sg[:, k, :], sg[:, k, :], ps[:, UP_BANK[k], :],
                                              ALU.mult).then_inc(upf_rd, 1)
                if not last:
                    dve.wait_ge(score, 8 * it + 8)
                    copy_k(it + 2)
                    dve.wait_ge(pv_mm, 4 * it + 4)
                    copy_v(it + 2)
                assert own.n == OWN[fox], own.n

            with dve.Fori(0, PAIRS) as j:
                attend(j, j, True, False)
            st.n += OWN[True] * PAIRS
            with dve.Fori(0, PAIRS - 1) as j:
                attend(j, j + PAIRS, False, False)
            attend(PAIRS - 1, LAST, False, True)
            st.n += OWN[False] * PAIRS

            for e in range(PAIRS):
                dve.wait_ge(ysb_hi, e + 1)
                dve.tensor_tensor(ys_lo[:, e, :], yT[:, PAIRS + e, :], ys_hi[:, e, :].bitcast(F32),
                                  ALU.subtract).then_inc(ysb_lo, 1)

            def merged_lo(k):
                dve.wait_ge(mg_h, k + 1)
                dve.tensor_tensor(mg_lo[:, k, :], sg[:, k, :], mg_hi[:, k, :].bitcast(F32),
                                  ALU.subtract).then_inc(mg, 1)

            dve.wait_ge(upf_rd, KT)
            dve.wait_ge(g_ok, LAST + 1)
            for k in range(KT):
                dve.wait_ge(up_mm, k + 1)
                st.done(dve.tensor_tensor(sg[:, KT + k, :], sg[:, KT + k, :], ps[:, k % 4, :], ALU.mult))
                dve.tensor_tensor(sg[:, k, :], sg[:, k, :], sg[:, KT + k, :], ALU.add).then_inc(mg_f, 1)
                if k > 0:
                    merged_lo(k - 1)
            merged_lo(KT - 1)

            def h1t_copy(t):
                dve.wait_ge(h1t_mm, 2 * t + 2)
                if t > 0:
                    dve.wait_ge(r_mm, t)
                dve.tensor_copy(h1T[:, 4:8, :], ps[:, 5, :].rearrange("p (k c) -> p k c", c=P)).then_inc(h1t_v, 1)

            def logits(t):
                dve.wait_ge(r_mm, t + 1)
                dve.tensor_tensor(lg[:, t, :], ps[:, 6 + t % 2, 0:NR], rbias[:], ALU.add).then_inc(lg_ok, 1)

            dve.wait_ge(rows_in[1], 32)
            dve.wait_ge(rb_in, 32)
            for t in range(TT):
                for c in range(2):
                    half = h[:, t, c * S:(c + 1) * S]
                    dve.wait_ge(o_mm, 2 * t + c + 1)
                    a = dve.scalar_tensor_tensor(out=half, in0=half, scalar=ALPHA, in1=ps[:, 2 * (t % 2) + c, :],
                                                 op0=ALU.mult, op1=ALU.add).then_inc(o_rd, 1)
                dve.wait_ge(o_rd, 2 * t + 2)
                st.done(norm(TT + t, t, h[:, t, :], h[:, t, :]))
                st.done(dve.tensor_tensor(h[:, t, :], h[:, t, :], rows[:, 0, :], ALU.mult))
                dve.tensor_tensor(h[:, t, :], h[:, t, :], rows[:, 1, :], ALU.add).then_inc(h1_ok, 1)
                if t > 0:
                    h1t_copy(t - 1)
                    if t > 1:
                        logits(t - 2)
            logits(TT - 2)
            h1t_copy(TT - 1)
            logits(TT - 1)
            dve.wait_ge(lg_ok, TT)

            gl = lg[:, :, 0:NG]
            el = lg[:, :, NG:NR]

            def row(n):
                return r4[:, n, :]

            def wide(ap, n):
                return ap.unsqueeze(2).to_broadcast([P, TT, n])

            def first_max(vals, eq, key, top, width, drop):
                d = desc[:, E - width:E].unsqueeze(1).to_broadcast([P, TT, width])
                st.done(dve.tensor_reduce(row(top), vals, AX.X, ALU.max))
                st.done(dve.tensor_tensor(eq, vals, wide(row(top), width), ALU.is_equal))
                st.done(dve.tensor_tensor(eq, eq, d, ALU.mult))
                st.done(dve.tensor_reduce(row(drop), eq, AX.X, ALU.max))
                st.done(dve.tensor_tensor(key, d, wide(row(drop), width), ALU.is_equal))

            ghot = gt[:, 2, :, :]
            first_max(gl, gt[:, 3, :, :], ghot, 0, NG, 1)
            dve.tensor_tensor(gt[:, 0, :, :], gl, wide(row(0), NG), ALU.subtract).then_inc(gx, 1)
            st.done(dve.tensor_scalar(gt[:, 3, :, :], ghot, 1.0, BIG, ALU.subtract, ALU.mult))
            st.done(dve.tensor_tensor(rt[0][:].rearrange("p t (g e) -> p t g e", e=EPG),
                                      el.rearrange("p t (g e) -> p t g e", e=EPG),
                                      gt[:, 3, :, :].unsqueeze(3).to_broadcast([P, TT, NG, EPG]), ALU.add))
            first_max(rt[0][:], rt[1][:], rt[2][:], 2, E, 1)
            st.done(dve.scalar_tensor_tensor(out=rt[0][:], in0=rt[2][:], scalar=-2.0 * BIG, in1=rt[0][:],
                                             op0=ALU.mult, op1=ALU.add))
            first_max(rt[0][:], rt[1][:], rt[3][:], 3, E, 1)
            dve.tensor_tensor(ehot[:], rt[2][:], rt[3][:], ALU.add).then_inc(eh_ok, 1)
            dve.tensor_tensor(row(4), row(3), row(2), ALU.subtract).then_inc(gx, 1)
            dve.wait_ge(gx_a, 1)
            st.done(dve.tensor_reduce(row(6), gt[:, 1, :, :], AX.X, ALU.add))
            dve.wait_ge(gx_a, 2)
            st.done(dve.scalar_tensor_tensor(out=row(7), in0=row(5), scalar=1.0, in1=row(6),
                                             op0=ALU.add, op1=ALU.mult))
            st.done(dve.reciprocal(gate[:, 0, :], row(7)))
            st.done(dve.tensor_tensor(gate[:, 1, :], gate[:, 0, :], row(5), ALU.mult))
            dve.wait_ge(rank_mm, 1)
            cnt = ps[:, 7, 0:E]
            st.done(dve.tensor_copy(ov[:, 0, :], cnt))
            st.done(dve.tensor_tensor(cnt8[:], ov[:, 0, :].unsqueeze(2).to_broadcast([P, E, 8]),
                                      thr[:].unsqueeze(1).to_broadcast([P, E, 8]), ALU.is_gt))
            st.done(dve.tensor_reduce(ov[:, 1, :], cnt8[:], AX.X, ALU.add))
            st.done(dve.tensor_tensor_scan(ov[:, 2, :], ov[:, 1, :], zero[:, :].to_broadcast([P, E]), 0.0,
                                           ALU.add, ALU.add))
            st.done(dve.tensor_tensor(ov[:, 1, :], ov[:, 2, :], ov[:, 1, :], ALU.subtract))
            st.done(dve.tensor_scalar(ov[:, 1, :], ov[:, 1, :], float(CAP), float(CAP * (E - 1)), ALU.mult, ALU.add))
            st.done(dve.scalar_tensor_tensor(out=ov[:, 3, :], in0=io[:, 0:E], scalar=float(CAP), in1=ov[:, 1, :],
                                             op0=ALU.mult, op1=ALU.subtract))
            rank = ps[:, 7, P:P + TT * E].rearrange("p (t e) -> p t e", e=E)

            def tiles(ap):
                return ap.unsqueeze(1).to_broadcast([P, TT, E])

            st.done(dve.tensor_copy(rt[4][:], rank))
            st.done(dve.tensor_scalar(rt[5][:], rt[4][:], float(CAP), None, ALU.is_lt))
            st.done(dve.tensor_tensor(rt[5][:], rt[5][:], tiles(ov[:, 3, :]), ALU.mult))
            st.done(dve.tensor_tensor(rt[5][:], rt[5][:], tiles(ov[:, 1, :]), ALU.add))
            st.done(dve.tensor_tensor(rt[4][:], rt[4][:], rt[5][:], ALU.add))
            for c in range(2):
                st.done(dve.tensor_tensor(rt[5 + c][:], rt[4][:], rt[2 + c][:], ALU.mult))
                st.done(dve.tensor_reduce(dest[:, c, :], rt[5 + c][:], AX.X, ALU.add))
            st.done(dve.tensor_copy(dsh[:], dest[:]))

            def one_hot(own, n):
                marks = []
                for t in range(TT):
                    marks.append(own.mark(dve.tensor_scalar(oh[:, t, :], io[:], dsh[:, 0, t:t + 1], None, ALU.is_equal)))
                for t in range(TT):
                    own.wait(marks[t])
                    ins = dve.scalar_tensor_tensor(out=oh[:, t, :], in0=io[:], scalar=dsh[:, 1, t:t + 1],
                                                   in1=oh[:, t, :], op0=ALU.is_equal, op1=ALU.add)
                    ins.then_inc(oh_ok, 1)
                dve.wait_ge(oh_ok, n * 4 + 4)
                own.done(dve.tensor_scalar(dsh[:], dsh[:], float(-QB * CAP), None, ALU.add))

            one_hot(st, 0)
            st.done(dve.tensor_tensor(ovc[:], ov[:, 2, :].unsqueeze(1).to_broadcast([P, MAXOV, E]),
                                      io[:, 0:MAXOV].unsqueeze(2).to_broadcast([P, MAXOV, E]), ALU.is_le))
            st.done(dve.tensor_reduce(eb[:, 1:], ovc[:], AX.X, ALU.add))
            st.done(dve.tensor_scalar(eb[:, 1:], eb[:, 1:], float(E - 1), None, ALU.min))
            st.done(dve.tensor_tensor(cnt8[:, 0, 0:4], ov[:, 2, E - 1:E].to_broadcast([P, 4]), gw4[:], ALU.is_gt))
            st.done(dve.tensor_reduce(eb[:, 0:1], cnt8[:, 0, 0:4], AX.X, ALU.add))
            st.done(dve.tensor_scalar(eb[:, 0:1], eb[:, 0:1], float(MAIN), None, ALU.add))
            st.done(dve.tensor_copy(destu[:], dest[:]))
            dve.tensor_copy(ctl[:], eb[:]).then_inc(ctl_ok, 1)
            dve.wait_ge(ctl_ok, 1)

            def xg_copy(n):
                dve.wait_ge(ga_mm, n)
                for b in range(1, 4, 2):
                    dve.tensor_copy(xg[:, 2 * b:2 * b + 2, :], ps[:, b, :].rearrange("p (k c) -> p k c", k=2)
                                    ).then_inc(xg_v, 1)

            xg_copy(1)
            groups = dve.value_load(ctl[0:1, 0:1], min_val=MAIN, max_val=MAIN + MAXOV // QB)
            with dve.Fori(0, groups) as g:
                own = Steps(dve, dve_s, st.n + (TT + 1) * g)
                one_hot(own, g + 1)
                for q in range(QB):
                    n = QB * g + q
                    dve.wait_ge(si_ok, n + 1)
                    dve.wait_ge(h3_mm, n + 1)
                    dve.tensor_tensor(hm[:], silu[:], ps[:, 5, 0:2 * P], ALU.mult).then_inc(hm_ok, 1)
                    dve.wait_ge(ht_mm, n + 1)
                    dve.tensor_copy(hmT[:].rearrange("p j c -> p (j c)"), ps[:, 6, 0:2 * P]).then_inc(ht_ok, 1)
                xg_copy(g + 2)
                assert own.n == TT + 1
            dve.wait_ge(part_s, PART_STEPS * TT)
            st = Steps(dve, fin_d)
            for t in range(TT):
                a = st.mark(dve.tensor_scalar(h[:, t, :], h[:, t, :], ALPHA, None, ALU.mult))
            st.wait(a)
            dve.sem_inc(fin_h, 1)
            dve.wait_ge(rows_in[2], 32)

            def gather_sum(t):
                if t == 0:
                    dve.wait_ge(yg_in[0], 32)
                    st.done(dve.scalar_tensor_tensor(out=h[:, 0, :], in0=yg[:, 0, 0, :], scalar=gate[:, 0, 0:1],
                                                     in1=h[:, 0, :], op0=ALU.mult, op1=ALU.add))
                else:
                    dve.wait_ge(yg_in[t], 32)
                    dve.wait_ge(fin_s, t)
                st.done(dve.scalar_tensor_tensor(out=h[:, t, :], in0=yg[:, 1, t, :], scalar=gate[:, 1, t:t + 1],
                                                 in1=h[:, t, :], op0=ALU.mult, op1=ALU.add))
                moments(t, h[:, t, :])

            def scales(t):
                rstd(2 * TT + t, t)
                dve.scalar_tensor_tensor(out=lnt[:, 3, t:t + 1], in0=mv[:, t, 0:1], scalar=-1.0,
                                         in1=lnt[:, 1, t:t + 1], op0=ALU.mult, op1=ALU.mult).then_inc(fin_r, 1)

            def gain(t):
                dve.wait_ge(fin_n, t + 1)
                return dve.tensor_tensor(h[:, t, :], h[:, t, :], rows[:, 0, :], ALU.mult).then_inc(fin_v, 1)

            for t in range(TT):
                gather_sum(t)
                scales(t)
                if t > 0:
                    gain(t - 1)
            gain(TT - 1)
            dve.wait_ge(fin_v, TT)
            dve.tensor_tensor(h[:, TT - 1, :], h[:, TT - 1, :], rows[:, 1, :], ALU.add).then_inc(fin_l, 1)

        @block.tensor
        def _(pe):
            pe.wait_ge(consts, 1)
            for t in range(TT):
                pe.wait_ge(xn_ok, t + 1)
                for k in range(KT):
                    mm = pe.transpose(ps[:, k, t * P:(t + 1) * P], xn[:, t, k * P:(k + 1) * P], ident[:])
            mm.then_inc(xt_ok, 1)

            def project(c, bank, n, done):
                width = NH if c == FORGET else P
                pe.wait_ge(lo_ok[c], n)
                for m, k in enumerate(KORD):
                    if c == FORGET:
                        pe.wait_ge(hT_h, m + 1)
                        pe.wait_ge((hT_p, hT_v)[m % 2], m // 2 + 1)
                    pe.matmul(ps[0:width, bank, :], low[c][:, k, :], hT_hi[:, k, :], start=(m == 0), stop=False)
                    pe.matmul(ps[0:width, bank, :], high[c][:, k, :], hT_lo[:, k, :], start=False, stop=False)
                    mm = pe.matmul(ps[0:width, bank, :], high[c][:, k, :], hT_hi[:, k, :],
                                   start=False, stop=(m == KT - 1))
                mm.then_inc(done, 1)

            def turn_v(n):
                pe.wait_ge(vt_sb, n)
                for t in range(TT):
                    mm = pe.transpose(ps[:, 7, t * P:(t + 1) * P], vT[:, t * P:(t + 1) * P], ident[:])
                mm.then_inc(vt_mm, 1)

            project(FORGET, 4, 1, fl_mm)
            project(Q, 5, 1, q_mm)
            project(K, 6, 1, k_mm)
            project(V, 7, 1, v_mm)
            turn_v(1)

            def attend(j, it, fox, last):
                read = f_read if fox else s_z

                def scores(u):
                    W = P * (TT - u)
                    i = TT - 1 - u
                    for a in range(2):
                        if u > 0:
                            pe.wait_ge(read, 8 * j + 2 * u + a - 1)
                        pe.matmul(ps[:, a, 0:W], qz[:, a, i * P:(i + 1) * P], kT[:, 0:W],
                                  start=True, stop=True).then_inc(score, 1)

                def turn(u):
                    i = TT - 1 - u
                    for a in range(2):
                        pe.wait_ge(f_prob if fox else s_prob, 8 * j + 2 * u + a + 1)
                        for s in range(i + 1):
                            mm = pe.transpose(ps[:, 2 + a, s * P:(s + 1) * P], wc[:, a, s * P:(s + 1) * P], ident[:])
                        mm.then_inc(pt_mm, 1)

                def values(u):
                    i = TT - 1 - u
                    if u == 0:
                        pe.wait_ge(v_sb, it + 1)
                    pe.wait_ge(pt_a, 4 * it + u + 1)
                    pe.wait_ge(pt_v, 4 * it + u + 1)
                    for s in range(i + 1):
                        for a in range(2):
                            mm = pe.matmul(ps[64 * a:64 * a + 64, 4, i * P:(i + 1) * P], vp[:, s, 64 * a:64 * a + 64],
                                           probT[:, a, s * P:(s + 1) * P], start=(s == 0), stop=(s == i))
                    mm.then_inc(pv_mm, 1)

                def gate_tile(c):
                    if c == 0:
                        pe.wait_ge(q_sb, 2 * it + 2)
                    else:
                        pe.wait_ge(k_sb, it + 1)
                    project(G0 + c, 5 + c, it + 1, g_mm)

                def up_early(k):
                    bank = UP_BANK[k]
                    if k >= 3:
                        pe.wait_ge(upf_rd, k - 2)
                    for e in range(PAIRS):
                        mm = pe.matmul(ps[:, bank, :], wupf[:, e, k * P:(k + 1) * P], yT[:, e, :],
                                       start=(e == 0), stop=(e == PAIRS - 1))
                    mm.then_inc(upf_mm, 1)

                pe.wait_ge(q_sb, 2 * it + 2)
                pe.wait_ge(k_sb, it + 1)
                scores(0)
                gate_tile(0)
                gate_tile(1)
                if last:
                    pe.wait_ge(wupf_in, 16)
                    pe.wait_ge(y_sb, NFOX)
                    pe.wait_ge(v_sb, it + 1)
                    up_early(0)
                scores(1)
                turn(0)
                if not last:
                    pe.wait_ge(v_sb, it + 1)
                    project(V, 7, it + 2, v_mm)
                else:
                    pe.wait_ge(g_exp, 2 * it + 1)
                    up_early(1)
                values(0)
                scores(2)
                if last:
                    pe.wait_ge(g_exp, 2 * it + 2)
                    up_early(2)
                turn(1)
                if not last:
                    pe.wait_ge(g_exp, 2 * it + 1)
                    project(Q, 5, it + 2, q_mm)
                else:
                    up_early(3)
                    up_early(4)
                values(1)
                scores(3)
                turn(2)
                if not last:
                    pe.wait_ge(g_exp, 2 * it + 2)
                    project(K, 6, it + 2, k_mm)
                else:
                    for k in UP_ROWS[3]:
                        up_early(k)
                values(2)
                turn(3)
                if not last:
                    turn_v(it + 2)
                values(3)

            with pe.Fori(0, PAIRS) as j:
                attend(j, j, True, False)
            with pe.Fori(0, PAIRS - 1) as j:
                attend(j, j + PAIRS, False, False)
            attend(PAIRS - 1, LAST, False, True)

            def split_product(bank, pairs):
                for n, ((lh, ll), (rh, rl)) in enumerate(pairs):
                    pe.matmul(ps[:, bank, :], ll, rh, start=(n == 0), stop=False)
                    pe.matmul(ps[:, bank, :], lh, rl, start=False, stop=False)
                    mm = pe.matmul(ps[:, bank, :], lh, rh, start=False, stop=(n == len(pairs) - 1))
                return mm

            pe.wait_ge(ups_lo, PAIRS)
            pe.wait_ge(ysb_lo, PAIRS)
            for k in range(KT):
                if k >= 4:
                    pe.wait_ge(mg_f, k - 3)
                cols = slice(k * P, (k + 1) * P)
                split_product(k % 4, [((wus_hi[:, e, cols], wus_lo[:, e, cols]), (ys_hi[:, e, :], ys_lo[:, e, :]))
                                      for e in range(PAIRS)]).then_inc(up_mm, 1)

            def project_out(t):
                rows_ = slice(t * P, (t + 1) * P)
                for c in range(2):
                    cols = slice(c * S, (c + 1) * S)
                    if t >= 2:
                        pe.wait_ge(o_rd, 2 * (t - 2) + c + 1)
                    split_product(2 * (t % 2) + c,
                                  [((mg_hi[:, k, rows_], mg_lo[:, k, rows_]), (wo_hi[:, k, cols], wo_lo[:, k, cols]))
                                   for k in range(KT)]).then_inc(o_mm, 1)

            def turn_h1(t):
                pe.wait_ge(h1_ok, t + 1)
                for c in range(2):
                    if t > 0:
                        pe.wait_ge((h1t_a, h1t_v)[c], t)
                    for k in range(4):
                        mm = pe.transpose(ps[:, 4 + c, k * P:(k + 1) * P], h[:, t, (4 * c + k) * P:(4 * c + k + 1) * P],
                                          ident[:])
                    mm.then_inc(h1t_mm, 1)

            def route(t):
                if t == 0:
                    pe.wait_ge(wr_in, 32)
                if t >= 2:
                    pe.wait_ge(lg_ok, t - 1)
                pe.wait_ge(h1t_a, t + 1)
                pe.wait_ge(h1t_v, t + 1)
                for k in range(KT):
                    mm = pe.matmul(ps[:, 6 + t % 2, 0:P], h1T[:, k, :], wr[:, k, :],
                                   start=(k == 0), stop=(k == KT - 1))
                mm.then_inc(r_mm, 1)

            pe.wait_ge(wo_l, KT)
            pe.wait_ge(mg, KT)
            project_out(0)
            project_out(1)
            turn_h1(0)
            project_out(2)
            route(0)
            turn_h1(1)
            project_out(3)
            route(1)
            turn_h1(2)
            route(2)
            turn_h1(3)
            route(3)

            pe.wait_ge(eh_ok, 1)
            for t in range(TT):
                for s in range(t + 1):
                    pe.matmul(ps[:, 7, P + t * E:P + (t + 1) * E], (tri if s == t else ones)[:], ehot[:, s, :],
                              start=(s == 0), stop=(s == t))
            for s in range(TT):
                mm = pe.matmul(ps[:, 7, 0:E], ones[:], ehot[:, s, :], start=(s == 0), stop=(s == TT - 1))
            mm.then_inc(rank_mm, 1)

            def gather(dk):
                for t in range(TT):
                    for c in range(3):
                        mm = pe.matmul(ps[:, dk // 2, (dk % 2) * 256:(dk % 2) * 256 + 256],
                                       parts[:, c, t, dk * P:(dk + 1) * P], oh[:, t, :],
                                       start=(t == 0 and c == 0), stop=(t == TT - 1 and c == 2))
                return mm

            pe.wait_ge(oh_ok, TT)
            pe.wait_ge(part_s, PART_STEPS * TT)
            for dk in range(KT):
                mm = gather(dk)
            mm.then_inc(ga_mm, 1)

            pe.wait_ge(ctl_ok, 1)
            groups = pe.value_load(ctl[0:1, 0:1], min_val=MAIN, max_val=MAIN + MAXOV // QB)
            with pe.Fori(0, groups) as g:
                for q in range(QB):
                    n = QB * g + q
                    slots = (3 * (q % 2), 3 * (q % 2) + 1)
                    loaded = 32 * g + 16 * (q // 2) + 16
                    if q == 0:
                        pe.wait_ge(xg_a, 2 * g + 2)
                        pe.wait_ge(xg_v, 2 * g + 2)
                    for c, done in ((0, h1_mm), (1, h3_mm)):
                        pe.wait_ge(ring_in[slots[c]], loaded)
                        w = ring[slots[c]]
                        for k in range(KT):
                            for half in range(2):
                                mm = pe.matmul(ps[64 * half:64 * half + 64, 4 + c, 0:256],
                                               xg[:, k, q * CAP:(q + 1) * CAP],
                                               w[:, k * FE + half * 256:k * FE + half * 256 + 256],
                                               start=(k == 0), stop=(k == KT - 1))
                        mm.then_inc(done, 1)
                    if q == 0:
                        pe.wait_ge(oh_ok, TT * g + 2 * TT)
                    gather(2 * q)
                    pe.wait_ge(hm_ok, n + 1)
                    for c in range(2):
                        mm = pe.transpose(ps[:, 6, c * P:(c + 1) * P], hm[:, c * P:(c + 1) * P], ident[:])
                    mm.then_inc(ht_mm, 1)
                    mm = gather(2 * q + 1)
                    if q == QB - 1:
                        mm.then_inc(ga_mm, 1)
                    pe.wait_ge(ht_ok, n + 1)
                    pe.wait_ge(w2_in[q], 16 * g + 16)
                    w = w2buf[q]
                    for k in range(FT):
                        for half in range(2):
                            mm = pe.matmul(ps[64 * half:64 * half + 64, 7, :],
                                           hmT[:, k % 2, 64 * (k // 2):64 * (k // 2) + 64],
                                           w[:, k * D + half * S:k * D + half * S + S],
                                           start=(k == 0), stop=(k == FT - 1))
                    mm.then_inc(ye_mm, 1)


_INS = ['x', 'ln_in_g', 'ln_in_b', 'w_in', 'b_forget', 'w_up_fox', 'w_up_sb', 'w_out', 'ln1_g', 'ln1_b',
        'w_group', 'b_group', 'w_expert_router', 'b_expert_router', 'w1', 'w3', 'w2', 'ln2_g', 'ln2_b']


def kernel(**inputs):
    import numpy as _np
    import concourse.bacc as _bacc
    from concourse import mybir as _mybir
    from concourse.bass_utils import run_bass_kernel_spmd as _run

    nc = _bacc.Bacc("TRN2", target_bir_lowering=False, num_devices=1)
    arrays, args = {}, []
    for name in _INS:
        a = _np.ascontiguousarray(inputs[name])
        arrays[f"in_{name}_dram"] = a
        args.append(nc.dram_tensor(f"in_{name}_dram", a.shape, _mybir.dt.from_np(a.dtype), kind="ExternalInput").ap())
    args.append(nc.dram_tensor("out_0_dram", (1, S, D), F32, kind="ExternalOutput").ap())
    build(nc, *args)
    res = _run(nc, [arrays], core_ids=[0])
    return res.results[0]["out_0_dram"]
```

```python
from contextlib import ExitStack

import concourse.bass as bass
from concourse import mybir

ALU = mybir.AluOpType
ACT = mybir.ActivationFunctionType
AX = mybir.AxisListType
F32 = mybir.dt.float32
F32R = mybir.dt.float32r
BF16 = mybir.dt.bfloat16
I32 = mybir.dt.int32
U32 = mybir.dt.uint32

P = 128
D = 1024
S = 512
KT = D // P
TT = S // P
HD = 64
NH = 8
PAIRS = NH * HD // P
DH = NH * HD
SCALE = HD ** -0.5
GATE0 = 6 * DH + NH
SB_SHIFT = 3 * DH + NH
E = 32
NG = 4
EPG = E // NG
FE = 512
FT = FE // P
CAP = 64
QB = 4
MAIN = E // QB
MAXOV = 16
SLOTS = (E + MAXOV) * CAP
NR = NG + E
ALPHA = 2.0 ** 0.25
EPS = 1e-5
BIG = 1e30
UP_ROWS = [[0], [1, 2], [3, 4], [5, 6, 7]]
UP_BANK = [7, 5, 6, 7, 5, 6, 7, 5]
CUTS = (32, 48)
PIECE = 16
PART_STEPS = 10
KORD = [4, 5, 6, 7, 0, 1, 2, 3]
EXP_LN = "natural_log_exp_and_others"
FIRST_COLS = [slice(CAP, 2 * CAP), slice(2 * CAP, QB * CAP)]
assert E * PIECE == S
RING = 6
UNIT = 4096


class Steps:

    def __init__(self, eng, sem, base=0):
        self.eng, self.sem, self.base, self.n = eng, sem, base, 0

    def mark(self, ins):
        self.n += 1
        ins.then_inc(self.sem, 1)
        return self.base + self.n

    def wait(self, value):
        self.eng.wait_ge(self.sem, value)

    def done(self, ins):
        self.wait(self.mark(ins))


def build(nc, x, ln_in_g, ln_in_b, w_in, b_forget, w_up_fox, w_up_sb, w_out, ln1_g, ln1_b,
          w_group, b_group, w_expert_router, b_expert_router, w1, w3, w2, ln2_g, ln2_b, out):
    ctx = ExitStack()
    with ctx:
        base = (nc.sbuf_base + 63) // 64 * 64

        def at(name, offset, shape, dt=F32):
            return nc.alloc_sbuf_tensor_at(name, [shape[0]] + list(shape[1:]), dt, offset=offset)

        KB = 1024
        r = [base + 16 * KB * n for n in range(RING)]
        ring = [at(f"ring{n}", r[n], [P, UNIT]) for n in range(RING)]
        g_hi = at("g_hi", r[0], [P, 2, KT, P], F32R)
        g_lo = at("g_lo", r[0] + 8 * KB, [P, 2, KT, P], F32R)
        g_raw = at("g_raw", r[0] + 8 * KB, [P, 2, KT, P])
        w_hi = at("w_hi", r[1], [P, 3, KT, P], F32R)
        probT = at("probT", r[1] + 12 * KB, [P, 2, S])
        wa = at("wa", r[2], [P, 2, S])
        wb = at("wb", r[2] + 4 * KB, [P, 2, S])
        wc = at("wc", r[2] + 8 * KB, [P, 2, S])
        negf = at("negf", r[2] + 12 * KB, [P, 2, S])
        qz = at("qz", r[3], [P, 2, S])
        kT = at("kT", r[3] + 4 * KB, [P, S])
        vp = at("vp", r[3] + 6 * KB, [P, TT, P])
        vT = at("vT", r[3] + 8 * KB, [P, S])
        gexp = at("gexp", r[3] + 12 * KB, [P, 2, S])
        wupf = at("wupf", r[4], [P, PAIRS, D])
        w_lo = at("w_lo", r[5], [P, 3, KT, P], F32R)
        w_raw = at("w_raw", r[5], [P, 3, KT, P])
        wups = at("wups", r[5], [P, PAIRS, D])
        wus_lo = at("wus_lo", r[5], [P, PAIRS, D], F32R)
        wus_hi = at("wus_hi", r[0], [P, PAIRS, D], F32R)
        wo_hi = at("wo_hi", r[1], [P, KT, D], F32R)
        mg_hi = at("mg_hi", r[3], [P, KT, S], F32R)
        b0 = base + 16 * KB * RING
        h = at("h", b0, [P, TT, D])
        b1 = b0 + 16 * KB
        hTf = at("hTf", b1 + 16 * KB, [P, KT, S])
        sg = at("sg", b1, [P, 2 * KT, S])
        mg_lo = at("mg_lo", b1, [P, KT, S], F32R)
        xn = at("xn", b1, [P, TT, D])
        parts = at("parts", b1 + 16 * KB, [P, 3, TT, D], BF16)
        b2 = b1 + 32 * KB
        yT = at("yT", b2, [P, 2 * PAIRS, S])
        ys_hi = at("ys_hi", b2, [P, PAIRS, S], F32R)
        ys_lo = at("ys_lo", b2 + 8 * KB, [P, PAIRS, S], F32R)
        wr = at("wr", b2 + 8 * KB, [P, KT, P])
        h1T = at("h1T", b2 + 12 * KB, [P, KT, P])
        b3 = b2 + 16 * KB
        hT_hi = at("hT_hi", b3, [P, KT, S], F32R)
        hT_lo = at("hT_lo", b3 + 16 * KB, [P, KT, S], F32R)
        wo_lo = at("wo_lo", b3, [P, KT, D], F32R)
        wout = at("wout", b3, [P, KT, D])
        w2buf = [ring[2], ring[5], at("w2_2", b1, [P, UNIT]), at("w2_3", b2 + 8 * KB, [P, UNIT])]
        xg = at("xg", b3 + 8 * KB, [P, KT, QB * CAP])
        oh = at("oh", b3 + 16 * KB, [P, TT, QB * CAP], BF16)
        silu = at("silu", b3 + 18 * KB, [P, 2 * P])
        hm = at("hm", b3 + 19 * KB, [P, 2 * P])
        hmT = at("hmT", b3 + 20 * KB, [P, 2, P])
        ysb = at("ysb", b3 + 22 * KB, [P, 2, S])
        rt = [at(f"rt{n}", b3 + 26 * KB + 512 * n, [P, TT, E]) for n in range(8)]
        ovc = at("ovc", b3 + 30 * KB, [P, MAXOV, E])
        cnt8 = at("cnt8", b3 + 18 * KB, [P, E, 8])
        ehot = at("ehot", b3 + 19 * KB, [P, TT, E], BF16)
        b4 = b3 + 32 * KB
        rows = at("rows", b4, [P, 2, D])
        cur = b4 + 8 * KB
        small = {}

        def sm(name, shape, dt=F32):
            nonlocal cur
            n = 1
            for s in shape[1:]:
                n *= s
            small[name] = at(name, cur, shape, dt)
            cur += (n * (2 if dt == BF16 else 4) + 31) // 32 * 32
            return small[name]

        ident = sm("ident", [P, P])
        cmask = sm("cmask", [P, P])
        keep = sm("keep", [P, P])
        smask = sm("smask", [P, P])
        tri = sm("tri", [P, P], BF16)
        ones = sm("ones", [P, P], BF16)
        io = sm("io", [P, QB * CAP])
        desc = sm("desc", [P, E])
        thr = sm("thr", [P, 8])
        zero = sm("zero", [P, 1])
        inT = sm("inT", [P, 2, KT])
        bfor = sm("bfor", [NH, 1])
        rbias = sm("rbias", [P, NR])
        stats = sm("stats", [P, TT, 2, 6])
        mv = sm("mv", [P, TT, 2])
        lnt = sm("lnt", [P, 4, TT])
        mx = sm("mx", [P, 2, 8])
        rs = sm("rs", [P, 2, 8])
        lg = sm("lg", [P, TT, NR])
        gt = sm("gt", [P, 4, TT, NG])
        r4 = sm("r4", [P, 12, TT])
        gate = sm("gate", [P, 2, TT])
        dest = sm("dest", [P, 2, TT])
        dsh = sm("dsh", [P, 2, TT])
        destu = sm("destu", [P, 2, TT], U32)
        ov = sm("ov", [P, 4, E])
        eb = sm("eb", [P, MAXOV + 2])
        ctl = sm("ctl", [P, MAXOV + 2], I32)
        gw4 = sm("gw4", [P, 4])
        many = sm("many", [P, E + MAXOV], I32)
        rest = sm("rest", [P, D // 4])
        assert cur <= nc.sbuf_usable_end, (cur, nc.sbuf_usable_end)
        f_hi = at("f_hi", r[3] + 10 * KB, [P, KT, NH], F32R)
        f_lo = at("f_lo", r[3] + 11 * KB, [P, KT, NH], F32R)
        f_raw = at("f_raw", r[3] + 11 * KB, [P, KT, NH])
        fl = at("fl", r[2], [NH, 4, S])
        ioi = at("ioi", cur - QB * CAP * 4, [P, QB * CAP], I32)
        dg = at("dg", b3 + 8 * KB, [P, 1 + 2 * TT, P])
        yg = at("yg", r[0], [P, 2, TT, D])

        ps = ctx.enter_context(nc.psum_tensor("ps", [P, 8, S], F32))
        fdram = nc.dram_tensor("forget_sums", (NH, S), F32, kind="Internal").ap()
        ydram = nc.dram_tensor("y_by_slot", (SLOTS, D), F32, kind="Internal").ap()

        def sem(name):
            return ctx.enter_context(nc.semaphore(name))

        x_in = [sem(f"x_in{t}") for t in range(TT)]
        rows_in = [sem(f"rows_in{n}") for n in range(3)]
        inT_in = sem("inT_in")
        rb_in = sem("rb_in")
        bf_in = sem("bf_in")
        NAMES = ("q", "k", "v", "gate0", "gate1", "forget")
        raw_in = [sem(f"raw_{n}") for n in NAMES]
        hi_ok = [sem(f"hi_{n}") for n in NAMES]
        lo_ok = [sem(f"lo_{n}") for n in NAMES]
        wupf_in = sem("wupf_in")
        wups_in = sem("wups_in")
        wout_in = sem("wout_in")
        wr_in = sem("wr_in")
        f_out = sem("f_out")
        nf_in = sem("nf_in")
        ring_in = [sem(f"ring_in{n}") for n in range(RING)]
        w2_in = [sem(f"w2_in{n}") for n in range(QB)]
        y_init = sem("y_init")
        y_out = [sem(f"y_out{n}") for n in range(2)]
        stored = sem("stored")
        yg_in = [[sem(f"yg_in{t}_{c}") for c in range(2)] for t in range(TT)]
        o_out = sem("o_out")

        pool_s = sem("pool_s")
        consts = sem("consts")
        qz_zero = sem("qz_zero")
        dve_s = sem("dve_s")
        act_s = sem("act_s")
        var_ok = sem("var_ok")
        rstd_ok = sem("rstd_ok")
        xn_ok = sem("xn_ok")
        xt_ok = sem("xt_ok")
        hT_h = sem("hT_h")
        hT_t = sem("hT_t")
        hT_p = sem("hT_p")
        hT_v = sem("hT_v")
        fl_mm = sem("fl_mm")
        fl_a = sem("fl_a")
        fl_v = sem("fl_v")
        score = sem("score")
        f_read = sem("f_read")
        f_negm = sem("f_negm")
        f_exp = sem("f_exp")
        f_prob = sem("f_prob")
        s_abs = sem("s_abs")
        s_z = sem("s_z")
        s_ln = sem("s_ln")
        s_um = sem("s_um")
        s_prob = sem("s_prob")
        pt_mm = sem("pt_mm")
        pt_a = sem("pt_a")
        pt_v = sem("pt_v")
        pv_mm = sem("pv_mm")
        y_sb = sem("y_sb")
        g_mm = sem("g_mm")
        g_exp = sem("g_exp")
        g_ok = sem("g_ok")
        q_mm = sem("q_mm")
        k_mm = sem("k_mm")
        v_mm = sem("v_mm")
        q_sb = sem("q_sb")
        k_sb = sem("k_sb")
        v_sb = sem("v_sb")
        vt_sb = sem("vt_sb")
        vt_mm = sem("vt_mm")
        ups_hi = sem("ups_hi")
        ups_lo = sem("ups_lo")
        ysb_hi = sem("ysb_hi")
        ysb_lo = sem("ysb_lo")
        wo_h = sem("wo_h")
        wo_l = sem("wo_l")
        mg_f = sem("mg_f")
        mg_h = sem("mg_h")
        up_mm = sem("up_mm")
        upf_mm = sem("upf_mm")
        upf_rd = sem("upf_rd")
        mg = sem("mg")
        o_mm = sem("o_mm")
        o_rd = sem("o_rd")
        h1_ok = sem("h1_ok")
        h1t_mm = sem("h1t_mm")
        h1t_a = sem("h1t_a")
        r_mm = sem("r_mm")
        lg_ok = sem("lg_ok")
        part_s = sem("part_s")
        wr_ok = sem("wr_ok")
        gx = sem("gx")
        gx_a = sem("gx_a")
        eh_ok = sem("eh_ok")
        rank_mm = sem("rank_mm")
        oh0_ok = sem("oh0_ok")
        oh_ok = sem("oh_ok")
        many_ok = sem("many_ok")
        ctl_ok = sem("ctl_ok")
        ga0_mm = sem("ga0_mm")
        xg0_a = sem("xg0_a")
        xg0_v = sem("xg0_v")
        ga_mm = sem("ga_mm")
        xg_a = sem("xg_a")
        xg_v = sem("xg_v")
        h1_mm = sem("h1_mm")
        h3_mm = sem("h3_mm")
        si_ok = sem("si_ok")
        hm_ok = sem("hm_ok")
        ht_mm = sem("ht_mm")
        ht_ok = sem("ht_ok")
        ye_mm = sem("ye_mm")
        ye_sb = sem("ye_sb")
        dg_ok = sem("dg_ok")
        fin_y = sem("fin_y")
        rows_used = sem("rows_used")
        fin_d = sem("fin_d")
        fin_r = sem("fin_r")
        fin_n = sem("fin_n")
        fin_l = sem("fin_l")
        fin_v = sem("fin_v")
        fin_p = sem("fin_p")

        x_t = x[0].rearrange("(t p) d -> t p d", p=P)
        out_t = out[0].rearrange("(t p) d -> t p d", p=P)
        win = w_in[0].rearrange("(k p) c -> p k c", p=P)
        NFOX = PAIRS
        Q, K, V, G0, FORGET = 0, 1, 2, 3, 5
        high = [w_hi[:, 0], w_hi[:, 1], w_hi[:, 2], g_hi[:, 0], g_hi[:, 1], f_hi[:]]
        low = [w_lo[:, 0], w_lo[:, 1], w_lo[:, 2], g_lo[:, 0], g_lo[:, 1], f_lo[:]]
        raw = [w_raw[:, 0], w_raw[:, 1], w_raw[:, 2], g_raw[:, 0], g_raw[:, 1], f_raw[:]]
        LAST = 2 * PAIRS - 1

        block = ctx.enter_context(nc.Block())

        @block.sync
        def _(sp):
            for t in range(TT):
                sp.dma_start(h[:, t, :], x_t[t]).then_inc(x_in[t], 16)
            sp.dma_start(inT[:, 0, :], ln_in_g.rearrange("(k p) -> p k", p=P),
                             allow_slow_non_contiguous=True).then_inc(inT_in, 16)
            sp.dma_start(inT[:, 1, :], ln_in_b.rearrange("(k p) -> p k", p=P),
                             allow_slow_non_contiguous=True).then_inc(inT_in, 16)
            def load_raw(c, col):
                width = NH if c == FORGET else P
                sp.dma_start(raw[c], win[:, :, bass.ds(col, width)]).then_inc(raw_in[c], 16)

            def load_negf(head):
                for a in range(2):
                    sp.dma_start(negf[:, a, :], fdram[head + a].partition_broadcast(P)).then_inc(nf_in, 16)

            load_raw(FORGET, 3 * DH)
            for c in (Q, K, V):
                load_raw(c, c * DH)
            for c in range(2):
                load_raw(G0 + c, GATE0 + c * P)
            sp.dma_start(rows[:, 0, :], ln_in_g.partition_broadcast(P)).then_inc(rows_in[0], 16)
            sp.dma_start(rows[:, 1, :], ln_in_b.partition_broadcast(P)).then_inc(rows_in[0], 16)
            for c, done in ((Q, q_mm), (K, k_mm), (V, v_mm)):
                sp.wait_ge(done, 1)
                load_raw(c, P + c * DH)
            sp.wait_ge(f_out, 16)
            load_negf(0)
            sp.dma_start(wupf[:], w_up_fox[0].rearrange("(k p) n -> p k n", p=P)).then_inc(wupf_in, 16)
            sp.wait_ge(rows_used, 1)
            sp.dma_start(rows[:, 0, :], ln1_g[0].partition_broadcast(P)).then_inc(rows_in[1], 16)
            sp.dma_start(rows[:, 1, :], ln1_b[0].partition_broadcast(P)).then_inc(rows_in[1], 16)

            def refill(it, qkv, fox):
                for c in range(2):
                    sp.wait_ge(g_mm, 2 * it + 1 + c)
                    load_raw(G0 + c, 2 * P * it + (GATE0 + 2 * P + c * P))
                if qkv is not None:
                    for c, done in ((V, v_mm), (Q, q_mm), (K, k_mm)):
                        sp.wait_ge(done, it + 2)
                        load_raw(c, P * it + (2 * P + qkv + c * DH))
                if fox:
                    sp.wait_ge(f_read, 8 * it + 8)
                    load_negf(2 * it + 2)

            def fill_pieces(cuts):
                for cut in cuts:
                    sp.dma_start(ydram[0:E * CAP, :].rearrange("(e r) d -> e r d", r=CAP)[:, cut:cut + PIECE, :],
                                 x[0].rearrange("(e r) d -> e r d", e=E)).then_inc(y_init, 16)

            with sp.Fori(0, NFOX - 2) as it:
                refill(it, 0, True)
            refill(NFOX - 2, SB_SHIFT - NFOX * P, True)
            for n in range(E * CAP, SLOTS, S):
                sp.dma_start(ydram[n:n + S, :], x[0]).then_inc(y_out[n // S % 2], 16)
            with sp.Fori(NFOX - 1, LAST - 1) as it:
                refill(it, SB_SHIFT - NFOX * P, False)
            fill_pieces(CUTS[1:])
            refill(LAST - 1, None, False)
            fill_pieces(CUTS[:1])
            sp.wait_ge(k_mm, LAST + 1)
            sp.dma_start(wups[:], w_up_sb[0].rearrange("(k p) n -> p k n", p=P)).then_inc(wups_in, 16)
            sp.wait_ge(g_mm, 2 * (LAST + 1))
            sp.dma_start(wout[:], w_out[0].rearrange("(k p) n -> p k n", p=P)).then_inc(wout_in, 16)

            def load_w13(e, half, k):
                slot = 3 * half + k
                src = (w1, w3)[k][0, e].rearrange("(k p) f -> p k f", p=P)
                sp.dma_start(ring[slot][:].rearrange("p (k f) -> p k f", f=FE), src).then_inc(ring_in[slot], 16)

            def load_w2(e, place):
                src = w2[0, e].rearrange("(k p) n -> p k n", p=P)
                sp.dma_start(w2buf[place][:].rearrange("p (k n) -> p k n", n=D), src).then_inc(w2_in[place], 16)

            sp.wait_ge(upf_mm, KT)
            load_w13(1, 1, 1)
            sp.wait_ge(up_mm, KT)
            load_w13(0, 0, 0)
            load_w2(1, 1)
            sp.wait_ge(wr_ok, 1)
            sp.dma_start(wr[:, :, 0:NG], w_group[0].rearrange("(k p) c -> p k c", p=P)).then_inc(wr_in, 16)
            sp.dma_start(wr[:, :, NG:NR], w_expert_router[0].rearrange("(k p) c -> p k c", p=P)).then_inc(wr_in, 16)
            sp.wait_ge(o_mm, 2 * TT)
            load_w13(0, 0, 1)
            load_w2(0, 0)
            load_w13(1, 1, 0)
            load_w2(2, 2)
            sp.wait_ge(h1_ok, TT)
            sp.dma_start(rows[:, 0, :], ln2_g[0].partition_broadcast(P)).then_inc(rows_in[2], 16)
            sp.dma_start(rows[:, 1, :], ln2_b[0].partition_broadcast(P)).then_inc(rows_in[2], 16)
            sp.wait_ge(r_mm, TT)
            load_w2(3, 3)

            def refill_w13(done, e, half):
                for k, used in enumerate((h1_mm, h3_mm)):
                    sp.wait_ge(used, done + 1)
                    load_w13(e, half, k)

            with sp.Fori(0, MAIN - 1) as g:
                for q in range(QB):
                    refill_w13(QB * g + q, QB * g + (q + 2), q % 2)
                    sp.wait_ge(ye_mm, QB * g + q + 1)
                    load_w2(QB * g + (q + QB), q)
            for q in range(QB - 2):
                refill_w13(QB * (MAIN - 1) + q, QB * (MAIN - 1) + q + 2, q % 2)
            sp.wait_ge(ctl_ok, 1)
            groups = sp.value_load(ctl[0:1, 0:1], min_val=MAIN, max_val=MAIN + MAXOV // QB)
            with sp.If(groups > MAIN):
                with sp.Fori(MAIN, groups) as g:
                    for q in range(QB):
                        e = sp.value_load(ctl[0:1, bass.ds(QB * g + (q + 1 - E), 1)], min_val=0, max_val=E - 1)
                        refill_w13(QB * g + (q - 2), e, q % 2)
                        sp.wait_ge(ye_mm, QB * g + (q - QB + 1))
                        load_w2(e, q)
            with sp.Else():
                sp.nop()
            for n in range(2):
                sp.wait_ge(y_out[n], groups * (QB * 48) + 16)
            sp.sem_inc(stored, 1)
            for t in range(TT - 1):
                sp.wait_ge(fin_p, t + 1)
                sp.dma_start(out_t[t], h[:, t, :]).then_inc(o_out, 16)
            for c in range(2):
                sp.wait_ge(fin_l, c + 1)
                half = slice(c * S, (c + 1) * S)
                sp.dma_start(out_t[TT - 1][:, half], h[:, TT - 1, half]).then_inc(o_out, 16)
            sp.wait_ge(o_out, 16 * (TT + 1))

        @block.gpsimd
        def _(pool):
            st = Steps(pool, pool_s)
            pool.dma_start(bfor[:], b_forget[0].rearrange("(h o) -> h o", o=1)).then_inc(bf_in, 16)
            st.mark(pool.memset(ident[:], 0.0))
            st.mark(pool.memset(cmask[:], 0.0))
            st.mark(pool.memset(tri[:], 1.0))
            st.mark(pool.iota(ioi[:], pattern=[[1, QB * CAP]], base=0, channel_multiplier=0))
            st.mark(pool.memset(keep[:], 1.0))
            st.mark(pool.memset(smask[:], 0.0))
            a = st.mark(pool.memset(ones[:], 1.0))
            st.wait(a)
            pool.affine_select(out=ident[:], in_=ident[:], compare_op=ALU.not_equal, fill=1.0, base=0,
                               pattern=[[-1, P]], channel_multiplier=1).then_inc(consts, 1)
            pool.memset(zero[:], 0.0).then_inc(consts, 1)
            pool.affine_select(out=cmask[:], in_=cmask[:], compare_op=ALU.is_ge, fill=-BIG, base=0,
                               pattern=[[-1, P]], channel_multiplier=1).then_inc(consts, 1)
            pool.affine_select(out=keep[:], in_=keep[:], compare_op=ALU.is_gt, fill=0.0, base=0,
                               pattern=[[-1, P]], channel_multiplier=1).then_inc(consts, 1)
            pool.affine_select(out=smask[:], in_=smask[:], compare_op=ALU.is_gt, fill=-BIG, base=0,
                               pattern=[[-1, P]], channel_multiplier=1).then_inc(consts, 1)
            pool.affine_select(out=tri[:], in_=tri[:], compare_op=ALU.is_gt, fill=0.0, base=0,
                               pattern=[[1, P]], channel_multiplier=-1).then_inc(consts, 1)
            b = st.mark(pool.tensor_copy(io[:], ioi[:]))
            st.wait(b)
            pool.tensor_scalar(desc[:], io[:, 0:E], -1.0, float(E), ALU.mult, ALU.add).then_inc(consts, 1)
            pool.tensor_scalar(thr[:], io[:, 0:8], float(CAP), float(CAP), ALU.mult, ALU.add).then_inc(consts, 1)
            pool.tensor_scalar(gw4[:], io[:, 0:4], float(QB), None, ALU.mult).then_inc(consts, 1)
            pool.dma_start(rbias[:, 0:NG], b_group[0].partition_broadcast(P)).then_inc(rb_in, 16)
            pool.dma_start(rbias[:, NG:NR], b_expert_router[0].partition_broadcast(P)).then_inc(rb_in, 16)

            for c in (FORGET, Q, K, V):
                pool.wait_ge(hi_ok[c], 1)
                pool.tensor_tensor(low[c], raw[c], high[c].bitcast(F32),
                                   ALU.subtract).then_inc(lo_ok[c], 1)
            for n in range(0, KT, 2):
                k = KORD[n]
                pool.wait_ge(hT_t, n + 1)
                pool.tensor_tensor(hT_lo[:, k, :], hTf[:, k, :], hT_hi[:, k, :].bitcast(F32),
                                   ALU.subtract).then_inc(hT_p, 1)
            for c in (G0, G0 + 1):
                pool.wait_ge(hi_ok[c], 1)
                pool.tensor_tensor(low[c], raw[c], high[c].bitcast(F32),
                                   ALU.subtract).then_inc(lo_ok[c], 1)
            pool.wait_ge(fl_v, 1)
            pool.dma_start(fdram[:, :], fl[:, 2, :]).then_inc(f_out, 16)

            def split_lo(c, n):
                pool.wait_ge(hi_ok[c], n)
                pool.tensor_tensor(low[c], raw[c], high[c].bitcast(F32),
                                   ALU.subtract).then_inc(lo_ok[c], 1)

            with pool.Fori(0, LAST) as it:
                for c in (V, Q, K, G0, G0 + 1):
                    split_lo(c, it + 2)

            for e in range(PAIRS):
                pool.wait_ge(ups_hi, e + 1)
                pool.tensor_tensor(wus_lo[:, e, :], wups[:, e, :], wus_hi[:, e, :].bitcast(F32),
                                   ALU.subtract).then_inc(ups_lo, 1)
            for k in range(KT):
                pool.wait_ge(wo_h, k + 1)
                pool.tensor_tensor(wo_lo[:, k, :], wout[:, k, :], wo_hi[:, k, :].bitcast(F32),
                                   ALU.subtract).then_inc(wo_l, 1)
            pool.wait_ge(up_mm, KT)
            pool.memset(wr[:], 0.0).then_inc(wr_ok, 1)
            pool.wait_ge(mg, KT)
            pst = Steps(pool, part_s)
            for t in range(TT):
                pool.wait_ge(h1_ok, t + 1)
                pst.done(pool.tensor_copy(parts[:, 0, t, :], h[:, t, :]))
                pst.done(pool.tensor_tensor(parts[:, 1, t, :], h[:, t, :], parts[:, 0, t, :], ALU.subtract))
                for c in range(0, D, D // 4):
                    q = slice(c, c + D // 4)
                    pst.done(pool.tensor_tensor(rest[:], h[:, t, q], parts[:, 0, t, q], ALU.subtract))
                    pst.done(pool.tensor_tensor(parts[:, 2, t, q], rest[:], parts[:, 1, t, q], ALU.subtract))

            pool.wait_ge(stored, 1)
            for t in range(TT):
                for c in range(2):
                    pool.indirect_dma_start(yg[:, c, t, :], None, ydram[:, :],
                                            bass.IndirectOffsetOnAxis(ap=destu[:, c, t:t + 1], axis=0)
                                            ).then_inc(yg_in[t][c], 16)
            for t in range(TT - 1):
                pool.wait_ge(fin_v, t + 1)
                pool.tensor_tensor(h[:, t, :], h[:, t, :], rows[:, 1, :], ALU.add).then_inc(fin_p, 1)

        @block.scalar
        def _(act):
            st = Steps(act, act_s)
            act.preload_act_table_set(EXP_LN)

            def rsqrt(n, t):
                act.wait_ge(var_ok, n + 1)
                st.done(act.activation(lnt[:, 1, t:t + 1], lnt[:, 0, t:t + 1], ACT.Ln))
                act.activation(lnt[:, 1, t:t + 1], lnt[:, 1, t:t + 1], ACT.Exp, scale=-0.5).then_inc(rstd_ok, 1)

            def split_hi(c, n):
                act.wait_ge(raw_in[c], 16 * n)
                act.activation(high[c], raw[c], ACT.Copy).then_inc(hi_ok[c], 1)

            rsqrt(0, 0)
            rsqrt(1, 1)
            split_hi(FORGET, 1)
            split_hi(Q, 1)
            rsqrt(2, 2)
            split_hi(K, 1)
            rsqrt(3, 3)
            split_hi(V, 1)
            act.wait_ge(inT_in, 32)
            act.wait_ge(xt_ok, 1)
            for k in KORD:
                act.activation(hT_hi[:, k, :], ps[:, k, :], ACT.Identity, bias=inT[:, 1, k:k + 1],
                               scale=inT[:, 0, k:k + 1]).then_inc(hT_h, 1)
            for c in range(2):
                split_hi(G0 + c, 1)
            act.wait_ge(fl_mm, 1)
            act.wait_ge(bf_in, 16)
            st.done(act.activation(fl[:, 0, :], ps[0:NH, 4, :], ACT.Identity, bias=bfor[:, 0:1]))
            st.done(act.activation(fl[:, 1, :], fl[:, 0, :], ACT.Abs))
            st.done(act.activation(fl[:, 1, :], fl[:, 1, :], ACT.Exp, scale=-1.0))
            act.activation(fl[:, 1, :], fl[:, 1, :], ACT.Ln, bias=1.0).then_inc(fl_a, 1)

            def copy_q(n):
                act.wait_ge(q_mm, n)
                for a in range(2):
                    rows_ = slice(64 * a, 64 * a + 64)
                    act.activation(qz[rows_, a, :], ps[rows_, 5, :], ACT.Copy, scale=SCALE).then_inc(q_sb, 1)

            act.wait_ge(qz_zero, 2)
            copy_q(1)

            def copy_vt(n):
                act.wait_ge(v_mm, n)
                act.activation(vT[:], ps[:, 7, :], ACT.Copy).then_inc(vt_sb, 1)

            copy_vt(1)

            def gate_exp(it, c):
                act.wait_ge(g_mm, 2 * it + c + 1)
                act.activation(gexp[:, c, :], ps[:, 5 + c, :], ACT.Exp, scale=-1.0).then_inc(g_exp, 1)

            def gate_ln(own, it):
                act.wait_ge(g_exp, 2 * it + 2)
                return own.mark(act.activation(gexp[:], gexp[:], ACT.Ln, bias=1.0))

            def gate_sigmoid(it):
                act.activation(sg[:, bass.ds(2 * it, 2), :], gexp[:], ACT.Exp, scale=-1.0).then_inc(g_ok, 1)

            OWN = {True: 1, False: 8 + 1}

            def attend(j, it, fox, last):
                own = Steps(act, act_s, st.n + OWN[fox] * j)
                if not last:
                    split_hi(V, it + 2)
                for u in range(TT):
                    i = TT - 1 - u
                    W = P * (i + 1)
                    if fox:
                        for a in range(2):
                            act.wait_ge(f_negm, j * 8 + 2 * u + a + 1)
                            if u > 0:
                                act.wait_ge(pt_mm, 8 * it + 2 * u + a - 1)
                            act.activation(wc[:, a, 0:W], wa[:, a, 0:W], ACT.Exp, bias=mx[:, 1, 2 * u + a:2 * u + a + 1],
                                           accum_out=rs[:, 0, 2 * u + a:2 * u + a + 1]).then_inc(f_exp, 1)
                    else:
                        for a in range(2):
                            act.wait_ge(s_z, 8 * j + 2 * u + a + 1)
                            act.activation(wa[:, a, 0:W], wb[:, a, 0:W], ACT.Abs).then_inc(s_abs, 1)
                        marks = []
                        for a in range(2):
                            act.wait_ge(s_abs, j * 8 + 2 * u + a + 1)
                            marks.append(own.mark(act.activation(wa[:, a, 0:W], wa[:, a, 0:W], ACT.Exp, scale=-1.0)))
                        for a in range(2):
                            own.wait(marks[a])
                            act.activation(wa[:, a, 0:W], wa[:, a, 0:W], ACT.Ln, bias=1.0).then_inc(s_ln, 1)
                        for a in range(2):
                            act.wait_ge(s_um, j * 8 + 2 * u + a + 1)
                            if u > 0:
                                act.wait_ge(pt_mm, 8 * it + 2 * u + a - 1)
                            act.activation(wc[:, a, 0:W], wb[:, a, 0:W], ACT.Exp).then_inc(s_prob, 1)
                    if u == 0:
                        gate_exp(it, 0)
                        gate_exp(it, 1)
                    if u == 2:
                        logs = gate_ln(own, it)
                        if not last:
                            copy_vt(it + 2)
                    if u == 3:
                        own.wait(logs)
                        gate_sigmoid(it)
                    if u == 3 and not last:
                        act.wait_ge(score, 8 * it + 8)
                        copy_q(it + 2)
                    act.wait_ge(pt_mm, 8 * it + 2 * u + 1)
                    if u > 0:
                        act.wait_ge(pv_mm, 4 * it + u)
                    act.activation(probT[:, 0, 0:W], ps[:, 2, 0:W], ACT.Copy).then_inc(pt_a, 1)
                    if not last:
                        split_hi((Q, K, G0, G0 + 1)[u], it + 2)
                    else:
                        act.wait_ge(wups_in, 16)
                        act.wait_ge(g_mm, 2 * (LAST + 1))
                        act.activation(wus_hi[:, u, :], wups[:, u, :], ACT.Copy).then_inc(ups_hi, 1)
                if last:
                    act.wait_ge(upf_mm, KT)
                    act.wait_ge(y_sb, LAST)
                    for e in range(PAIRS - 1):
                        act.activation(ys_hi[:, e, :], yT[:, PAIRS + e, :], ACT.Copy).then_inc(ysb_hi, 1)
                act.wait_ge(pv_mm, 4 * it + 4)
                act.activation(yT[:, bass.ds(it, 1), :], ps[:, 4:5, :], ACT.Copy).then_inc(y_sb, 1)
                assert own.n == OWN[fox]

            act.wait_ge(rows_used, 1)
            with act.Fori(0, PAIRS) as j:
                attend(j, j, True, False)
            st.n += OWN[True] * PAIRS
            with act.Fori(0, PAIRS - 1) as j:
                attend(j, j + PAIRS, False, False)
            attend(PAIRS - 1, LAST, False, True)
            st.n += OWN[False] * PAIRS

            act.wait_ge(y_sb, LAST + 1)
            act.activation(ys_hi[:, PAIRS - 1, :], yT[:, LAST, :], ACT.Copy).then_inc(ysb_hi, 1)
            act.wait_ge(wout_in, 16)
            for k in range(KT):
                act.activation(wo_hi[:, k, :], wout[:, k, :], ACT.Copy).then_inc(wo_h, 1)
                act.wait_ge(mg_f, k + 1)
                act.activation(mg_hi[:, k, :], sg[:, k, :], ACT.Copy).then_inc(mg_h, 1)

            def h1t_copy(t):
                if t > 0:
                    act.wait_ge(r_mm, t)
                for c in range(2):
                    act.wait_ge(h1t_mm, 2 * t + c + 1)
                    act.activation(h1T[:, 4 * c:4 * c + 4, :], ps[:, 4 + c, :].rearrange("p (k c) -> p k c", c=P),
                                   ACT.Copy).then_inc(h1t_a, 1)

            for t in range(TT):
                rsqrt(TT + t, t)
                if t > 0:
                    h1t_copy(t - 1)
            h1t_copy(TT - 1)
            act.wait_ge(gx, 1)
            act.activation(gt[:, 1, :, :], gt[:, 0, :, :], ACT.Exp).then_inc(gx_a, 1)
            act.wait_ge(gx, 2)
            act.activation(r4[:, 5, :], r4[:, 4, :], ACT.Exp).then_inc(gx_a, 1)

            def xg_copy(done, n, cols, copied):
                act.wait_ge(done, n)
                for b in range(0, 4, 2):
                    act.activation(xg[:, 2 * b:2 * b + 2, cols],
                                   ps[:, b, :].rearrange("p (k c) -> p k c", k=2)[:, :, cols],
                                   ACT.Copy).then_inc(copied, 1)

            def store(n, q, low, high):
                for half in range(2):
                    dst = ydram[bass.ds(CAP * n + low, high - low), half * S:(half + 1) * S]
                    act.dma_start(dst, ysb[64 * half + low:64 * half + high, q % 2, :]).then_inc(y_out[q % 2], 16)

            def expert_group(g, first, last):
                for q in range(QB):
                    n = QB * g + q
                    act.wait_ge(h1_mm, n + 1)
                    act.activation(silu[:], ps[:, 4, 0:2 * P], ACT.Silu).then_inc(si_ok, 1)
                    if first and q == 0:
                        xg_copy(ga0_mm, 2, FIRST_COLS[0], xg0_a)
                    if first and q == 1:
                        xg_copy(ga_mm, 1, FIRST_COLS[1], xg_a)
                    if q == QB - 1 and not last:
                        xg_copy(ga_mm, g + 2, slice(0, QB * CAP), xg_a)
                    act.wait_ge(ye_mm, n + 1)
                    act.wait_ge(y_out[q % 2], 192 * g + 96 * (q // 2) + 16)
                    act.activation(ysb[:, q % 2, :], ps[:, 7, :], ACT.Copy).then_inc(ye_sb, 1)
                    act.wait_ge(ye_sb, n + 1)
                    store(n, q, 0, CUTS[0])
                    tokens = act.value_load(many[0:1, bass.ds(n, 1)], min_val=0, max_val=S)
                    for cut in CUTS:
                        with act.If(tokens > cut):
                            store(n, q, cut, cut + PIECE)
                        with act.Else():
                            act.sem_inc(y_out[q % 2], 32)

            xg_copy(ga0_mm, 1, slice(0, CAP), xg0_a)
            act.wait_ge(many_ok, 2)
            act.wait_ge(y_init, 16 * len(CUTS))
            expert_group(0, True, False)
            act.wait_ge(ctl_ok, 1)
            final = act.value_load(ctl[0:1, MAXOV + 1:MAXOV + 2], min_val=MAIN - 1, max_val=MAIN - 1 + MAXOV // QB)
            with act.Fori(1, final) as g:
                expert_group(g, False, False)
            expert_group(final, False, True)

            act.preload_act_table_set(EXP_LN)
            for t in range(TT):
                rsqrt(2 * TT + t, t)
                act.wait_ge(fin_r, t + 1)
                act.activation(h[:, t, :].rearrange("p (c n) -> p c n", n=S), ps[:, 2 * t:2 * t + 2, :], ACT.Identity,
                               bias=lnt[:, 3, t:t + 1], scale=lnt[:, 1, t:t + 1]).then_inc(fin_n, 1)

        @block.vector
        def _(dve):
            st = Steps(dve, dve_s)

            def moments(t, halves):
                for c in range(2):
                    a = st.mark(dve.bn_stats(stats[:, t, c, :], halves(c)))
                st.wait(a)
                st.done(dve.bn_aggr(mv[:, t, :], stats[:, t, :, :]))
                dve.tensor_scalar(lnt[:, 0, t:t + 1], mv[:, t, 1:2], EPS, None, ALU.add).then_inc(var_ok, 1)

            def rstd(n, t):
                v, r0, w = lnt[:, 0, t:t + 1], lnt[:, 1, t:t + 1], lnt[:, 2, t:t + 1]
                dve.wait_ge(rstd_ok, n + 1)
                st.done(dve.tensor_tensor(w, r0, r0, ALU.mult))
                st.done(dve.tensor_tensor(w, w, v, ALU.mult))
                st.done(dve.tensor_scalar(w, w, -0.5, 1.5, ALU.mult, ALU.add))
                st.done(dve.tensor_tensor(r0, r0, w, ALU.mult))

            def normalise(t, src, dst):
                return dve.tensor_scalar(dst, src, mv[:, t, 0:1], lnt[:, 1, t:t + 1], ALU.subtract, ALU.mult)

            dve.memset(qz[64:128, 0, :], 0.0).then_inc(qz_zero, 1)
            dve.memset(qz[0:64, 1, :], 0.0).then_inc(qz_zero, 1)
            for t in range(TT):
                dve.wait_ge(x_in[t], 16)
                moments(t, lambda c: h[:, t, c * S:(c + 1) * S])
                if t > 0:
                    rstd(t - 1, t - 1)
                    normalise(t - 1, h[:, t - 1, :], xn[:, t - 1, :]).then_inc(xn_ok, 1)
            rstd(TT - 1, TT - 1)
            normalise(TT - 1, h[:, TT - 1, :], xn[:, TT - 1, :]).then_inc(xn_ok, 1)
            dve.wait_ge(inT_in, 32)
            for n, k in enumerate(KORD):
                dve.wait_ge(hT_h, n + 1)
                dve.tensor_scalar(hTf[:, k, :], ps[:, k, :], inT[:, 0, k:k + 1], inT[:, 1, k:k + 1],
                                  ALU.mult, ALU.add).then_inc(hT_t, 1)
                if n % 2:
                    dve.wait_ge(hT_t, n + 1)
                    dve.tensor_tensor(hT_lo[:, k, :], hTf[:, k, :], hT_hi[:, k, :].bitcast(F32),
                                      ALU.subtract).then_inc(hT_v, 1)

            def copy_k(n):
                dve.wait_ge(k_mm, n)
                dve.tensor_copy(kT[:], ps[:, 6, :]).then_inc(k_sb, 1)

            def copy_v(n):
                dve.wait_ge(vt_mm, n)
                dve.tensor_copy(vp[:].rearrange("p t c -> p (t c)"), ps[:, 7, :]).then_inc(v_sb, 1)

            dve.wait_ge(fl_a, 1)
            dve.wait_ge(consts, 9)
            st.done(dve.scalar_tensor_tensor(out=fl[:, 2, :], in0=fl[:, 0, :], scalar=0.0, in1=fl[:, 1, :],
                                             op0=ALU.min, op1=ALU.subtract))
            st.done(dve.tensor_tensor_scan(fl[:, 3, :], fl[:, 2, :], zero[0:NH, :].to_broadcast([NH, S]), 0.0,
                                           ALU.add, ALU.add))
            dve.tensor_scalar(fl[:, 2, :], fl[:, 3, :], -1.0, None, ALU.mult).then_inc(fl_v, 1)
            copy_k(1)
            copy_v(1)
            dve.wait_ge(rows_in[0], 32)
            dve.wait_ge(xn_ok, TT)
            for t in range(TT):
                a = st.mark(dve.tensor_tensor(h[:, t, :], xn[:, t, :], rows[:, 0, :], ALU.mult))
            for t in range(TT):
                st.wait(a - (TT - 1) + t)
                ins = dve.tensor_tensor(h[:, t, :], h[:, t, :], rows[:, 1, :], ALU.add)
                if t < TT - 1:
                    st.mark(ins)
            ins.then_inc(rows_used, 1)
            dve.wait_ge(rows_used, 1)
            dve.wait_ge(f_out, 16)

            OWN = {True: 8 + 8 + 8, False: 32}

            def attend(j, it, fox, last):
                own = Steps(dve, dve_s, st.n + OWN[fox] * j)
                for u in range(TT):
                    i = TT - 1 - u
                    W = P * (i + 1)
                    dg = slice(i * P, i * P + P)
                    if fox:
                        if u == 0:
                            dve.wait_ge(nf_in, 32 * it + 32)
                        for a in range(2):
                            dve.wait_ge(score, 8 * it + 2 * u + a + 1)
                            dve.tensor_tensor(wa[:, a, 0:W], ps[:, a, 0:W], negf[:, a, 0:W],
                                              ALU.add).then_inc(f_read, 1)
                        marks = []
                        for a in range(2):
                            dve.wait_ge(f_read, 8 * j + 2 * u + a + 1)
                            marks.append(own.mark(dve.tensor_tensor(wa[:, a, dg], wa[:, a, dg], cmask[:], ALU.add)))
                        for a in range(2):
                            c = 2 * u + a
                            own.wait(marks[a])
                            marks[a] = own.mark(dve.tensor_reduce(mx[:, 0, c:c + 1], wa[:, a, 0:W], AX.X, ALU.max))
                        for a in range(2):
                            c = 2 * u + a
                            own.wait(marks[a])
                            dve.tensor_scalar(mx[:, 1, c:c + 1], mx[:, 0, c:c + 1], -1.0, None,
                                              ALU.mult).then_inc(f_negm, 1)
                        marks = []
                        for a in range(2):
                            c = 2 * u + a
                            dve.wait_ge(f_exp, 8 * j + c + 1)
                            marks.append(own.mark(dve.reciprocal(rs[:, 1, c:c + 1], rs[:, 0, c:c + 1])))
                        for a in range(2):
                            c = 2 * u + a
                            own.wait(marks[a])
                            dve.tensor_scalar(wc[:, a, 0:W], wc[:, a, 0:W], rs[:, 1, c:c + 1], None,
                                              ALU.mult).then_inc(f_prob, 1)
                    else:
                        for a in range(2):
                            dve.wait_ge(score, 8 * it + 2 * u + a + 1)
                            dve.tensor_copy(wb[:, a, 0:W], ps[:, a, 0:W]).then_inc(s_z, 1)
                        marks = []
                        for a in range(2):
                            dve.wait_ge(s_ln, 8 * j + 2 * u + a + 1)
                            dve.wait_ge(s_z, 8 * j + 2 * u + a + 1)
                            marks.append(own.mark(dve.scalar_tensor_tensor(
                                out=wa[:, a, 0:W], in0=wb[:, a, 0:W], scalar=0.0, in1=wa[:, a, 0:W],
                                op0=ALU.max, op1=ALU.add)))
                        for a in range(2):
                            own.wait(marks[a])
                            marks[a] = own.mark(dve.tensor_tensor(wa[:, a, dg], wa[:, a, dg], keep[:], ALU.mult))
                        for a in range(2):
                            own.wait(marks[a])
                            rev = wa[:, a, 0:W][:, ::-1]
                            marks[a] = own.mark(dve.tensor_tensor_scan(
                                rev, rev, zero[:, :].to_broadcast([P, W]), 0.0, ALU.add, ALU.add))
                        for a in range(2):
                            own.wait(marks[a])
                            marks[a] = own.mark(dve.tensor_tensor(wb[:, a, 0:W], wb[:, a, 0:W], wa[:, a, 0:W],
                                                                  ALU.subtract))
                        for a in range(2):
                            own.wait(marks[a])
                            dve.tensor_tensor(wb[:, a, dg], wb[:, a, dg], smask[:], ALU.add).then_inc(s_um, 1)
                    dve.wait_ge(pt_mm, 8 * it + 2 * u + 2)
                    if u > 0:
                        dve.wait_ge(pv_mm, 4 * it + u)
                    dve.tensor_copy(probT[:, 1, 0:W], ps[:, 3, 0:W]).then_inc(pt_v, 1)
                    if last:
                        dve.wait_ge(g_ok, NFOX)
                        for k in UP_ROWS[u]:
                            dve.wait_ge(upf_mm, k + 1)
                            dve.tensor_tensor(sg[:, k, :], sg[:, k, :], ps[:, UP_BANK[k], :],
                                              ALU.mult).then_inc(upf_rd, 1)
                if not last:
                    dve.wait_ge(score, 8 * it + 8)
                    copy_k(it + 2)
                    dve.wait_ge(pv_mm, 4 * it + 4)
                    copy_v(it + 2)
                assert own.n == OWN[fox], own.n

            with dve.Fori(0, PAIRS) as j:
                attend(j, j, True, False)
            st.n += OWN[True] * PAIRS
            with dve.Fori(0, PAIRS - 1) as j:
                attend(j, j + PAIRS, False, False)
            attend(PAIRS - 1, LAST, False, True)
            st.n += OWN[False] * PAIRS

            for e in range(PAIRS):
                dve.wait_ge(ysb_hi, e + 1)
                dve.tensor_tensor(ys_lo[:, e, :], yT[:, PAIRS + e, :], ys_hi[:, e, :].bitcast(F32),
                                  ALU.subtract).then_inc(ysb_lo, 1)

            def merged_lo(k):
                dve.wait_ge(mg_h, k + 1)
                dve.tensor_tensor(mg_lo[:, k, :], sg[:, k, :], mg_hi[:, k, :].bitcast(F32),
                                  ALU.subtract).then_inc(mg, 1)

            dve.wait_ge(upf_rd, KT)
            dve.wait_ge(g_ok, LAST + 1)
            for k in range(KT):
                dve.wait_ge(up_mm, k + 1)
                st.done(dve.tensor_tensor(sg[:, KT + k, :], sg[:, KT + k, :], ps[:, k % 4, :], ALU.mult))
                dve.tensor_tensor(sg[:, k, :], sg[:, k, :], sg[:, KT + k, :], ALU.add).then_inc(mg_f, 1)
                if k > 0:
                    merged_lo(k - 1)
            merged_lo(KT - 1)

            def logits(t):
                dve.wait_ge(r_mm, t + 1)
                dve.tensor_tensor(lg[:, t, :], ps[:, 6 + t % 2, 0:NR], rbias[:], ALU.add).then_inc(lg_ok, 1)

            dve.wait_ge(rows_in[1], 32)
            dve.wait_ge(rb_in, 32)
            for t in range(TT):
                for c in range(2):
                    half = h[:, t, c * S:(c + 1) * S]
                    dve.wait_ge(o_mm, 2 * t + c + 1)
                    a = dve.scalar_tensor_tensor(out=half, in0=half, scalar=ALPHA, in1=ps[:, 2 * (t % 2) + c, :],
                                                 op0=ALU.mult, op1=ALU.add).then_inc(o_rd, 1)
                dve.wait_ge(o_rd, 2 * t + 2)
                moments(t, lambda c: h[:, t, c * S:(c + 1) * S])
                rstd(TT + t, t)
                st.done(normalise(t, h[:, t, :], h[:, t, :]))
                st.done(dve.tensor_tensor(h[:, t, :], h[:, t, :], rows[:, 0, :], ALU.mult))
                dve.tensor_tensor(h[:, t, :], h[:, t, :], rows[:, 1, :], ALU.add).then_inc(h1_ok, 1)
                if t > 1:
                    logits(t - 2)
            logits(TT - 2)
            logits(TT - 1)
            dve.wait_ge(lg_ok, TT)

            gl = lg[:, :, 0:NG]
            el = lg[:, :, NG:NR]

            def row(n):
                return r4[:, n, :]

            def wide(ap, n):
                return ap.unsqueeze(2).to_broadcast([P, TT, n])

            def first_max(vals, eq, key, top, width, drop):
                d = desc[:, E - width:E].unsqueeze(1).to_broadcast([P, TT, width])
                st.done(dve.tensor_reduce(row(top), vals, AX.X, ALU.max))
                st.done(dve.tensor_tensor(eq, vals, wide(row(top), width), ALU.is_equal))
                st.done(dve.tensor_tensor(eq, eq, d, ALU.mult))
                st.done(dve.tensor_reduce(row(drop), eq, AX.X, ALU.max))
                st.done(dve.tensor_tensor(key, d, wide(row(drop), width), ALU.is_equal))

            ghot = gt[:, 2, :, :]
            first_max(gl, gt[:, 3, :, :], ghot, 0, NG, 1)
            dve.tensor_tensor(gt[:, 0, :, :], gl, wide(row(0), NG), ALU.subtract).then_inc(gx, 1)
            st.done(dve.tensor_scalar(gt[:, 3, :, :], ghot, 1.0, BIG, ALU.subtract, ALU.mult))
            st.done(dve.tensor_tensor(rt[0][:].rearrange("p t (g e) -> p t g e", e=EPG),
                                      el.rearrange("p t (g e) -> p t g e", e=EPG),
                                      gt[:, 3, :, :].unsqueeze(3).to_broadcast([P, TT, NG, EPG]), ALU.add))
            first_max(rt[0][:], rt[1][:], rt[2][:], 2, E, 1)
            st.done(dve.scalar_tensor_tensor(out=rt[0][:], in0=rt[2][:], scalar=-2.0 * BIG, in1=rt[0][:],
                                             op0=ALU.mult, op1=ALU.add))
            first_max(rt[0][:], rt[1][:], rt[3][:], 3, E, 1)
            dve.tensor_tensor(ehot[:], rt[2][:], rt[3][:], ALU.add).then_inc(eh_ok, 1)
            dve.tensor_tensor(row(4), row(3), row(2), ALU.subtract).then_inc(gx, 1)
            dve.wait_ge(gx_a, 1)
            st.done(dve.tensor_reduce(row(6), gt[:, 1, :, :], AX.X, ALU.add))
            dve.wait_ge(gx_a, 2)
            st.done(dve.scalar_tensor_tensor(out=row(7), in0=row(5), scalar=1.0, in1=row(6),
                                             op0=ALU.add, op1=ALU.mult))
            st.done(dve.reciprocal(gate[:, 0, :], row(7)))
            st.done(dve.tensor_tensor(gate[:, 1, :], gate[:, 0, :], row(5), ALU.mult))
            dve.wait_ge(rank_mm, 1)
            cnt = ps[:, 7, 0:E]
            st.done(dve.tensor_tensor(cnt8[:], cnt.unsqueeze(2).to_broadcast([P, E, 8]),
                                      thr[:].unsqueeze(1).to_broadcast([P, E, 8]), ALU.is_gt))
            st.done(dve.tensor_reduce(ov[:, 1, :], cnt8[:], AX.X, ALU.add))
            st.done(dve.tensor_tensor_scan(ov[:, 2, :], ov[:, 1, :], zero[:, :].to_broadcast([P, E]), 0.0,
                                           ALU.add, ALU.add))
            st.done(dve.tensor_tensor(ov[:, 1, :], ov[:, 2, :], ov[:, 1, :], ALU.subtract))
            st.done(dve.tensor_scalar(ov[:, 1, :], ov[:, 1, :], float(CAP), float(CAP * (E - 1)), ALU.mult, ALU.add))
            st.done(dve.scalar_tensor_tensor(out=ov[:, 3, :], in0=io[:, 0:E], scalar=float(CAP), in1=ov[:, 1, :],
                                             op0=ALU.mult, op1=ALU.subtract))
            rank = ps[:, 7, P:P + TT * E].rearrange("p (t e) -> p t e", e=E)

            def tiles(ap):
                return ap.unsqueeze(1).to_broadcast([P, TT, E])

            st.mark(dve.tensor_tensor(rt[4][:], rank, tiles(ov[:, 1, :]), ALU.add))
            st.done(dve.scalar_tensor_tensor(out=rt[5][:], in0=rank, scalar=float(CAP), in1=tiles(ov[:, 3, :]),
                                             op0=ALU.is_lt, op1=ALU.mult))
            st.done(dve.tensor_tensor(rt[4][:], rt[4][:], rt[5][:], ALU.add))
            a = [st.mark(dve.tensor_tensor(rt[5 + c][:], rt[4][:], rt[2 + c][:], ALU.mult)) for c in range(2)]
            for c in range(2):
                st.wait(a[c])
                a[c] = st.mark(dve.tensor_reduce(dest[:, c, :], rt[5 + c][:], AX.X, ALU.add))
            st.wait(a[1])

            def one_hot(own, n):
                marks = []
                for t in range(TT):
                    marks.append(first_choice(own, dsh, t, slice(0, QB * CAP)))
                for t in range(TT):
                    own.wait(marks[t])
                    second_choice(dsh, t, slice(0, QB * CAP), oh_ok)
                dve.wait_ge(oh_ok, n * 4 + 4)
                own.done(dve.tensor_scalar(dsh[:], dsh[:], float(-QB * CAP), None, ALU.add))

            def first_choice(own, slot, t, cols):
                return own.mark(dve.tensor_scalar(oh[:, t, cols], io[:, cols], slot[:, 0, t:t + 1], None, ALU.is_equal))

            def second_choice(slot, t, cols, done):
                dve.scalar_tensor_tensor(out=oh[:, t, cols], in0=io[:, cols], scalar=slot[:, 1, t:t + 1],
                                         in1=oh[:, t, cols], op0=ALU.is_equal, op1=ALU.add).then_inc(done, 1)

            for cols, done in ((slice(0, CAP), oh0_ok), (slice(CAP, QB * CAP), oh_ok)):
                marks = [first_choice(st, dest, t, cols) for t in range(TT)]
                for t in range(TT):
                    st.wait(marks[t])
                    second_choice(dest, t, cols, done)
            dve.wait_ge(oh_ok, TT)
            st.done(dve.tensor_scalar(dsh[:], dest[:], float(-QB * CAP), None, ALU.add))
            dve.tensor_copy(many[:, 0:E], cnt).then_inc(many_ok, 1)
            dve.memset(many[:, E:], CAP).then_inc(many_ok, 1)
            st.done(dve.tensor_tensor(ovc[:], ov[:, 2, :].unsqueeze(1).to_broadcast([P, MAXOV, E]),
                                      io[:, 0:MAXOV].unsqueeze(2).to_broadcast([P, MAXOV, E]), ALU.is_le))
            st.done(dve.tensor_reduce(eb[:, 1:MAXOV + 1], ovc[:], AX.X, ALU.add))
            st.done(dve.tensor_scalar(eb[:, 1:MAXOV + 1], eb[:, 1:MAXOV + 1], float(E - 1), None, ALU.min))
            st.done(dve.tensor_tensor(cnt8[:, 0, 0:4], ov[:, 2, E - 1:E].to_broadcast([P, 4]), gw4[:], ALU.is_gt))
            st.done(dve.tensor_reduce(eb[:, 0:1], cnt8[:, 0, 0:4], AX.X, ALU.add))
            st.mark(dve.tensor_scalar(eb[:, MAXOV + 1:], eb[:, 0:1], float(MAIN - 1), None, ALU.add))
            st.done(dve.tensor_scalar(eb[:, 0:1], eb[:, 0:1], float(MAIN), None, ALU.add))
            st.done(dve.tensor_copy(destu[:], dest[:]))
            dve.tensor_copy(ctl[:], eb[:]).then_inc(ctl_ok, 1)
            dve.wait_ge(ctl_ok, 1)

            def xg_copy(done, n, cols, copied):
                dve.wait_ge(done, n)
                for b in range(1, 4, 2):
                    dve.tensor_copy(xg[:, 2 * b:2 * b + 2, cols],
                                    ps[:, b, :].rearrange("p (k c) -> p k c", k=2)[:, :, cols]).then_inc(copied, 1)

            def expert_group(g, first, last):
                own = Steps(dve, dve_s, st.n + (TT + 1) * g)
                for q in range(QB):
                    n = QB * g + q
                    dve.wait_ge(si_ok, n + 1)
                    dve.wait_ge(h3_mm, n + 1)
                    dve.tensor_tensor(hm[:], silu[:], ps[:, 5, 0:2 * P], ALU.mult).then_inc(hm_ok, 1)
                    if first and q == 0:
                        xg_copy(ga0_mm, 2, FIRST_COLS[0], xg0_v)
                    if first and q == 1:
                        xg_copy(ga_mm, 1, FIRST_COLS[1], xg_v)
                    if q == 0 and not (first or last):
                        dve.wait_ge(ga_mm, g + 1)
                        one_hot(own, g + 1)
                    dve.wait_ge(ht_mm, n + 1)
                    dve.tensor_copy(hmT[:].rearrange("p j c -> p (j c)"), ps[:, 6, 0:2 * P]).then_inc(ht_ok, 1)
                    if q == 1 and first:
                        one_hot(own, g + 1)
                if not last:
                    xg_copy(ga_mm, g + 2, slice(0, QB * CAP), xg_v)
                    assert own.n == TT + 1

            xg_copy(ga0_mm, 1, slice(0, CAP), xg0_v)
            expert_group(0, True, False)
            final = dve.value_load(ctl[0:1, MAXOV + 1:MAXOV + 2], min_val=MAIN - 1, max_val=MAIN - 1 + MAXOV // QB)
            with dve.Fori(1, final) as g:
                expert_group(g, False, False)
            expert_group(final, False, True)
            st = Steps(dve, fin_d)
            dve.tensor_scalar(dg[:, 0, :], ident[:], ALPHA, None, ALU.mult).then_inc(dg_ok, 1)
            for t in range(TT):
                for c in range(2):
                    dve.tensor_scalar(dg[:, 1 + 2 * t + c, :], ident[:], gate[:, c, t:t + 1], None,
                                      ALU.mult).then_inc(dg_ok, 1)
            dve.wait_ge(part_s, PART_STEPS * TT)
            dve.wait_ge(rows_in[2], 32)

            def ready(t, c):
                dve.wait_ge(fin_y, 2 * t + c + 1)
                return ps[:, 2 * t + c, :]

            def scales(t):
                rstd(2 * TT + t, t)
                dve.scalar_tensor_tensor(out=lnt[:, 3, t:t + 1], in0=mv[:, t, 0:1], scalar=-1.0,
                                         in1=lnt[:, 1, t:t + 1], op0=ALU.mult, op1=ALU.mult).then_inc(fin_r, 1)

            def gain(t):
                dve.wait_ge(fin_n, t + 1)
                return dve.tensor_tensor(h[:, t, :], h[:, t, :], rows[:, 0, :], ALU.mult).then_inc(fin_v, 1)

            for t in range(TT):
                moments(t, lambda c: ready(t, c))
                scales(t)
                if t > 0:
                    gain(t - 1)
            gain(TT - 1)
            dve.wait_ge(fin_v, TT)
            for c in range(2):
                half = slice(c * S, (c + 1) * S)
                dve.tensor_tensor(h[:, TT - 1, half], h[:, TT - 1, half], rows[:, 1, half], ALU.add).then_inc(fin_l, 1)

        @block.tensor
        def _(pe):
            pe.wait_ge(consts, 1)
            for t in range(TT):
                pe.wait_ge(xn_ok, t + 1)
                for k in range(KT):
                    mm = pe.transpose(ps[:, k, t * P:(t + 1) * P], xn[:, t, k * P:(k + 1) * P], ident[:])
            mm.then_inc(xt_ok, 1)

            def project(c, bank, n, done):
                width = NH if c == FORGET else P
                pe.wait_ge(lo_ok[c], n)
                for m, k in enumerate(KORD):
                    if c == FORGET:
                        pe.wait_ge(hT_h, m + 1)
                        pe.wait_ge((hT_p, hT_v)[m % 2], m // 2 + 1)
                    pe.matmul(ps[0:width, bank, :], low[c][:, k, :], hT_hi[:, k, :], start=(m == 0), stop=False)
                    pe.matmul(ps[0:width, bank, :], high[c][:, k, :], hT_lo[:, k, :], start=False, stop=False)
                    mm = pe.matmul(ps[0:width, bank, :], high[c][:, k, :], hT_hi[:, k, :],
                                   start=False, stop=(m == KT - 1))
                mm.then_inc(done, 1)

            def turn_v(n):
                pe.wait_ge(vt_sb, n)
                for t in range(TT):
                    mm = pe.transpose(ps[:, 7, t * P:(t + 1) * P], vT[:, t * P:(t + 1) * P], ident[:])
                mm.then_inc(vt_mm, 1)

            project(FORGET, 4, 1, fl_mm)
            project(Q, 5, 1, q_mm)
            project(K, 6, 1, k_mm)
            project(V, 7, 1, v_mm)
            turn_v(1)

            def attend(j, it, fox, last):
                read = f_read if fox else s_z

                def scores(u):
                    W = P * (TT - u)
                    i = TT - 1 - u
                    for a in range(2):
                        if u > 0:
                            pe.wait_ge(read, 8 * j + 2 * u + a - 1)
                        pe.matmul(ps[:, a, 0:W], qz[:, a, i * P:(i + 1) * P], kT[:, 0:W],
                                  start=True, stop=True).then_inc(score, 1)

                def turn(u):
                    i = TT - 1 - u
                    for a in range(2):
                        pe.wait_ge(f_prob if fox else s_prob, 8 * j + 2 * u + a + 1)
                        for s in range(i + 1):
                            mm = pe.transpose(ps[:, 2 + a, s * P:(s + 1) * P], wc[:, a, s * P:(s + 1) * P], ident[:])
                        mm.then_inc(pt_mm, 1)

                def values(u):
                    i = TT - 1 - u
                    if u == 0:
                        pe.wait_ge(v_sb, it + 1)
                    pe.wait_ge(pt_a, 4 * it + u + 1)
                    pe.wait_ge(pt_v, 4 * it + u + 1)
                    for s in range(i + 1):
                        for a in range(2):
                            mm = pe.matmul(ps[64 * a:64 * a + 64, 4, i * P:(i + 1) * P], vp[:, s, 64 * a:64 * a + 64],
                                           probT[:, a, s * P:(s + 1) * P], start=(s == 0), stop=(s == i))
                    mm.then_inc(pv_mm, 1)

                def gate_tile(c):
                    if c == 0:
                        pe.wait_ge(q_sb, 2 * it + 2)
                    else:
                        pe.wait_ge(k_sb, it + 1)
                    project(G0 + c, 5 + c, it + 1, g_mm)

                def up_early(k):
                    bank = UP_BANK[k]
                    if k >= 3:
                        pe.wait_ge(upf_rd, k - 2)
                    for e in range(PAIRS):
                        mm = pe.matmul(ps[:, bank, :], wupf[:, e, k * P:(k + 1) * P], yT[:, e, :],
                                       start=(e == 0), stop=(e == PAIRS - 1))
                    mm.then_inc(upf_mm, 1)

                pe.wait_ge(q_sb, 2 * it + 2)
                pe.wait_ge(k_sb, it + 1)
                scores(0)
                gate_tile(0)
                gate_tile(1)
                if last:
                    pe.wait_ge(wupf_in, 16)
                    pe.wait_ge(y_sb, NFOX)
                    pe.wait_ge(v_sb, it + 1)
                    up_early(0)
                scores(1)
                turn(0)
                if not last:
                    pe.wait_ge(v_sb, it + 1)
                    project(V, 7, it + 2, v_mm)
                else:
                    pe.wait_ge(g_exp, 2 * it + 1)
                    up_early(1)
                values(0)
                scores(2)
                if last:
                    pe.wait_ge(g_exp, 2 * it + 2)
                    up_early(2)
                turn(1)
                if not last:
                    pe.wait_ge(g_exp, 2 * it + 1)
                    project(Q, 5, it + 2, q_mm)
                else:
                    up_early(3)
                    up_early(4)
                values(1)
                scores(3)
                turn(2)
                if not last:
                    pe.wait_ge(g_exp, 2 * it + 2)
                    project(K, 6, it + 2, k_mm)
                else:
                    for k in UP_ROWS[3]:
                        up_early(k)
                values(2)
                turn(3)
                if not last:
                    turn_v(it + 2)
                values(3)

            with pe.Fori(0, PAIRS) as j:
                attend(j, j, True, False)
            with pe.Fori(0, PAIRS - 1) as j:
                attend(j, j + PAIRS, False, False)
            attend(PAIRS - 1, LAST, False, True)

            def split_product(bank, left, right, start, stop):
                pe.matmul(ps[:, bank, :], left[1], right[0], start=start, stop=False)
                pe.matmul(ps[:, bank, :], left[0], right[1], start=False, stop=False)
                return pe.matmul(ps[:, bank, :], left[0], right[0], start=False, stop=stop)

            def up(k, e):
                cols = slice(k * P, (k + 1) * P)
                return split_product(k % 4, (wus_hi[:, e, cols], wus_lo[:, e, cols]), (ys_hi[:, e, :], ys_lo[:, e, :]),
                                     e == 0, e == PAIRS - 1)

            pe.wait_ge(ups_lo, PAIRS)
            pe.wait_ge(ysb_lo, PAIRS - 1)
            for k in range(4):
                for e in range(PAIRS - 1):
                    up(k, e)
            pe.wait_ge(ysb_lo, PAIRS)
            for k in range(4):
                up(k, PAIRS - 1).then_inc(up_mm, 1)
            for k in range(4, KT):
                pe.wait_ge(mg_f, k - 3)
                for e in range(PAIRS):
                    mm = up(k, e)
                mm.then_inc(up_mm, 1)

            def project_out(t):
                rows_ = slice(t * P, (t + 1) * P)
                for c in range(2):
                    cols = slice(c * S, (c + 1) * S)
                    if t < 2:
                        pe.wait_ge(mg_f, 5 + 2 * t + c)
                    else:
                        pe.wait_ge(o_rd, 2 * (t - 2) + c + 1)
                    for k in range(KT):
                        if t == 0 and c == 0:
                            pe.wait_ge(wo_l, k + 1)
                            pe.wait_ge(mg, k + 1)
                        mm = split_product(2 * (t % 2) + c, (mg_hi[:, k, rows_], mg_lo[:, k, rows_]),
                                           (wo_hi[:, k, cols], wo_lo[:, k, cols]), k == 0, k == KT - 1)
                    mm.then_inc(o_mm, 1)

            def turn_h1(t):
                pe.wait_ge(h1_ok, t + 1)
                for c in range(2):
                    if t > 0:
                        pe.wait_ge(h1t_a, 2 * t + c - 1)
                    for k in range(4):
                        mm = pe.transpose(ps[:, 4 + c, k * P:(k + 1) * P], h[:, t, (4 * c + k) * P:(4 * c + k + 1) * P],
                                          ident[:])
                    mm.then_inc(h1t_mm, 1)

            def route(t):
                if t == 0:
                    pe.wait_ge(wr_in, 32)
                if t >= 2:
                    pe.wait_ge(lg_ok, t - 1)
                pe.wait_ge(h1t_a, 2 * t + 2)
                for k in range(KT):
                    mm = pe.matmul(ps[:, 6 + t % 2, 0:P], h1T[:, k, :], wr[:, k, :],
                                   start=(k == 0), stop=(k == KT - 1))
                mm.then_inc(r_mm, 1)

            project_out(0)
            project_out(1)
            turn_h1(0)
            project_out(2)
            route(0)
            turn_h1(1)
            project_out(3)
            route(1)
            turn_h1(2)
            route(2)
            turn_h1(3)
            route(3)

            pe.wait_ge(eh_ok, 1)
            for t in range(TT):
                for s in range(t + 1):
                    pe.matmul(ps[:, 7, P + t * E:P + (t + 1) * E], (tri if s == t else ones)[:], ehot[:, s, :],
                              start=(s == 0), stop=(s == t))
            for s in range(TT):
                mm = pe.matmul(ps[:, 7, 0:E], ones[:], ehot[:, s, :], start=(s == 0), stop=(s == TT - 1))
            mm.then_inc(rank_mm, 1)

            def gather_part(dk, t, cols):
                for c in range(3):
                    mm = pe.matmul(ps[:, dk // 2, (dk % 2) * 256 + cols.start:(dk % 2) * 256 + cols.stop],
                                   parts[:, c, t, dk * P:(dk + 1) * P], oh[:, t, cols],
                                   start=(t == 0 and c == 0), stop=(t == TT - 1 and c == 2))
                return mm

            def gather(dk, cols=slice(0, QB * CAP)):
                for t in range(TT):
                    mm = gather_part(dk, t, cols)
                return mm

            FIRST_TILES = [((), ()), ((), ()), ((0, 1, 2), (3,)), ((4, 5, 6), (7,))]

            def expert_group(g, first, last):
                for q in range(QB):
                    n = QB * g + q
                    slots = (3 * (q % 2), 3 * (q % 2) + 1)
                    loaded = 32 * g + 16 * (q // 2) + 16
                    if first and q < 2:
                        pe.wait_ge(xg0_a, 2 * q + 2)
                        pe.wait_ge(xg0_v, 2 * q + 2)
                    elif q == 0:
                        pe.wait_ge(xg_a, 2 * g + 2)
                        pe.wait_ge(xg_v, 2 * g + 2)
                    for c, done in ((0, h1_mm), (1, h3_mm)):
                        pe.wait_ge(ring_in[slots[c]], loaded)
                        w = ring[slots[c]]
                        for k in range(KT):
                            for half in range(2):
                                mm = pe.matmul(ps[64 * half:64 * half + 64, 4 + c, 0:256],
                                               xg[:, k, q * CAP:(q + 1) * CAP],
                                               w[:, k * FE + half * 256:k * FE + half * 256 + 256],
                                               start=(k == 0), stop=(k == KT - 1))
                        mm.then_inc(done, 1)
                    if first and q < 2:
                        if q == 0:
                            pe.wait_ge(oh_ok, TT)
                        for dk in range(KT):
                            mm = gather(dk, FIRST_COLS[q])
                        mm.then_inc((ga0_mm, ga_mm)[q], 1)
                    before, after = FIRST_TILES[q] if first else ((2 * q,), (2 * q + 1,))
                    if not last:
                        if before and 0 in before:
                            pe.wait_ge(oh_ok, TT * g + 2 * TT)
                        for dk in before:
                            gather(dk)
                    pe.wait_ge(hm_ok, n + 1)
                    for c in range(2):
                        mm = pe.transpose(ps[:, 6, c * P:(c + 1) * P], hm[:, c * P:(c + 1) * P], ident[:])
                    mm.then_inc(ht_mm, 1)
                    if not last:
                        for dk in after:
                            mm = gather(dk)
                        if q == QB - 1:
                            mm.then_inc(ga_mm, 1)
                    pe.wait_ge(ht_ok, n + 1)
                    pe.wait_ge(w2_in[q], 16 * g + 16)
                    w = w2buf[q]
                    for k in range(FT):
                        for half in range(2):
                            mm = pe.matmul(ps[64 * half:64 * half + 64, 7, :],
                                           hmT[:, k % 2, 64 * (k // 2):64 * (k // 2) + 64],
                                           w[:, k * D + half * S:k * D + half * S + S],
                                           start=(k == 0), stop=(k == FT - 1))
                    mm.then_inc(ye_mm, 1)
                    if first and q == 1:
                        pe.wait_ge(xg_a, 2)
                        pe.wait_ge(xg_v, 2)

            pe.wait_ge(part_s, PART_STEPS * TT)
            pe.wait_ge(oh0_ok, TT)
            for dk in range(KT):
                mm = gather(dk, slice(0, CAP))
            mm.then_inc(ga0_mm, 1)
            expert_group(0, True, False)
            pe.wait_ge(ctl_ok, 1)
            final = pe.value_load(ctl[0:1, MAXOV + 1:MAXOV + 2], min_val=MAIN - 1, max_val=MAIN - 1 + MAXOV // QB)
            with pe.Fori(1, final) as g:
                expert_group(g, False, False)
            expert_group(final, False, True)

            pe.wait_ge(dg_ok, 1 + 2 * TT)
            pe.wait_ge(ye_sb, QB * final + QB)
            for t in range(TT):
                for c in range(2):
                    pe.matmul(ps[:, 2 * t + c, :], dg[:, 0, :], h[:, t, c * S:(c + 1) * S], start=True, stop=False)
            for t in range(TT):
                for choice in range(2):
                    pe.wait_ge(yg_in[t][choice], 16)
                    for c in range(2):
                        mm = pe.matmul(ps[:, 2 * t + c, :], dg[:, 1 + 2 * t + choice, :],
                                       yg[:, choice, t, c * S:(c + 1) * S], start=False, stop=(choice == 1))
                        if choice == 1:
                            mm.then_inc(fin_y, 1)


_INS = ['x', 'ln_in_g', 'ln_in_b', 'w_in', 'b_forget', 'w_up_fox', 'w_up_sb', 'w_out', 'ln1_g', 'ln1_b',
        'w_group', 'b_group', 'w_expert_router', 'b_expert_router', 'w1', 'w3', 'w2', 'ln2_g', 'ln2_b']


def kernel(**inputs):
    import numpy as _np
    import concourse.bacc as _bacc
    from concourse import mybir as _mybir
    from concourse.bass_utils import run_bass_kernel_spmd as _run

    nc = _bacc.Bacc("TRN2", target_bir_lowering=False, num_devices=1)
    arrays, args = {}, []
    for name in _INS:
        a = _np.ascontiguousarray(inputs[name])
        arrays[f"in_{name}_dram"] = a
        args.append(nc.dram_tensor(f"in_{name}_dram", a.shape, _mybir.dt.from_np(a.dtype), kind="ExternalInput").ap())
    args.append(nc.dram_tensor("out_0_dram", (1, S, D), F32, kind="ExternalOutput").ap())
    build(nc, *args)
    res = _run(nc, [arrays], core_ids=[0])
    return res.results[0]["out_0_dram"]
```
